# Optimizing a Trainium2 kernel written in Bass

```python
import math
import jax, jax.numpy as jnp
from jax import lax
import numpy as np

D_MODEL = 2048
BATCH = 1
SEQ = 256
DEPTH = 1

PLE_DIM = 256
N_HEADS = 16
HEAD_DIM = 128
D_ATTN = N_HEADS * HEAD_DIM
D_RNN = ((4 * D_MODEL // 3 + 255) // 256) * 256
N_RNN_BLOCKS = 16
RNN_BLOCK = D_RNN // N_RNN_BLOCKS
CONV_WIDTH = 4
LRU_C = 8.0
D_FF = ((8 * D_MODEL + 3 * 256 - 1) // (3 * 256)) * 256
Q_BLOCK = 128
EPS = 1e-6

IN_WIDTHS = (D_RNN, D_RNN, D_ATTN, D_ATTN, D_ATTN, D_MODEL, D_MODEL)
D_IN = sum(IN_WIDTHS)
IN_SPLIT_POINTS = tuple(int(v) for v in np.cumsum(IN_WIDTHS)[:-1])


def rmsnorm(x, g):
    x32 = x.astype(jnp.float32)
    r = x32 * lax.rsqrt(jnp.mean(x32 * x32, axis=-1, keepdims=True) + EPS)
    return (r * g.astype(jnp.float32)).astype(x.dtype)

def causal_depthwise_conv(x, w, b):
    S = x.shape[1]
    xp = jnp.pad(x, ((0, 0), (CONV_WIDTH - 1, 0), (0, 0)))
    y = sum(xp[:, k:k + S, :] * w[k] for k in range(CONV_WIDTH))
    return y + b

def rg_lru(x, w_a, b_a, w_x, b_x, lam):
    B, S, _ = x.shape
    xb = x.reshape(B, S, N_RNN_BLOCKS, RNN_BLOCK)
    r = jax.nn.sigmoid(jnp.einsum('bsnc,ncd->bsnd', xb, w_a).reshape(B, S, D_RNN) + b_a)
    i = jax.nn.sigmoid(jnp.einsum('bsnc,ncd->bsnd', xb, w_x).reshape(B, S, D_RNN) + b_x)
    log_a = (-LRU_C * r.astype(jnp.float32) * jax.nn.softplus(-lam.astype(jnp.float32)))
    a = jnp.exp(log_a)
    u = jnp.sqrt(-jnp.expm1(2.0 * log_a)) * (i * x).astype(jnp.float32)

    def combine(c1, c2):
        a1, b1 = c1
        a2, b2 = c2
        return a1 * a2, a2 * b1 + b2

    _, h = lax.associative_scan(combine, (a, u), axis=1)
    return h.astype(x.dtype)

def head_rmsnorm(x, g):
    x32 = x.astype(jnp.float32)
    r = x32 * lax.rsqrt(jnp.mean(x32 * x32, axis=-1, keepdims=True) + EPS)
    return (r * g.astype(jnp.float32)).astype(x.dtype)

def stick_breaking_attention(q, k, v):
    S = q.shape[2]
    scale = 1.0 / math.sqrt(HEAD_DIM)
    outs = []
    for blk in range(S // Q_BLOCK):
        t0 = blk * Q_BLOCK
        tk = t0 + Q_BLOCK
        qb = q[:, :, t0:tk]
        kb = k[:, :, :tk]
        vb = v[:, :, :tk]
        z = jnp.einsum('bhqd,bhkd->bhqk', qb, kb).astype(jnp.float32) * scale
        q_pos = t0 + jnp.arange(Q_BLOCK)[:, None]
        k_pos = jnp.arange(tk)[None, :]
        causal = k_pos < q_pos
        log_keep = jnp.where(causal, jax.nn.log_sigmoid(-z), 0.0)
        incl = lax.cumsum(log_keep, axis=3, reverse=True)
        excl = jnp.concatenate([incl[..., 1:], jnp.zeros_like(incl[..., :1])], axis=-1)
        w = jnp.where(causal, jnp.exp(jax.nn.log_sigmoid(z) + excl), 0.0)
        outs.append(jnp.einsum('bhqk,bhkd->bhqd', w.astype(vb.dtype), vb))
    return jnp.concatenate(outs, axis=2)

def first_inputs(seed: int = 0) -> dict:
    key = jax.random.key(seed)
    ks = jax.random.split(key, 24)
    f32 = jnp.float32

    def nrm(k, shape, fan_in):
        return jax.random.normal(k, shape, f32) * (fan_in ** -0.5)

    def gain(k, shape):
        return 1.0 + 0.02 * jax.random.normal(k, shape, f32)

    u = jax.random.uniform(ks[9], (DEPTH, D_RNN), f32, 0.9, 0.999)
    s = u ** (1.0 / LRU_C)
    lru_lambda = jnp.log(s) - jnp.log1p(-s)

    return {
        "x": jax.random.normal(ks[0], (BATCH, SEQ, D_MODEL), f32),
        "p": jax.random.normal(ks[1], (DEPTH, BATCH, SEQ, PLE_DIM), f32),
        "g_mix": gain(ks[2], (DEPTH, D_MODEL)),
        "w_in": nrm(ks[3], (DEPTH, D_MODEL, D_IN), D_MODEL),
        "conv_w": nrm(ks[4], (DEPTH, CONV_WIDTH, D_RNN), CONV_WIDTH),
        "conv_b": 0.02 * jax.random.normal(ks[5], (DEPTH, D_RNN), f32),
        "w_rg_a": nrm(ks[6], (DEPTH, N_RNN_BLOCKS, RNN_BLOCK, RNN_BLOCK), RNN_BLOCK),
        "b_rg_a": 0.02 * jax.random.normal(ks[7], (DEPTH, D_RNN), f32),
        "w_rg_x": nrm(ks[8], (DEPTH, N_RNN_BLOCKS, RNN_BLOCK, RNN_BLOCK), RNN_BLOCK),
        "b_rg_x": 0.02 * jax.random.normal(ks[10], (DEPTH, D_RNN), f32),
        "lru_lambda": lru_lambda,
        "q_gain": gain(ks[11], (DEPTH, HEAD_DIM)),
        "k_gain": gain(ks[12], (DEPTH, HEAD_DIM)),
        "w_rnn_out": nrm(ks[13], (DEPTH, D_RNN, D_MODEL), D_RNN),
        "w_attn_out": nrm(ks[14], (DEPTH, D_ATTN, D_MODEL), D_ATTN),
        "w_o": nrm(ks[15], (DEPTH, D_MODEL, D_MODEL), D_MODEL),
        "g_ffn": gain(ks[16], (DEPTH, D_MODEL)),
        "w_ffn_gu": nrm(ks[17], (DEPTH, D_MODEL, 2 * D_FF), D_MODEL),
        "w_ffn_down": nrm(ks[18], (DEPTH, D_FF, D_MODEL), D_FF),
        "g_ple": gain(ks[19], (DEPTH, D_MODEL)),
        "w_ple_gate": nrm(ks[20], (DEPTH, D_MODEL, D_MODEL), D_MODEL),
        "w_ple_proj": nrm(ks[21], (DEPTH, PLE_DIM, D_MODEL), PLE_DIM),
    }

def first_block(x, p, g_mix, w_in, conv_w, conv_b, w_rg_a, b_rg_a, w_rg_x, b_rg_x,
              lru_lambda, q_gain, k_gain, w_rnn_out, w_attn_out, w_o, g_ffn,
              w_ffn_gu, w_ffn_down, g_ple, w_ple_gate, w_ple_proj):
    B, S, _ = x.shape
    for i in range(DEPTH):
        h = rmsnorm(x, g_mix[i])
        proj = h @ w_in[i]
        x_r, g_r, q, k, v, gate_r, gate_a = jnp.split(proj, IN_SPLIT_POINTS, axis=-1)

        xc = causal_depthwise_conv(x_r, conv_w[i], conv_b[i])
        y_r = jax.nn.gelu(g_r) * rg_lru(xc, w_rg_a[i], b_rg_a[i], w_rg_x[i], b_rg_x[i], lru_lambda[i])
        y_r = y_r @ w_rnn_out[i]

        q = head_rmsnorm(q.reshape(B, S, N_HEADS, HEAD_DIM).transpose(0, 2, 1, 3), q_gain[i])
        k = head_rmsnorm(k.reshape(B, S, N_HEADS, HEAD_DIM).transpose(0, 2, 1, 3), k_gain[i])
        v = v.reshape(B, S, N_HEADS, HEAD_DIM).transpose(0, 2, 1, 3)
        o = stick_breaking_attention(q, k, v)
        y_a = o.transpose(0, 2, 1, 3).reshape(B, S, D_ATTN) @ w_attn_out[i]

        mix = jax.nn.sigmoid(gate_r) * y_r + jax.nn.sigmoid(gate_a) * y_a
        x = x + mix @ w_o[i]

        h = rmsnorm(x, g_ffn[i])
        gu = h @ w_ffn_gu[i]
        g, u = jnp.split(gu, 2, axis=-1)
        x = x + (jax.nn.silu(g) * u) @ w_ffn_down[i]

        ple_gate = jax.nn.sigmoid(rmsnorm(x, g_ple[i]) @ w_ple_gate[i])
        x = x + ple_gate * (p[i] @ w_ple_proj[i])
    return x


DEPTH_2 = 2

D_MIX = D_MODEL
A_HEADS = 4
A_HEAD_DIM = 128
A_QK_HALF = A_HEAD_DIM // 2
D_A = A_HEADS * A_HEAD_DIM
B_HEADS = 8
B_HEAD_DIM = 128
D_B = B_HEADS * B_HEAD_DIM
DILATED_PATTERNS = ((128, 1), (512, 4), (2048, 16))
D_C = D_MIX - D_A - D_B
CONV_WIDTH_2 = 31

BLOCK = 128
N_BUCKETS = 32
MAX_DISTANCE = 2048
N_ATTN_HEADS = A_HEADS + B_HEADS
ALPHA = (2 * DEPTH_2) ** 0.25
BETA = (8 * DEPTH_2) ** -0.25
EPS_2 = 1e-5

IN_SIZES = (D_A, D_A, D_A, D_A,
            D_B, D_B, D_B, D_B,
            D_C, D_C, D_C)
D_IN_2 = sum(IN_SIZES)
IN_OFFSETS = [int(o) for o in np.cumsum(IN_SIZES)[:-1]]


def layer_norm(x, g, b):
    x32 = x.astype(jnp.float32)
    mu = jnp.mean(x32, axis=-1, keepdims=True)
    var = jnp.mean(jnp.square(x32 - mu), axis=-1, keepdims=True)
    y = (x32 - mu) * lax.rsqrt(var + EPS_2) * g.astype(jnp.float32) + b.astype(jnp.float32)
    return y.astype(x.dtype)

def t5_bucket(dist):
    max_exact = N_BUCKETS // 2
    d = jnp.maximum(dist, 0)
    df = jnp.maximum(d, 1).astype(jnp.float32)
    large = max_exact + (jnp.log(df / max_exact) / math.log(MAX_DISTANCE / max_exact)
                         * (N_BUCKETS - max_exact)).astype(jnp.int32)
    large = jnp.minimum(large, N_BUCKETS - 1)
    return jnp.where(d < max_exact, d, large)

def diff_attention(q, k, v, bias_dist, lam, lam_init, head_gain):
    B, S, H, _, Dq = q.shape
    nb = S // BLOCK
    scale = Dq ** -0.5
    qb = jnp.moveaxis(q.reshape(B, nb, BLOCK, H, 2, Dq), 1, 0)
    k_pos = jnp.arange(S)

    def one_block(args):
        qi, i = args
        q_pos = i * BLOCK + jnp.arange(BLOCK)
        dist = q_pos[:, None] - k_pos[None, :]
        bias = bias_dist[jnp.clip(dist, 0, S - 1)].astype(jnp.float32)
        s = jnp.einsum('bqhcd,bkhcd->bhcqk', qi, k).astype(jnp.float32) * scale
        s = s + jnp.transpose(bias, (2, 0, 1))[None, :, None]
        s = jnp.where(dist >= 0, s, -jnp.inf)
        p = jax.nn.softmax(s, axis=-1)
        a = p[:, :, 0] - lam * p[:, :, 1]
        return jnp.einsum('bhqk,bkhd->bqhd', a.astype(v.dtype), v)

    out = lax.map(one_block, (qb, jnp.arange(nb)))
    out = jnp.moveaxis(out, 0, 1).reshape(B, S, H, v.shape[-1]).astype(jnp.float32)
    out = out * lax.rsqrt(jnp.mean(jnp.square(out), axis=-1, keepdims=True) + EPS_2)
    out = out * head_gain.astype(jnp.float32) * (1.0 - lam_init)
    return out.astype(v.dtype)

def _residue_view(x, dil):
    B, S = x.shape[:2]
    L = S // dil
    xr = jnp.moveaxis(x.reshape((B, L, dil) + x.shape[2:]), 2, 1).reshape((B * dil, L) + x.shape[2:])
    pad = (-L) % BLOCK
    return jnp.pad(xr, ((0, 0), (0, pad)) + ((0, 0),) * (x.ndim - 2))

def _residue_unview(y, B, dil, L):
    y = y[:, :L]
    y = jnp.moveaxis(y.reshape((B, dil) + y.shape[1:]), 1, 2)
    return y.reshape((B, dil * L) + y.shape[3:])

def dilated_attention(q, k, v, bias_table):
    B, S, H, D = q.shape
    scale = D ** -0.5
    qi = jnp.arange(BLOCK)
    kj = jnp.arange(2 * BLOCK)
    lag = BLOCK + qi[:, None] - kj[None, :]
    outs, maxes, sums = [], [], []
    for window, dil in DILATED_PATTERNS:
        L = S // dil
        qr, kr, vr = _residue_view(q, dil), _residue_view(k, dil), _residue_view(v, dil)
        N, Lp = qr.shape[:2]
        nb = Lp // BLOCK
        qb = qr.reshape(N, nb, BLOCK, H, D)
        kp = jnp.pad(kr, ((0, 0), (BLOCK, 0), (0, 0), (0, 0))).reshape(N, nb + 1, BLOCK, H, D)
        vp = jnp.pad(vr, ((0, 0), (BLOCK, 0), (0, 0), (0, 0))).reshape(N, nb + 1, BLOCK, H, D)
        kb = jnp.concatenate([kp[:, :-1], kp[:, 1:]], axis=2)
        vb = jnp.concatenate([vp[:, :-1], vp[:, 1:]], axis=2)
        key_idx = (jnp.arange(nb) * BLOCK - BLOCK)[:, None] + kj[None, :]
        valid = ((lag >= 0) & (lag <= window // dil))[None] & (key_idx >= 0)[:, None, :]
        bias = bias_table[t5_bucket(kj * dil)]
        bias_qk = bias[jnp.clip(lag, 0, 2 * BLOCK - 1)].astype(jnp.float32)
        s = jnp.einsum('nbqhd,nbkhd->nbhqk', qb, kb).astype(jnp.float32) * scale
        s = s + jnp.transpose(bias_qk, (2, 0, 1))[None, None]
        s = jnp.where(valid[None, :, None], s, -jnp.inf)
        m = jnp.max(s, axis=-1)
        p = jnp.exp(s - m[..., None])
        l = jnp.sum(p, axis=-1)
        o = jnp.einsum('nbhqk,nbkhd->nbqhd', p.astype(v.dtype), vb).astype(jnp.float32)
        l_t = jnp.swapaxes(l, 2, 3)
        o = o / l_t[..., None]
        outs.append(_residue_unview(o.reshape(N, Lp, H, D), B, dil, L))
        maxes.append(_residue_unview(jnp.swapaxes(m, 2, 3).reshape(N, Lp, H), B, dil, L))
        sums.append(_residue_unview(l_t.reshape(N, Lp, H), B, dil, L))
    m_all = jnp.stack(maxes)
    w = jnp.stack(sums) * jnp.exp(m_all - jnp.max(m_all, axis=0, keepdims=True))
    out = jnp.sum(w[..., None] * jnp.stack(outs), axis=0) / jnp.sum(w, axis=0)[..., None]
    return out.astype(q.dtype)

def conformer_conv(u, glu_gate, w_dw, b_dw, ln_g, ln_b, w_pw):
    h = u * jax.nn.sigmoid(glu_gate)
    h = lax.conv_general_dilated(h, w_dw[:, None, :], window_strides=(1,),
                                 padding=[(CONV_WIDTH_2 - 1, 0)],
                                 dimension_numbers=('NWC', 'WIO', 'NWC'),
                                 feature_group_count=D_C) + b_dw
    h = jax.nn.silu(layer_norm(h, ln_g, ln_b))
    return h @ w_pw

def hybrid_layer(x, w_in, diff_lambda, diff_head_gain, conv_dw, conv_b, conv_ln_g, conv_ln_b,
                 conv_pw, w_out, ln_g, ln_b, rel_bias, lam_init):
    B, S, _ = x.shape
    proj = x @ w_in
    aq, ak, av, ag, bq, bk, bv, bg, cu, cglu, cg = jnp.split(proj, IN_OFFSETS, axis=-1)

    lam_v = diff_lambda.astype(jnp.float32)
    lam = (jnp.exp(jnp.sum(lam_v[0] * lam_v[1])) - jnp.exp(jnp.sum(lam_v[2] * lam_v[3]))
           + lam_init)
    bias_a = rel_bias[t5_bucket(jnp.arange(S))][:, :A_HEADS]
    ya = diff_attention(aq.reshape(B, S, A_HEADS, 2, A_QK_HALF),
                        ak.reshape(B, S, A_HEADS, 2, A_QK_HALF),
                        av.reshape(B, S, A_HEADS, A_HEAD_DIM),
                        bias_a, lam, lam_init, diff_head_gain).reshape(B, S, D_A)
    ya = ya * jax.nn.silu(ag)

    yb = dilated_attention(bq.reshape(B, S, B_HEADS, B_HEAD_DIM),
                           bk.reshape(B, S, B_HEADS, B_HEAD_DIM),
                           bv.reshape(B, S, B_HEADS, B_HEAD_DIM),
                           rel_bias[:, A_HEADS:]).reshape(B, S, D_B)
    yb = yb * jax.nn.silu(bg)

    yc = conformer_conv(cu, cglu, conv_dw, conv_b, conv_ln_g, conv_ln_b, conv_pw)
    yc = yc * jax.nn.silu(cg)

    y = jnp.concatenate([ya, yb, yc], axis=-1) @ w_out
    return layer_norm(ALPHA * x + y, ln_g, ln_b)

def second_inputs(seed: int = 0) -> dict:
    key = jax.random.key(seed)
    ks = jax.random.split(key, 14)
    nrm = jax.random.normal
    return {
        "x": nrm(ks[0], (BATCH, SEQ, D_MODEL), jnp.float32),
        "w_in": nrm(ks[1], (DEPTH_2, D_MODEL, D_IN_2), jnp.float32) * D_MODEL ** -0.5,
        "diff_lambda": 0.1 * nrm(ks[2], (DEPTH_2, 4, A_QK_HALF), jnp.float32),
        "diff_head_gain": 1.0 + 0.02 * nrm(ks[3], (DEPTH_2, A_HEAD_DIM), jnp.float32),
        "conv_dw": nrm(ks[4], (DEPTH_2, CONV_WIDTH_2, D_C), jnp.float32) * CONV_WIDTH_2 ** -0.5,
        "conv_b": 0.02 * nrm(ks[5], (DEPTH_2, D_C), jnp.float32),
        "conv_ln_g": 1.0 + 0.02 * nrm(ks[6], (DEPTH_2, D_C), jnp.float32),
        "conv_ln_b": 0.02 * nrm(ks[7], (DEPTH_2, D_C), jnp.float32),
        "conv_pw": nrm(ks[8], (DEPTH_2, D_C, D_C), jnp.float32) * D_C ** -0.5,
        "w_out": nrm(ks[9], (DEPTH_2, D_MIX, D_MODEL), jnp.float32) * (D_MIX ** -0.5 * BETA),
        "ln_g": 1.0 + 0.02 * nrm(ks[10], (DEPTH_2, D_MODEL), jnp.float32),
        "ln_b": 0.02 * nrm(ks[11], (DEPTH_2, D_MODEL), jnp.float32),
        "rel_bias": 0.5 * nrm(ks[12], (N_BUCKETS, N_ATTN_HEADS), jnp.float32),
    }

def second_block(x, w_in, diff_lambda, diff_head_gain, conv_dw, conv_b, conv_ln_g, conv_ln_b,
              conv_pw, w_out, ln_g, ln_b, rel_bias):
    for layer in range(DEPTH_2):
        lam_init = 0.8 - 0.6 * math.exp(-0.3 * layer)
        x = hybrid_layer(x, w_in[layer], diff_lambda[layer], diff_head_gain[layer],
                         conv_dw[layer], conv_b[layer], conv_ln_g[layer], conv_ln_b[layer],
                         conv_pw[layer], w_out[layer], ln_g[layer], ln_b[layer], rel_bias,
                         lam_init)
    return x


def setup_inputs(seed=0):
    out = dict(first_inputs(seed))
    for name, value in second_inputs(seed + 1).items():
        if name != "x":
            out[name + "_2"] = value
    return out


def reference(
    x, p, g_mix, w_in, conv_w, conv_b, w_rg_a, b_rg_a, w_rg_x, b_rg_x, lru_lambda, q_gain,
    k_gain, w_rnn_out, w_attn_out, w_o, g_ffn, w_ffn_gu, w_ffn_down, g_ple, w_ple_gate,
    w_ple_proj, w_in_2, diff_lambda_2, diff_head_gain_2, conv_dw_2, conv_b_2, conv_ln_g_2,
    conv_ln_b_2, conv_pw_2, w_out_2, ln_g_2, ln_b_2, rel_bias_2,
):
    x = first_block(
        x, p, g_mix, w_in, conv_w, conv_b, w_rg_a, b_rg_a, w_rg_x, b_rg_x, lru_lambda, q_gain,
        k_gain, w_rnn_out, w_attn_out, w_o, g_ffn, w_ffn_gu, w_ffn_down, g_ple, w_ple_gate,
        w_ple_proj,
    )
    return second_block(
        x, w_in_2, diff_lambda_2, diff_head_gain_2, conv_dw_2, conv_b_2, conv_ln_g_2,
        conv_ln_b_2, conv_pw_2, w_out_2, ln_g_2, ln_b_2, rel_bias_2,
    )


_drawn_inputs = setup_inputs


def setup_inputs(seed=0):
    import zlib

    import numpy as np

    out = dict(_drawn_inputs(seed))
    spreads = {}
    factors = {'g_mix': 5.259,
     'b_rg_a': 8.0,
     'b_rg_x': 8.0,
     'q_gain': 8.0,
     'k_gain': 8.0,
     'g_ffn': 4.262,
     'g_ple': 27.907,
     'diff_lambda_2': 6.755,
     'diff_head_gain_2': 43.367,
     'conv_b_2': 8.0,
     'conv_ln_g_2': 41.856,
     'conv_ln_b_2': 38.124}
    for name, (base, spread) in spreads.items():
        noise = np.random.default_rng([zlib.crc32(name.encode()), seed]).standard_normal(out[name].shape)
        drawn = base * np.exp(spread * noise) if base else spread * noise
        out[name] = __import__('jax').numpy.asarray(drawn.astype(out[name].dtype))
    for name, factor in factors.items():
        out[name] = (out[name] * factor).astype(out[name].dtype)
    return out
```

```python
import numpy as np
from contextlib import ExitStack
from collections import namedtuple
import concourse.bass as bass
from concourse import mybir

STOP = None

P = 128
T = 256
NB = T // P
D = 2048
DC = D // P
RNN = 2816
RC = RNN // P
RB = 176
TAPS = 4
FF = 5632
HALF = FF // 2
HC_ = HALF // P
PLE = 256
TAPS2 = 31
COLS = 256
SLOTS = 4
UK = 4
NBUCK = 32
HEADS2 = 12
CONVC = 4
EPS = 1e-6
EPS2 = 1e-5
ALPHA = 4.0 ** 0.25
QSCALE = 128.0 ** -0.5
ASCALE = 64.0 ** -0.5
GELU_C = 0.044715
GELU_S = float(np.sqrt(2.0 / np.pi))
NEG = -1e30
LRU_HALF_C = 4.0
LAM_INIT = [0.8 - 0.6 * float(np.exp(-0.3 * layer)) for layer in range(2)]

VEC_ROWS = [("g_mix", 16), ("g_ffn", 16), ("g_ple", 16), ("conv_b", 22), ("conv_w", 88), ("b_rg_a", 22),
            ("b_rg_x", 22), ("lru_lambda", 22), ("q_gain", 1), ("k_gain", 1), ("diff_head_gain_2", 2),
            ("conv_dw_2", 248), ("conv_b_2", 8), ("conv_ln_g_2", 8), ("conv_ln_b_2", 8), ("ln_g_2", 32),
            ("ln_b_2", 32)]
VEC_AT, _n = {}, 0
for _name, _rows in VEC_ROWS:
    VEC_AT[_name] = _n
    _n += _rows
VEC_N = _n
VEC_TILES = (VEC_N + P - 1) // P


def t5_bucket_np(d):
    exact = NBUCK // 2
    df = np.maximum(d, 1).astype(np.float32)
    large = exact + (np.log(df / np.float32(exact)) / np.float32(np.log(2048 / exact))
                     * np.float32(NBUCK - exact)).astype(np.int32)
    return np.where(d < exact, d, np.minimum(large, NBUCK - 1))


def shape_constants():
    eye = np.eye(P, dtype=np.float32)
    after = np.tril(np.ones((P, P), np.float32), -1)
    ones = np.ones((P, P), np.float32)
    flip = np.ascontiguousarray(eye[:, ::-1])
    before = np.triu(np.ones((P, P), np.float32), 1)
    keep = np.concatenate([before, ones, before], 1)
    mats = np.concatenate([eye, after, ones, flip], 1)
    i = np.arange(384)
    dist = 255 - i
    onehot = (t5_bucket_np(np.maximum(dist, 0))[None] == np.arange(NBUCK)[:, None]).astype(np.float32)
    add = np.zeros((HEADS2, 384), np.float32)
    times = (dist <= 128).astype(int) + (dist % 4 == 0) + (dist % 16 == 0)
    add[4:] = np.where(times > 0, np.log(np.maximum(times, 1)), NEG)
    add[:, dist < 0] = NEG
    return mats, keep, onehot, add


class Counts:

    def __init__(self, eng, who, turns, real):
        self.eng, self.who, self.turns, self.real = eng, who, turns, real
        self.n, self.per, self.var, self.first, self.loops = {}, {}, None, 0, 0

    def add(self, key, m=1):
        self.n[key] = self.n.get(key, 0) + m

    def value(self, key, extra=0, div=1, mul=1):
        n = self.n.get(key, 0) + extra
        if self.var is None:
            return mul * (n // div)
        k = self.per.get(key, 0)
        if k == 0:
            return mul * (n // div)
        assert k % div == 0 or not self.real
        k //= div
        c = mul * (n // div - self.first * k)
        v = self.var * (mul * k) if mul * k != 1 else self.var
        return v + c if c >= 0 else v - (-c)

    def next(self, key, m=1, mul=1):
        self.add(key, m)
        return self.value(key, mul=mul)

    def loop(self, first, last, body):
        if last - first < 2:
            for i in range(first, last):
                body(i)
            return
        name = (self.who, self.loops)
        self.loops += 1
        start = dict(self.n)
        self.per = self.turns.get(name, {})
        self.first = first
        with self.eng.Fori(first, last) as i:
            self.var = i
            body(i)
        self.var = None
        met = {k: v - start.get(k, 0) for k, v in self.n.items()}
        assert not self.real or met == {k: self.per.get(k, 0) for k in met}, (name, met, self.per)
        self.turns[name] = met
        for k, v in met.items():
            self.n[k] = start.get(k, 0) + v * (last - first)


class Group:

    def __init__(self, W, K, col, step, X, base=0):
        self.W, self.K, self.col, self.step, self.X, self.base = W, K, col, step, X, base

    def units(self):
        return [(k, min(UK, self.K - k)) for k in range(0, self.K, UK)]


class Phase:
    def __init__(self, name, n, body, fresh=False):
        self.name, self.n, self.body, self.fresh = name, n, body, fresh


def gate_tiles():
    strips, users = [], [[] for _ in range(RC)]
    for i in range(RC):
        n0, n1 = P * i // RB, (P * i + P - 1) // RB
        j0 = RB * n0 // P
        pieces = [(n, max(P * i, RB * n), min(P * i + P, RB * (n + 1))) for n in range(n0, n1 + 1)]
        strips.append((j0, pieces))
        for j in range(RC):
            if any(RB * n < P * j + P and RB * (n + 1) > P * j for n in range(n0, n1 + 1)):
                users[j].append(i)
    return strips, users


def program(nc, A, turns, real):
    fp = mybir.dt.float32
    fr = mybir.dt.float32r
    ALU = mybir.AluOpType
    ACT = mybir.ActivationFunctionType
    AX = mybir.AxisListType.X
    ctx = ExitStack()
    with ctx:
        def sb(name, shape, dt=fp):
            return ctx.enter_context(nc.sbuf_tensor(name, shape, dt))

        RAW = sb("RAW", [P, SLOTS, UK, COLS])
        WH = sb("WH", [P, SLOTS, UK, COLS], fr)
        WL = sb("WL", [P, SLOTS, UK, COLS], fr)
        XRES = sb("XRES", [P, DC, T])
        XH = sb("XH", [P, DC, 2 * T], fr)
        with nc.sbuf_tensor("YH", [P, RC, 2 * T], fr) as YH:
            pass
        AE = sb("AE", [P, 2, RC, T])
        MIX = sb("MIX", [P, DC, T])
        F = sb("F", [P, RC * T])
        RT = sb("RT", [P, 16 * T])
        G = sb("G", [P, 2, 2, T])
        TT = sb("TT", [P, 2, 2, T])
        MATS = sb("MATS", [P, 4 * P])
        VEC = sb("VEC", [P, VEC_TILES * P])
        DER = sb("DER", [P, 128])
        PG = ctx.enter_context(nc.psum_tensor("PG", [P, 4, 512], fp))
        PX = ctx.enter_context(nc.psum_tensor("PX", [P, 4, 512], fp))
        strip_dram = nc.dram_tensor("bias_strip", [HEADS2, 384], fp).ap()

        IDENT, AFTER, ONES, FLIP = (MATS[:, P * i:P * i + P] for i in range(4))
        Fv = F[:, :]
        XC = F[:, :].rearrange("p (c t) -> p c t", t=T)
        RTc = RT[:, :].rearrange("p (c t) -> p c t", t=T)
        Gf = G[:, :, :, :].rearrange("p a b t -> p a (b t)")
        Tf = TT[:, :, :, :].rearrange("p a b t -> p a (b t)")

        def vec(name, i=0, m=1):
            at = VEC_AT[name] + i
            return VEC[:, at:at + m] if isinstance(at, int) else VEC[:, bass.ds(at, m)]

        EPS_AP, EPS2_AP = EPS, EPS2
        VEC_DMAS = sum(1 + (at % P + rows - 1) // P for at, rows in
                       ((VEC_AT[n], r) for n, r in VEC_ROWS))
        TP_STRIP, TP_P, TP_OUT = DC // 2 + 2, DC // 2 + 3, DC // 2 + 3
        TPD_STRIP = TPD_OUT = DC // 2 + 2
        OPS_MIX = DC // 2 + DC // 2 + RC // 2 + DC // 2
        GATES_FROM = 8 * 3 + 3
        D_HBA, D_HBX, D_SP, D_NSP, D_QG, D_HG, D_NLAM, D_RED = 0, 22, 44, 66, 88, 89, 91, 93

        def der(at, m=1):
            return DER[:, at:at + m]

        QR = F[:, 0:1024].rearrange("p (a n) -> p a n", a=2)
        SQ2 = F[:, 1024:2048].rearrange("p (a n) -> p a n", a=2)
        V = F[:, 2048:2560].rearrange("p (a n) -> p a n", a=4)
        L = F[:, 2560:3328].rearrange("p (a n) -> p a n", a=2)
        SP = F[:, 3328:4096].rearrange("p (a n) -> p a n", a=2)
        T1 = F[:, 4096:4864].rearrange("p (a n) -> p a n", a=2)
        W = F[:, 4864:5632].rearrange("p (a n) -> p a n", a=2)
        KEEP = RT[:, 1024:1408]
        MS = RT[:, 2048:3072].rearrange("p (a n) -> p a n", a=2)
        R2 = RT[:, 3072:4096].rearrange("p (a n) -> p a n", a=2)
        S4 = F[:, 2560:4096].rearrange("p (a n) -> p a n", a=4)
        PTS = W
        OA = F[:, 4096:4608]
        SG = F[:, 1024:1536]
        SQa = F[:, 1536:2048]
        HCW = 32 + T
        HC = MIX[:, 0:5, :].rearrange("p c t -> p (c t)")[:, 0:CONVC * HCW].rearrange("p (c t) -> p c t", t=HCW)
        CA = MIX[:, 6:10, :]
        SC = MIX[:, 10:14, :]
        SC_SQ = MIX[:, 0:CONVC, :]
        MIXf = MIX[:, :, :].rearrange("p c t -> p (c t)")
        OUTV = MIXf.rearrange("p (b d) -> p b d", b=NB)
        AB = RT[:, 0:HEADS2 * T].rearrange("p (h t) -> p h t", t=T)

        def wv(ap):
            return ap.rearrange("(c p) n -> p c n", p=P)

        w_in = wv(A["w_in"][0])
        w_rnn, w_att, w_o = wv(A["w_rnn_out"][0]), wv(A["w_attn_out"][0]), wv(A["w_o"][0])
        w_gu, w_dn = wv(A["w_ffn_gu"][0]), wv(A["w_ffn_down"][0])
        w_pg, w_pp = wv(A["w_ple_gate"][0]), wv(A["w_ple_proj"][0])
        QO = 2 * RNN
        KO, VO = QO + D, QO + 2 * D
        GR, GA = QO + 3 * D, QO + 4 * D

        def seq(w, K, col, X, width=2, base=0):
            return [Group(w, K, col + COLS * j, COLS * width, X, base) for j in range(width)]

        phases = []
        body = []
        for m in range(2):
            for off in (QO, KO, VO):
                body.append(Group(w_in, DC, off + COLS * m, 2 * COLS, XH))
        phases.append(Phase("attn", 4, body, fresh=True))
        phases.append(Phase("gate_a0", 1, seq(w_in, DC, GA, XH, 4)))
        phases.append(Phase("gate_a1", 2, seq(w_in, DC, GA + 4 * COLS, XH)))
        phases.append(Phase("attn_out", 4, seq(w_att, DC, 0, YH), fresh=True))
        phases.append(Phase("x_r", 5, seq(w_in, DC, 0, XH)))
        phases.append(Phase("x_r_last", 1, seq(w_in, DC, 10 * COLS, XH, 1)))
        phases.append(Phase("lru_gates", 0, []))
        phases.append(Phase("gate_r", 1, seq(w_in, DC, GR, XH, 8)))
        phases.append(Phase("g_r", 5, seq(w_in, DC, RNN, XH)))
        phases.append(Phase("g_r_last", 1, seq(w_in, DC, RNN + 10 * COLS, XH, 1)))
        phases.append(Phase("rnn_out", 4, seq(w_rnn, RC, 0, YH), fresh=True))
        phases.append(Phase("tables", 0, []))
        phases.append(Phase("w_o", 4, seq(w_o, DC, 0, XH), fresh=True))
        phases.append(Phase("norm_ffn", 0, []))
        for h in range(2):
            gu = []
            for m in range(2):
                gu.append(Group(w_gu, DC, HALF * h + COLS * m, 2 * COLS, XH))
                gu.append(Group(w_gu, DC, FF + HALF * h + COLS * m, 2 * COLS, XH))
            phases.append(Phase(f"gu{h}", 5, gu, fresh=h == 0))
            phases.append(Phase(f"gu_last{h}", 1, [Group(w_gu, DC, HALF * h + 10 * COLS, 0, XH),
                                                   Group(w_gu, DC, FF + HALF * h + 10 * COLS, 0, XH)]))
            phases.append(Phase(f"down{h}", 4, seq(w_dn[:, HC_ * h:HC_ * h + HC_, :], HC_, 0, YH), fresh=True))
        phases.append(Phase("norm_ple", 0, []))
        phases.append(Phase("ple_proj", 1, seq(w_pp, 2, 0, YH, 8), fresh=True))
        phases.append(Phase("ple_gate", 4, seq(w_pg, DC, 0, XH), fresh=True))
        for l in range(2):
            w2, wp, wo = wv(A["w_in_2"][l]), wv(A["conv_pw_2"][l]), wv(A["w_out_2"][l])
            A0, B0, C0 = 0, 2048, 6144
            cb = [C0, C0 + 512, C0 + COLS, C0 + 512 + COLS, C0 + 1024, C0 + 1024 + COLS]
            phases.append(Phase(f"conf{l}", 1, [Group(w2, DC, c, 0, YH) for c in cb], fresh=True))
            phases.append(Phase(f"diff{l}", 1, [Group(w2, DC, A0 + 512 * o + COLS * m, 0, YH)
                                                for m in range(2) for o in range(4)]))
            phases.append(Phase(f"dil{l}", 4, [Group(w2, DC, B0 + 1024 * o, COLS, YH) for o in range(4)]))
            phases.append(Phase(f"pw_norm{l}", 0, []))
            phases.append(Phase(f"pw{l}", 1, seq(wp, CONVC, 0, YH, 2, base=DC), fresh=True))
            phases.append(Phase(f"out{l}", 4, seq(wo, DC, 0, XH), fresh="all"))
            phases.append(Phase(f"ln{l}", 0, []))
        if STOP:
            names = [p.name for p in phases]
            phases = phases[:names.index(STOP) + 1]

        NAMES = ["raw0", "raw1", "raw2", "raw3",
                 "hi", "lo",
                 "unit",
                 "evac",
                 "op",
                 "x_in", "mats", "vecs", "lam", "keep", "p_in", "tab", "strip", "tb", "out",
                 "tp",
                 "tpd",
                 "sq",
                 "sums",
                 "ss",
                 "act",
                 "dve",
                 "scores",
                 "later",
                 "rms",
                 "heads",
                 "scores2", "turned", "heads2",
                 "flip", "flipped",
                 "sum", "sumsq",
                 "final",
                 "chain",
                 "achain",
                 "ready",
                 "strip0", "strip1", "strip2", "strip3",
                 "wiped",
                 "xc",
                 "bd",
                 "bdd",
                 ]
        Semaphores = namedtuple("Semaphores", NAMES)
        s = Semaphores(*(ctx.enter_context(nc.semaphore("s_" + name)) for name in NAMES))
        raw_sems = [s.raw0, s.raw1, s.raw2, s.raw3]
        strip_sems = [s.strip0, s.strip1, s.strip2, s.strip3]
        strips, users = gate_tiles()
        last_user = [max(j for j in range(RC) if i in users[j]) for i in range(RC)]
        block = ctx.enter_context(nc.Block())

        def pair(X, i):
            return X[:, 2 * i:2 * i + 2, :] if isinstance(i, int) else X[:, bass.ds(2 * i, 2), :]

        def hi2(X, i, base=0):
            if isinstance(i, int):
                return X[:, base + 2 * i:base + 2 * i + 2, 0:T]
            return X[:, bass.ds(2 * i + base, 2), 0:T]

        def lo2(X, i, base=0):
            if isinstance(i, int):
                return X[:, base + 2 * i:base + 2 * i + 2, T:2 * T]
            return X[:, bass.ds(2 * i + base, 2), T:2 * T]

        @block.sync
        def _(sp):
            c = Counts(sp, "sp", turns, real)

            def load(grp, i):
                col = grp.col + grp.step * i if grp.step else grp.col
                cols = slice(col, col + COLS) if isinstance(col, int) else bass.ds(col, COLS)
                for k, nk in grp.units():
                    u = c.n.get("unit", 0)
                    if u >= SLOTS:
                        sp.wait_ge(s.lo, c.value("unit", 1 - SLOTS))
                    sp.dma_start(RAW[:, u % SLOTS, 0:nk, :], grp.W[:, k:k + nk, cols])\
                        .then_inc(raw_sems[u % SLOTS], 16)
                    c.add("unit")

            for ph in phases:
                def turn(i):
                    for grp in ph.body:
                        load(grp, i)
                if ph.n:
                    turn(0)
                    c.loop(1, ph.n, turn)
            for g in range(DC // 2):
                sp.wait_ge(s.tpd, 8 + 1 + 1 + g + 1)
                sp.dma_start(A["out"][0].rearrange("(b p) d -> p b d", p=P)[:, :, COLS * g:COLS * g + COLS],
                             OUTV[:, :, COLS * g:COLS * g + COLS]).then_inc(s.out, 16)
            sp.wait_ge(s.out, 16 * (DC // 2))

        BDS = RT[:, :].rearrange("p (s m n) -> p s m n", s=4, m=2)

        @block.gpsimd
        def _(pool):
            n = 0
            for i, (j0, pieces) in enumerate(strips):
                if i == 0:
                    pool.wait_ge(s.evac, GATES_FROM)
                if i >= 4:
                    pool.wait_ge(s.bd, last_user[i - 4] + 1)
                nc.gpsimd.memset(BDS[:, i % 4, :, :], 0.0).then_inc(s.wiped, 1)
                pool.wait_ge(s.wiped, i + 1)
                for n, r0, r1 in pieces:
                    at = RB * n - P * j0
                    for m, w in enumerate((A["w_rg_a"], A["w_rg_x"])):
                        pool.dma_start(BDS[r0 - P * i:r1 - P * i, i % 4, m, at:at + RB],
                                       w[0, n, r0 - RB * n:r1 - RB * n, :]).then_inc(strip_sems[i % 4], 16)

        strip_due = []
        _c = [0] * 4
        for i, (j0, pieces) in enumerate(strips):
            _c[i % 4] += 32 * len(pieces)
            strip_due.append(_c[i % 4])

        @block.scalar
        def _(act):
            c = Counts(act, "act", turns, real)

            def done(ins):
                ins.then_inc(s.achain, 1)
                act.wait_ge(s.achain, c.next("achain"))

            def split(grp):
                for k, nk in grp.units():
                    u = c.n.get("unit", 0)
                    act.wait_ge(raw_sems[u % SLOTS], c.value("unit", SLOTS, div=SLOTS, mul=16))
                    if u >= SLOTS:
                        act.wait_ge(s.unit, c.value("unit", 1 - SLOTS))
                    nc.scalar.activation(WH[:, u % SLOTS, 0:nk, :], RAW[:, u % SLOTS, 0:nk, :], ACT.Copy)\
                        .then_inc(s.hi, 1)
                    c.add("unit")

            def evacuated():
                act.wait_ge(s.evac, c.next("evac"))

            def from_dve():
                act.wait_ge(s.dve, c.next("dve"))

            def g(n=None):
                return Gf[:, (c.n["evac"] - 1) % 2, :]

            def a_q(i):
                evacuated()
                nc.scalar.activation(SQ2[:, 0, :], QR[:, 0, :], ACT.Square).then_inc(s.sq, 1)
                act.wait_ge(s.sq, c.next("sq"))

            def a_k(i):
                evacuated()
                nc.scalar.activation(SQ2[:, 1, :], QR[:, 1, :], ACT.Square).then_inc(s.sq, 1)
                act.wait_ge(s.sq, c.next("sq"))

            def a_v(i):
                evacuated()
                act.wait_ge(s.rms, c.next("rms"))
                done(nc.scalar.activation(MS, PX[:, 0:2, :], ACT.Identity, scale=1.0 / P, bias=EPS))
                done(nc.scalar.activation(SQ2, MS, ACT.Ln))
                done(nc.scalar.activation(SQ2, SQ2, ACT.Exp, scale=-0.5))
                nc.scalar.activation(R2, SQ2, ACT.Square).then_inc(s.act, 1)
                act.wait_ge(s.act, c.next("act"))

            def a_soft():
                act.wait_ge(s.scores, c.next("scores"))
                done(nc.scalar.activation(L, PX[:, 0:2, 0:384], ACT.Abs))
                done(nc.scalar.activation(L, L, ACT.Exp, scale=-1.0))
                nc.scalar.activation(L, L, ACT.Ln, bias=1.0).then_inc(s.act, 1)
                act.wait_ge(s.act, c.next("act"))

            def a_w():
                from_dve()
                nc.scalar.activation(W, T1, ACT.Exp).then_inc(s.act, 1)
                act.wait_ge(s.act, c.next("act"))

            def a_o(i):
                act.wait_ge(s.heads, c.next("heads"))
                nc.scalar.activation(hi2(YH, i), PX[:, 3, :].rearrange("p (c t) -> p c t", t=T), ACT.Copy)\
                    .then_inc(s.act, 1)
                act.wait_ge(s.act, c.next("act"))

            def post_attn(i, j):
                m, what = divmod(j, 3)
                now = 2 * i + m
                before = not (isinstance(i, int) and now == 0)
                if what == 0:
                    a_q(now)
                    if before:
                        a_soft()
                elif what == 1:
                    a_k(now)
                    if before:
                        a_w()
                else:
                    a_v(now)
                    if before:
                        a_o(now - 1)

            def tanh_half(dst):
                evacuated()
                nc.scalar.activation(dst, g().rearrange("p (c t) -> p c t", t=T), ACT.Tanh, scale=0.5)\
                    .then_inc(s.act, 1)
                act.wait_ge(s.act, c.next("act"))

            def post_gate_a(i, j, at):
                if at == 0 and j == 0:
                    a_soft()
                if at == 0 and j == 1:
                    a_w()
                if at == 0 and j == 2:
                    a_o(7)
                tanh_half(pair(MIX, at + 2 * i + j))

            def post_plain(i, j):
                evacuated()

            def split_pair(X, i, src=None, base=0):
                from_dve()
                nc.scalar.activation(hi2(X, i, base), TT[:, 0, :, :] if src is None else src, ACT.Copy)\
                    .then_inc(s.act, 1)
                act.wait_ge(s.act, c.next("act"))

            def lru_gates():
                act.wait_ge(s.xc, RC)
                for j in range(RC):
                    act.wait_ge(s.bd, j + 1)
                    if j:
                        from_dve()
                    b = j % 4
                    done(nc.scalar.activation(TT[:, 0, 0, :], PX[:, b, 0:T], ACT.Tanh, scale=0.5,
                                              bias=der(D_HBA + j)))
                    nc.scalar.activation(Gf[:, b // 2, T * (b % 2):T * (b % 2) + T], PX[:, b, T:2 * T], ACT.Tanh,
                                         scale=0.5, bias=der(D_HBX + j)).then_inc(s.bdd, 1)
                    act.wait_ge(s.bdd, c.next("bdd"))
                    nc.scalar.activation(AE[:, 0, j, :], TT[:, 0, 0, :], ACT.Exp, scale=der(D_NSP + j),
                                         bias=der(D_NSP + j))
                    nc.scalar.activation(TT[:, 0, 1, :], TT[:, 0, 0, :], ACT.Tanh, scale=der(D_SP + j),
                                         bias=der(D_SP + j)).then_inc(s.act, 1)
                    act.wait_ge(s.act, c.next("act"))

            def post_gate_r(i, j):
                if j == 0:
                    from_dve()
                    for n in range(0, RC, 11):
                        nc.scalar.activation(AE[:, 1, n:n + 11, :], AE[:, 1, n:n + 11, :], ACT.Sqrt, scale=0.25)\
                            .then_inc(s.act, 1)
                        act.wait_ge(s.act, c.next("act"))
                tanh_half(pair(RTc, j))

            def post_g_r(i, j, at=0):
                evacuated()
                nc.scalar.activation(Tf[:, 0, :], g(), ACT.Square, scale=float(np.sqrt(GELU_C))).then_inc(s.act, 1)
                act.wait_ge(s.act, c.next("act"))
                from_dve()
                nc.scalar.activation(Tf[:, 1, :], Tf[:, 0, :], ACT.Tanh, scale=GELU_S).then_inc(s.act, 1)
                act.wait_ge(s.act, c.next("act"))
                split_pair(YH, at + 2 * i + j)

            def post_rnn_out(i, j):
                evacuated()
                from_dve()
                nc.scalar.activation(hi2(XH, 2 * i + j), pair(MIX, 2 * i + j), ACT.Copy).then_inc(s.act, 1)
                act.wait_ge(s.act, c.next("act"))

            def squares(i, j):
                evacuated()
                from_dve()
                nc.scalar.activation(pair(XC, 2 * i + j), pair(XRES, 2 * i + j), ACT.Square).then_inc(s.sq, 1)
                act.wait_ge(s.sq, c.next("sq"))

            def norm():
                act.wait_ge(s.ss, c.next("ss"))
                nc.scalar.activation(Gf[:, 0, 0:T], PX[:, 0, 0:T], ACT.Sqrt, scale=1.0 / D, bias=EPS_AP)\
                    .then_inc(s.act, 1)
                act.wait_ge(s.act, c.next("act"))
                for q in range(DC // 2):
                    from_dve()
                    nc.scalar.activation(hi2(XH, q), TT[:, q % 2, :, :], ACT.Copy).then_inc(s.act, 1)
                    act.wait_ge(s.act, c.next("act"))

            def post_gu(i, j, at=0):
                evacuated()
                if j % 2 == 1:
                    return
                nc.scalar.activation(Tf[:, 0, :], g(), ACT.Tanh, scale=0.5).then_inc(s.act, 1)
                act.wait_ge(s.act, c.next("act"))

            def post_gu_u(n):
                split_pair(YH, n, TT[:, 1, :, :])

            def tables():
                act.wait_ge(s.op, OPS_MIX)
                act.dma_start(MIXf[0:NBUCK, 3072:3072 + HEADS2], A["rel_bias_2"]).then_inc(s.tab, 16)
                act.dma_start(MIXf[0:NBUCK, 3100:3484], A["c_onehot"]).then_inc(s.tab, 16)
                act.dma_start(MIXf[0:HEADS2, 3500:3884], A["c_add"]).then_inc(s.tab, 16)
                act.dma_start(RT[:, 3072:3584].rearrange("p (b d) -> p b d", b=NB),
                              A["p"][0, 0].rearrange("(b p) d -> p b d", p=P)).then_inc(s.p_in, 16)

            def norm_ffn():
                norm()
                act.wait_ge(s.tpd, TPD_STRIP)
                act.dma_start(strip_dram, MIXf[0:HEADS2, 3500:3884]).then_inc(s.strip, 16)
                act.wait_ge(s.strip, 16)
                for h in range(HEADS2):
                    rows = strip_dram[h, :]
                    toeplitz = bass.AP(tensor=rows.tensor, offset=rows.offset, ap=[[1, P], [1, T]])
                    act.dma_start(MIXf[:, T * h:T * h + T], toeplitz).then_inc(s.tb, 16)

            def ple():
                act.wait_ge(s.tp, TP_P)
                nc.scalar.activation(hi2(YH, 0), PX[:, 1, :].rearrange("p (c t) -> p c t", t=T), ACT.Copy)\
                    .then_inc(s.act, 1)
                act.wait_ge(s.act, c.next("act"))
                norm()

            def post_ple_gate(i, j):
                evacuated()
                nc.scalar.activation(Tf[:, 0, :], g(), ACT.Tanh, scale=0.5).then_inc(s.act, 1)
                act.wait_ge(s.act, c.next("act"))
                from_dve()
                nc.scalar.activation(hi2(YH, 2 * i + j), pair(XRES, 2 * i + j), ACT.Copy).then_inc(s.act, 1)
                act.wait_ge(s.act, c.next("act"))

            def post_conf(i, j):
                evacuated()
                if j in (1, 3):
                    nc.scalar.activation(Tf[:, 0, :], g(), ACT.Tanh, scale=0.5).then_inc(s.act, 1)
                    act.wait_ge(s.act, c.next("act"))
                if j in (4, 5):
                    nc.scalar.activation(Tf[:, 0, :], g(), ACT.Tanh, scale=0.5).then_inc(s.act, 1)
                    act.wait_ge(s.act, c.next("act"))

            def soft(n):
                for x in range(n):
                    from_dve()
                    for b, (lo, up) in enumerate(((0, P), (P, 3 * P))):
                        last = nc.scalar.activation(S4[:, x, lo:up], S4[:, x, lo:up], ACT.Exp,
                                                    bias=der(D_RED + 2 * x + b),
                                                    accum_out=der(D_RED + 8 + 2 * x + b))
                        last.then_inc(s.act, 1)
                        act.wait_ge(s.act, c.next("act"))

            def silu_gate():
                evacuated()
                nc.scalar.activation(Tf[:, 0, :], g(), ACT.Tanh, scale=0.5).then_inc(s.act, 1)
                act.wait_ge(s.act, c.next("act"))

            def diff_squares():
                from_dve()
                nc.scalar.activation(SQa, OA, ACT.Square).then_inc(s.sq, 1)
                act.wait_ge(s.sq, c.next("sq"))

            def diff_out(m):
                act.wait_ge(s.rms, c.next("rms"))
                done(nc.scalar.activation(Tf[:, 1, :], PX[:, 3, :], ACT.Ln, scale=1.0 / P, bias=EPS2_AP))
                nc.scalar.activation(Tf[:, 1, :], Tf[:, 1, :], ACT.Exp, scale=-0.5).then_inc(s.act, 1)
                act.wait_ge(s.act, c.next("act"))
                from_dve()
                nc.scalar.activation(hi2(XH, m), OA.rearrange("p (c t) -> p c t", t=T), ACT.Copy)\
                    .then_inc(s.act, 1)
                act.wait_ge(s.act, c.next("act"))

            def dil_out(i):
                from_dve()
                nc.scalar.activation(hi2(XH, i, base=4), OA.rearrange("p (c t) -> p c t", t=T), ACT.Copy)\
                    .then_inc(s.act, 1)
                act.wait_ge(s.act, c.next("act"))

            def post_diff(i, j):
                m, what = divmod(j, 4)
                if what == 0:
                    evacuated()
                    if m:
                        diff_squares()
                elif what == 1:
                    evacuated()
                    if m:
                        diff_out(m - 1)
                elif what == 2:
                    evacuated()
                    soft(4)
                else:
                    silu_gate()

            def post_dil(i, j):
                first = isinstance(i, int) and i == 0
                evacuated() if j < 3 else None
                if j == 0:
                    if first:
                        diff_squares()
                    else:
                        dil_out(i - 1)
                elif j == 1:
                    if first:
                        diff_out(1)
                elif j == 2:
                    soft(2)
                else:
                    silu_gate()

            def pw_norm():
                dil_out(3)
                from_dve()
                nc.scalar.activation(SC_SQ, CA, ACT.Square).then_inc(s.sq, 1)
                act.wait_ge(s.sq, c.next("sq"))
                act.wait_ge(s.sumsq, c.next("sumsq"))
                nc.scalar.activation(Gf[:, 0, 0:T], PX[:, 1, 0:T], ACT.Sqrt, scale=1.0 / 512, bias=EPS2_AP)\
                    .then_inc(s.act, 1)
                act.wait_ge(s.act, c.next("act"))
                from_dve()
                nc.scalar.activation(SC_SQ, CA, ACT.Tanh, scale=0.5).then_inc(s.act, 1)
                act.wait_ge(s.act, c.next("act"))
                from_dve()
                for q in range(2):
                    nc.scalar.activation(hi2(YH, q, base=DC), CA[:, 2 * q:2 * q + 2, :], ACT.Copy)\
                        .then_inc(s.act, 1)
                    act.wait_ge(s.act, c.next("act"))

            def post_pw(i, j):
                evacuated()
                split_pair(XH, j, base=12)

            def ln(l):
                from_dve()
                for q in range(8):
                    nc.scalar.activation(pair(XC, q), pair(XRES, q), ACT.Square).then_inc(s.sq, 1)
                    act.wait_ge(s.sq, c.next("sq"))
                act.wait_ge(s.sumsq, c.next("sumsq"))
                nc.scalar.activation(Gf[:, 0, 0:T], PX[:, 1, 0:T], ACT.Sqrt, scale=1.0 / D, bias=EPS2_AP)\
                    .then_inc(s.act, 1)
                act.wait_ge(s.act, c.next("act"))
                for q in range(8):
                    from_dve()
                    for e in range(2):
                        ch = 2 * q + e
                        last = nc.scalar.activation(XRES[:, ch, :], TT[:, q % 2, e, :], ACT.Identity,
                                                    bias=vec("ln_b_2", 16 * l + ch))
                    if l == 0:
                        done(last)
                    else:
                        last.then_inc(s.final, 1)
                        act.wait_ge(s.final, c.next("final"))
                    if l == 0:
                        nc.scalar.activation(hi2(YH, q), pair(XRES, q), ACT.Copy).then_inc(s.act, 1)
                        act.wait_ge(s.act, c.next("act"))

            act.dma_start(MATS[:, :], A["c_mats"]).then_inc(s.mats, 16)
            act.dma_start(F[:, 0:NB * D].rearrange("p (b d) -> p b d", b=NB),
                          A["x"][0].rearrange("(b p) d -> p b d", p=P)).then_inc(s.x_in, 16)
            row = 0
            for name, rows in VEC_ROWS:
                src = A[name].rearrange("a k (c p) -> (a k c) p", p=P) if len(A[name].shape) == 3 else \
                    A[name].rearrange("a (c p) -> (a c) p", p=P)
                at = 0
                while at < rows:
                    r = (row + at) % P
                    m = min(rows - at, P - r)
                    t = (row + at) // P
                    act.dma_start(RT[r:r + m, P * t:P * t + P], src[at:at + m, :]).then_inc(s.vecs, 16)
                    at += m
                row += rows
            act.dma_start(KEEP, A["c_keep"]).then_inc(s.keep, 16)
            act.dma_start(Fv[:, NB * D:NB * D + 512],
                          A["diff_lambda_2"].rearrange("l a d -> (l a d)").partition_broadcast(P)).then_inc(s.lam, 16)

            for q in range(DC // 2):
                act.wait_ge(s.tpd, q + 1)
                nc.scalar.activation(pair(MIX, q), pair(XRES, q), ACT.Square).then_inc(s.sq, 1)
                act.wait_ge(s.sq, c.next("sq"))
            act.wait_ge(s.tpd, DC // 2 + 1)
            for half, src in ((D_HBA, "b_rg_a"), (D_HBX, "b_rg_x")):
                nc.scalar.activation(der(half, RC), vec(src, 0, RC), ACT.Copy, scale=0.5)
            nc.scalar.activation(der(D_QG), vec("q_gain"), ACT.Copy, scale=QSCALE)
            for l in range(2):
                nc.scalar.activation(der(D_HG + l), vec("diff_head_gain_2", l), ACT.Copy, scale=1.0 - LAM_INIT[l])
            done(nc.scalar.activation(der(D_SP, RC), vec("lru_lambda", 0, RC), ACT.Abs))
            done(nc.scalar.activation(der(D_SP, RC), der(D_SP, RC), ACT.Exp, scale=-1.0))
            nc.scalar.activation(der(D_SP, RC), der(D_SP, RC), ACT.Ln, bias=1.0).then_inc(s.act, 1)
            act.wait_ge(s.act, c.next("act"))
            from_dve()
            nc.scalar.activation(der(D_RED, 4), der(D_RED, 4), ACT.Exp).then_inc(s.act, 1)
            act.wait_ge(s.act, c.next("act"))

            def post(name):
                return {
                    "attn": post_attn,
                    "gate_a0": lambda i, j: post_gate_a(i, j, 0),
                    "gate_a1": lambda i, j: post_gate_a(i, j, 4),
                    "attn_out": post_plain, "x_r": post_plain, "x_r_last": post_plain,
                    "gate_r": post_gate_r, "g_r": post_g_r,
                    "g_r_last": lambda i, j: post_g_r(i, j, 10),
                    "rnn_out": post_rnn_out, "w_o": squares,
                    "gu0": lambda i, j: post_gu_step(i, j, 0), "gu1": lambda i, j: post_gu_step(i, j, 0),
                    "gu_last0": lambda i, j: post_gu_step(i, j, 10), "gu_last1": lambda i, j: post_gu_step(i, j, 10),
                    "down0": post_plain, "down1": squares,
                    "ple_proj": post_plain, "ple_gate": post_ple_gate,
                    "conf": post_conf, "diff": post_diff, "dil": post_dil, "pw": post_pw, "out": post_plain,
                }.get(name) or post(name[:-1])

            def post_gu_step(i, j, at):
                post_gu(i, j)
                if j % 2 == 1:
                    post_gu_u(at + 2 * i + j // 2)

            between = {"lru_gates": lru_gates, "tables": tables, "norm_ffn": norm_ffn, "norm_ple": ple,
                       "pw_norm0": pw_norm, "pw_norm1": pw_norm, "ln0": lambda: ln(0), "ln1": lambda: ln(1)}
            pending = [norm]
            for ph in phases:
                if ph.name in between:
                    pending.append(between[ph.name])
                    continue
                fn, J = post(ph.name), len(ph.body)
                for j, grp in enumerate(ph.body):
                    split(grp)
                    for job in pending:
                        job()
                    pending = [lambda fn=fn, j=j: fn(0, j)]

                def turn(i):
                    for j, grp in enumerate(ph.body):
                        split(grp)
                        fn(i - 1, J - 1) if j == 0 else fn(i, j - 1)
                c.loop(1, ph.n, turn)
                pending = [lambda fn=fn, n=ph.n, J=J: fn(n - 1, J - 1)]
            for job in pending:
                job()

        @block.vector
        def _(dve):
            c = Counts(dve, "dve", turns, real)
            V_ = nc.vector

            def done(ins):
                ins.then_inc(s.chain, 1)
                dve.wait_ge(s.chain, c.next("chain"))

            def split(grp):
                for k, nk in grp.units():
                    u = c.n.get("unit", 0)
                    dve.wait_ge(s.hi, c.value("unit", 1))
                    V_.tensor_tensor(WL[:, u % SLOTS, 0:nk, :], RAW[:, u % SLOTS, 0:nk, :],
                                     WH[:, u % SLOTS, 0:nk, :].bitcast(fp), ALU.subtract).then_inc(s.lo, 1)
                    c.add("unit")

            def from_act(m=1):
                dve.wait_ge(s.act, c.next("act", m))

            def evacuate(grp, dst=None):
                par = c.n.get("group", 0) % 2
                dve.wait_ge(s.unit, c.next("seen", len(grp.units())))
                out = G[:, par, :, :] if dst is None else dst
                V_.reduce_sum(out, PG[:, 2 * par:2 * par + 2, :].rearrange("p b (h t) -> p b t h", h=2), AX)\
                    .then_inc(s.evac, 1)
                c.add("group")
                dve.wait_ge(s.evac, c.value("group"))
                return Gf[:, par, :]

            def two(ap):
                return ap.rearrange("p (c t) -> p c t", t=T)

            def low(X, i, src, base=0):
                from_act()
                V_.tensor_tensor(lo2(X, i, base), src, hi2(X, i, base).bitcast(fp), ALU.subtract).then_inc(s.op, 1)
                dve.wait_ge(s.op, c.next("op"))

            def a_q(grp, i):
                evacuate(grp, two(QR[:, 0, :]))

            def a_k(grp, i):
                evacuate(grp, two(QR[:, 1, :]))

            def a_v(grp, i):
                evacuate(grp)
                from_act()
                done(V_.scalar_tensor_tensor(MS, MS, -0.5, R2, ALU.mult, ALU.mult))
                done(V_.scalar_tensor_tensor(SQ2, MS, 1.5, SQ2, ALU.add, ALU.mult))
                V_.scalar_tensor_tensor(QR[:, 0, :], QR[:, 0, :], der(D_QG), SQ2[:, 0, :], ALU.mult, ALU.mult)
                V_.scalar_tensor_tensor(QR[:, 1, :], QR[:, 1, :], vec("k_gain"), SQ2[:, 1, :], ALU.mult, ALU.mult)\
                    .then_inc(s.ready, 1)
                dve.wait_ge(s.ready, c.next("ready"))

            def a_soft():
                V_.tensor_copy(V, PX[:, 2, :].rearrange("p (a n) -> p a n", a=4))
                from_act()
                z = PX[:, 0:2, 0:384]
                done(V_.scalar_tensor_tensor(SP, z, 0.0, L, ALU.max, ALU.add))
                V_.tensor_tensor(T1, z, SP, ALU.subtract)
                V_.tensor_tensor(SP, SP, KEEP.unsqueeze(1).broadcast_to([P, 2, 384]), ALU.mult).then_inc(s.ready, 1)
                dve.wait_ge(s.ready, c.next("ready"))

            def a_w():
                dve.wait_ge(s.later, c.next("later"))
                V_.tensor_tensor(T1, T1, PX[:, 2:4, 0:384], ALU.subtract).then_inc(s.dve, 1)
                dve.wait_ge(s.dve, c.next("dve"))
                from_act()
                V_.tensor_tensor(W, W, KEEP.unsqueeze(1).broadcast_to([P, 2, 384]), ALU.mult).then_inc(s.ready, 1)
                dve.wait_ge(s.ready, c.next("ready"))

            def a_o(i):
                dve.wait_ge(s.heads, c.next("heads"))
                low(YH, i, two(PX[:, 3, :]))

            def post_attn(grp, i, j):
                m, what = divmod(j, 3)
                now = 2 * i + m
                before = not (isinstance(i, int) and now == 0)
                if what == 0:
                    if before:
                        dve.wait_ge(s.scores, c.next("scores"))
                    a_q(grp, now)
                    if before:
                        a_soft()
                elif what == 1:
                    a_k(grp, now)
                    if before:
                        a_w()
                else:
                    a_v(grp, now)
                    if before:
                        a_o(now - 1)

            def post_gate_a(grp, i, j, at):
                if at == 0 and j == 0:
                    dve.wait_ge(s.scores, c.next("scores"))
                    evacuate(grp)
                    a_soft()
                elif at == 0 and j == 1:
                    evacuate(grp)
                    a_w()
                elif at == 0 and j == 2:
                    evacuate(grp)
                    a_o(7)
                else:
                    evacuate(grp)
                from_act()

            def post_attn_out(grp, i, j):
                x = evacuate(grp)
                m = pair(MIX, 2 * i + j)
                V_.scalar_tensor_tensor(m, m, 1.0, two(x), ALU.add, ALU.mult)

            def post_x_r(grp, i, j, at=0):
                x = evacuate(grp)
                for e in range(2):
                    ch = 4 * i + 2 * j + e + at
                    src = x[:, e * T:e * T + T]
                    dst = XC[:, ch, :] if isinstance(ch, int) else XC[:, bass.ds(ch, 1), :].squeeze(1)
                    done(V_.tensor_scalar(dst, src, vec("conv_w", 3 * RC + ch), vec("conv_b", ch),
                                          ALU.mult, ALU.add))
                    for k in (2, 1, 0):
                        d = TAPS - 1 - k
                        part = dst[:, d:T]
                        ins = V_.scalar_tensor_tensor(part, src[:, 0:T - d], vec("conv_w", k * RC + ch), part,
                                                      ALU.mult, ALU.add)
                        if k:
                            done(ins)
                        else:
                            ins.then_inc(s.xc, 1)
                            dve.wait_ge(s.xc, c.next("xc"))

            def lru_gates():
                def finish(j):
                    b = j % 4
                    return V_.scalar_tensor_tensor(XC[:, j, :], Gf[:, b // 2, T * (b % 2):T * (b % 2) + T], 1.0,
                                                   XC[:, j, :], ALU.add, ALU.mult)
                for j in range(RC):
                    from_act()
                    done(V_.tensor_tensor(Tf[:, 1, 0:T], AE[:, 0, j, :], AE[:, 0, j, :], ALU.mult))
                    if j >= 3:
                        finish(j - 3)
                    V_.scalar_tensor_tensor(AE[:, 1, j, :], Tf[:, 1, 0:T], 1.0, TT[:, 0, 1, :], ALU.add, ALU.mult)\
                        .then_inc(s.dve, 1)
                    dve.wait_ge(s.dve, c.next("dve"))
                for j in range(RC - 3, RC):
                    done(finish(j))

            def scan(j):
                e = AE[:, 1, j, :]
                done(V_.tensor_tensor(e, e, XC[:, j, :], ALU.mult))
                V_.tensor_tensor_scan(XC[:, j, :], AE[:, 0, j, :], e, 0.0, ALU.mult, ALU.add)

            def post_gate_r(grp, i, j):
                if j == 0:
                    from_act(2)
                evacuate(grp)
                from_act()
                for n in range(3 * j, min(3 * j + 3, RC)):
                    scan(n)

            def post_g_r(grp, i, j, at=0):
                x = evacuate(grp)
                n = at + 2 * i + j
                from_act()
                V_.scalar_tensor_tensor(Tf[:, 0, :], Tf[:, 0, :], 1.0, x, ALU.add, ALU.mult).then_inc(s.dve, 1)
                dve.wait_ge(s.dve, c.next("dve"))
                from_act()
                done(V_.scalar_tensor_tensor(Tf[:, 1, :], Tf[:, 1, :], 1.0, x, ALU.add, ALU.mult))
                V_.tensor_tensor(TT[:, 0, :, :], TT[:, 1, :, :], pair(XC, n), ALU.mult).then_inc(s.dve, 1)
                dve.wait_ge(s.dve, c.next("dve"))
                low(YH, n, TT[:, 0, :, :])

            def post_rnn_out(grp, i, j):
                x = evacuate(grp)
                n = 2 * i + j
                r, m = pair(RTc, n), pair(MIX, n)
                done(V_.scalar_tensor_tensor(r, r, 1.0, two(x), ALU.add, ALU.mult))
                V_.scalar_tensor_tensor(m, r, 0.5, m, ALU.mult, ALU.add).then_inc(s.dve, 1)
                dve.wait_ge(s.dve, c.next("dve"))
                low(XH, n, m)

            def residual(grp, i, j, scale, tell=True):
                x = evacuate(grp)
                m = pair(XRES, 2 * i + j)
                ins = V_.scalar_tensor_tensor(m, two(x), scale, m, ALU.mult, ALU.add)
                if tell:
                    ins.then_inc(s.dve, 1)
                    dve.wait_ge(s.dve, c.next("dve"))

            def norm(gain):
                from_act()
                V_.reciprocal(Gf[:, 0, T:2 * T], Gf[:, 0, 0:T]).then_inc(s.chain, 1)
                dve.wait_ge(s.chain, c.next("chain"))
                for q in range(DC // 2):
                    for e in range(2):
                        ins = V_.scalar_tensor_tensor(TT[:, q % 2, e, :], XRES[:, 2 * q + e, :],
                                                      vec(gain, 2 * q + e), Gf[:, 0, T:2 * T], ALU.mult, ALU.mult)
                    ins.then_inc(s.dve, 1)
                    dve.wait_ge(s.dve, c.next("dve"))
                    if q:
                        low(XH, q - 1, TT[:, (q - 1) % 2, :, :])
                low(XH, DC // 2 - 1, TT[:, (DC // 2 - 1) % 2, :, :])

            def norm_ffn():
                dve.wait_ge(s.tab, 48)
                dve.wait_ge(s.tp, TP_STRIP)
                V_.tensor_tensor(MIXf[0:HEADS2, 3500:3884], PX[0:HEADS2, 1, 0:384], MIXf[0:HEADS2, 3500:3884],
                                 ALU.add).then_inc(s.tpd, 1)
                dve.wait_ge(s.tpd, c.next("tpd"))
                norm("g_ffn")

            def post_gu(grp, i, j, at=0):
                x = evacuate(grp)
                if j % 2 == 0:
                    from_act()
                    V_.scalar_tensor_tensor(Tf[:, 1, :], Tf[:, 0, :], 1.0, x, ALU.add, ALU.mult)\
                        .then_inc(s.chain, 1)
                    c.add("chain")
                else:
                    n = at + 2 * i + j // 2
                    dve.wait_ge(s.chain, c.value("chain"))
                    V_.scalar_tensor_tensor(Tf[:, 1, :], Tf[:, 1, :], 0.5, x, ALU.mult, ALU.mult).then_inc(s.dve, 1)
                    dve.wait_ge(s.dve, c.next("dve"))
                    low(YH, n, TT[:, 1, :, :])

            def ple():
                dve.wait_ge(s.tp, TP_P)
                low(YH, 0, two(PX[:, 1, :]))
                norm("g_ple")
                for h in range(HEADS2 // 2):
                    dve.wait_ge(s.flip, h + 1)
                    V_.tensor_copy(AB[:, 2 * h:2 * h + 2, :], two(PX[:, 2 + h % 2, :])).then_inc(s.flipped, 1)
                    dve.wait_ge(s.flipped, c.next("flipped"))

            def post_ple_proj(grp, i, j):
                evacuate(grp, pair(XC, j))

            def post_ple_gate(grp, i, j):
                evacuate(grp)
                n = 2 * i + j
                from_act()
                done(V_.scalar_tensor_tensor(TT[:, 1, :, :], TT[:, 0, :, :], 1.0, pair(XC, n), ALU.add, ALU.mult))
                x = pair(XRES, n)
                V_.scalar_tensor_tensor(x, TT[:, 1, :, :], 0.5, x, ALU.mult, ALU.add).then_inc(s.dve, 1)
                dve.wait_ge(s.dve, c.next("dve"))
                low(YH, n, x)

            def post_conf(grp, i, j, l):
                h = 2 * (j // 2)
                if j == 0:
                    done(V_.memset(HC[:, :, 0:32], 0.0))
                if j in (0, 2):
                    evacuate(grp, HC[:, h:h + 2, 32:32 + T])
                elif j in (1, 3):
                    evacuate(grp)
                    h = 2 * (j // 2)
                    from_act()
                    done(V_.tensor_scalar(Tf[:, 1, :], Tf[:, 0, :], 0.5, 0.5, ALU.mult, ALU.add))
                    x = HC[:, h:h + 2, 32:32 + T]
                    done(V_.tensor_tensor(x, x, TT[:, 1, :, :], ALU.mult))
                else:
                    x = evacuate(grp)
                    from_act()
                    V_.scalar_tensor_tensor(SC[:, 2 * (j - 4):2 * (j - 4) + 2, :], TT[:, 0, :, :], 1.0, two(x),
                                            ALU.add, ALU.mult)

            def taps(k, m, l):
                for t in range(m):
                    tap = k + t
                    for ch in range(CONVC):
                        row = (l * TAPS2) * CONVC + ch
                        at = tap * CONVC + row
                        off = tap + 2
                        src = HC[:, ch, off:off + T] if isinstance(tap, int) else \
                            HC[:, ch, bass.ds(off, T)]
                        if isinstance(tap, int) and tap == 0:
                            ins = V_.tensor_scalar(CA[:, ch, :], src, vec("conv_dw_2", at),
                                                   vec("conv_b_2", CONVC * l + ch), ALU.mult, ALU.add)
                        else:
                            ins = V_.scalar_tensor_tensor(CA[:, ch, :], src, vec("conv_dw_2", at), CA[:, ch, :],
                                                          ALU.mult, ALU.add)
                    done(ins)

            def scores(n, scale, head):
                for x in range(n):
                    h = head(x)
                    ab = AB[:, h, :] if isinstance(h, int) else AB[:, bass.ds(h, 1), :].squeeze(1)
                    V_.scalar_tensor_tensor(S4[:, x, 0:P], PX[:, x, 0:P], scale, ab[:, P:2 * P], ALU.mult, ALU.add)
                    done(V_.scalar_tensor_tensor(S4[:, x, P:3 * P], PX[:, x, P:3 * P], scale, ab, ALU.mult, ALU.add))
                    V_.tensor_reduce(der(D_RED + 2 * x), S4[:, x, 0:P], AX, ALU.max, negate=True)
                    V_.tensor_reduce(der(D_RED + 2 * x + 1), S4[:, x, P:3 * P], AX, ALU.max, negate=True)\
                        .then_inc(s.dve, 1)
                    dve.wait_ge(s.dve, c.next("dve"))

            def inverse_sums(n):
                from_act(2 * n)
                done(V_.reciprocal(der(D_RED + 16, 2 * n), der(D_RED + 8, 2 * n)))

            def transposed():
                dve.wait_ge(s.turned, c.next("turned"))
                V_.tensor_copy(V, PX[:, 2, :].rearrange("p (a n) -> p a n", a=4))
                V_.tensor_copy(PTS, PX[:, 0:2, 0:384]).then_inc(s.ready, 1)
                dve.wait_ge(s.ready, c.next("ready"))

            def gate(grp):
                x = evacuate(grp)
                from_act()
                V_.scalar_tensor_tensor(SG, Tf[:, 0, :], 1.0, x, ALU.add, ALU.mult)
                transposed()

            def gated():
                dve.wait_ge(s.heads2, c.next("heads2"))
                V_.scalar_tensor_tensor(OA, PX[:, 3, :], 0.5, SG, ALU.mult, ALU.mult).then_inc(s.dve, 1)
                dve.wait_ge(s.dve, c.next("dve"))

            def diff_gated():
                dve.wait_ge(s.heads2, c.next("heads2"))
                V_.tensor_copy(OA, PX[:, 3, :]).then_inc(s.dve, 1)
                dve.wait_ge(s.dve, c.next("dve"))

            def diff_out(m, l):
                from_act()
                done(V_.scalar_tensor_tensor(OA, OA, der(D_HG + l), Tf[:, 1, :], ALU.mult, ALU.mult))
                V_.scalar_tensor_tensor(OA, OA, 0.5, SG, ALU.mult, ALU.mult).then_inc(s.dve, 1)
                dve.wait_ge(s.dve, c.next("dve"))
                low(XH, m, two(OA))

            def post_diff(grp, i, j, l):
                m, what = divmod(j, 4)
                if what == 0:
                    evacuate(grp, two(QR[:, 0, :]))
                    if m:
                        diff_gated()
                elif what == 1:
                    evacuate(grp, two(QR[:, 1, :]))
                    if m:
                        diff_out(m - 1, l)
                elif what == 2:
                    evacuate(grp)
                    dve.wait_ge(s.scores2, c.next("scores2"))
                    scores(4, ASCALE, lambda x: 2 * m + x // 2)
                    inverse_sums(4)
                    for h in range(2):
                        done(V_.tensor_scalar(der(D_RED + 16 + 4 * h + 2, 2), der(D_RED + 16 + 4 * h + 2, 2),
                                              der(D_NLAM + l), None, ALU.mult))
                        for b, (lo, up) in enumerate(((0, P), (P, 3 * P))):
                            x = S4[:, 2 * h, lo:up]
                            done(V_.tensor_scalar(x, x, der(D_RED + 16 + 4 * h + b), None, ALU.mult))
                            ins = V_.scalar_tensor_tensor(x, S4[:, 2 * h + 1, lo:up],
                                                          der(D_RED + 16 + 4 * h + 2 + b), x, ALU.mult, ALU.add)
                    ins.then_inc(s.ready, 1)
                    dve.wait_ge(s.ready, c.next("ready"))
                else:
                    gate(grp)
                if j:
                    taps(j - 1, 1, l)

            def post_dil(grp, i, j, l):
                first = isinstance(i, int) and i == 0
                if j == 0:
                    evacuate(grp, two(QR[:, 0, :]))
                    if first:
                        diff_gated()
                    else:
                        gated()
                        low(XH, i - 1, two(OA), base=4)
                elif j == 1:
                    evacuate(grp, two(QR[:, 1, :]))
                    if first:
                        diff_out(1, l)
                elif j == 2:
                    evacuate(grp)
                    dve.wait_ge(s.scores2, c.next("scores2"))
                    scores(2, QSCALE, lambda x: 2 * i + (4 + x))
                    inverse_sums(2)
                    for h in range(2):
                        for b, (lo, up) in enumerate(((0, P), (P, 3 * P))):
                            x = S4[:, h, lo:up]
                            ins = V_.tensor_scalar(x, x, der(D_RED + 16 + 2 * h + b), None, ALU.mult)
                    ins.then_inc(s.ready, 1)
                    dve.wait_ge(s.ready, c.next("ready"))
                else:
                    gate(grp)
                at, m = ((0, 2), (2, 1), (3, 2), (5, 1))[j]
                taps(6 * i + (7 + at), m, l)

            def pw_norm(l):
                gated()
                low(XH, 3, two(OA), base=4)
                dve.wait_ge(s.sum, c.next("sum"))
                done(V_.tensor_scalar(Gf[:, 0, T:2 * T], PX[:, 0, 0:T], -1.0 / 512, None, ALU.mult))
                V_.tensor_tensor(CA, CA, Gf[:, 0, T:2 * T].unsqueeze(1).broadcast_to([P, CONVC, T]), ALU.add)\
                    .then_inc(s.dve, 1)
                dve.wait_ge(s.dve, c.next("dve"))
                from_act()
                done(V_.reciprocal(Gf[:, 0, T:2 * T], Gf[:, 0, 0:T]))
                for ch in range(CONVC):
                    done(V_.scalar_tensor_tensor(CA[:, ch, :], CA[:, ch, :], vec("conv_ln_g_2", CONVC * l + ch),
                                                 Gf[:, 0, T:2 * T], ALU.mult, ALU.mult))
                    ins = V_.tensor_scalar(CA[:, ch, :], CA[:, ch, :], vec("conv_ln_b_2", CONVC * l + ch), None,
                                           ALU.add)
                ins.then_inc(s.dve, 1)
                dve.wait_ge(s.dve, c.next("dve"))
                from_act()
                done(V_.scalar_tensor_tensor(CA, SC_SQ, 1.0, CA, ALU.add, ALU.mult))
                V_.tensor_scalar(CA, CA, 0.5, None, ALU.mult).then_inc(s.dve, 1)
                dve.wait_ge(s.dve, c.next("dve"))
                for q in range(2):
                    low(YH, q, CA[:, 2 * q:2 * q + 2, :], base=DC)

            def post_pw(grp, i, j):
                x = evacuate(grp)
                V_.scalar_tensor_tensor(TT[:, 0, :, :], two(x), 0.5, SC[:, 2 * j:2 * j + 2, :], ALU.mult, ALU.mult)\
                    .then_inc(s.dve, 1)
                dve.wait_ge(s.dve, c.next("dve"))
                low(XH, j, TT[:, 0, :, :], base=12)

            def post_out(grp, i, j):
                x = evacuate(grp)
                m = pair(XRES, 2 * i + j)
                V_.scalar_tensor_tensor(m, m, ALPHA, two(x), ALU.mult, ALU.add).then_inc(s.sums, 1)
                dve.wait_ge(s.sums, c.next("sums"))

            def ln(l):
                dve.wait_ge(s.sum, c.next("sum"))
                done(V_.tensor_scalar(Gf[:, 0, T:2 * T], PX[:, 0, 0:T], -1.0 / D, None, ALU.mult))
                V_.tensor_tensor(XRES[:, :, :], XRES[:, :, :],
                                 Gf[:, 0, T:2 * T].unsqueeze(1).broadcast_to([P, DC, T]), ALU.add).then_inc(s.dve, 1)
                dve.wait_ge(s.dve, c.next("dve"))
                from_act()
                done(V_.reciprocal(Gf[:, 0, T:2 * T], Gf[:, 0, 0:T]))
                for q in range(DC // 2):
                    if q >= 2:
                        if l == 0:
                            low(YH, q - 2, pair(XRES, q - 2))
                        else:
                            dve.wait_ge(s.final, q - 1)
                    for e in range(2):
                        ins = V_.scalar_tensor_tensor(TT[:, q % 2, e, :], XRES[:, 2 * q + e, :],
                                                      vec("ln_g_2", DC * l + 2 * q + e), Gf[:, 0, T:2 * T],
                                                      ALU.mult, ALU.mult)
                    ins.then_inc(s.dve, 1)
                    dve.wait_ge(s.dve, c.next("dve"))
                for q in (6, 7):
                    if l == 0:
                        low(YH, q, pair(XRES, q))

            for q in range(DC // 2):
                dve.wait_ge(s.tp, q + 1)
                V_.tensor_copy(pair(XRES, q), two(PG[:, q % 4, :])).then_inc(s.tpd, 1)
                dve.wait_ge(s.tpd, c.next("tpd"))
            dve.wait_ge(s.tp, DC // 2 + 1)
            V_.tensor_copy(VEC[:, 0:512], PX[:, 2, :])
            V_.tensor_copy(VEC[:, 512:VEC_N], PX[:, 3, 0:VEC_N - 512]).then_inc(s.tpd, 1)
            dve.wait_ge(s.tpd, DC // 2 + 1)
            from_act()
            done(V_.tensor_scalar(Tf[:, 0, 0:RC], vec("lru_lambda", 0, RC), 0.0, None, ALU.min))
            done(V_.tensor_tensor(der(D_SP, RC), der(D_SP, RC), Tf[:, 0, 0:RC], ALU.subtract))
            done(V_.tensor_scalar(der(D_SP, RC), der(D_SP, RC), LRU_HALF_C, None, ALU.mult))
            V_.tensor_scalar(der(D_NSP, RC), der(D_SP, RC), -1.0, None, ALU.mult)
            dve.wait_ge(s.lam, 16)
            lam = Fv[:, NB * D:NB * D + 512].rearrange("p (g two d) -> p g two d", two=2, d=64)
            done(V_.tensor_tensor(Tf[:, 1, 0:256].rearrange("p (g d) -> p g d", d=64), lam[:, :, 0, :],
                                  lam[:, :, 1, :], ALU.mult))
            V_.reduce_sum(der(D_RED, 4), Tf[:, 1, 0:256].rearrange("p (g d) -> p g d", d=64), AX).then_inc(s.dve, 1)
            dve.wait_ge(s.dve, c.next("dve"))
            from_act()
            for l in range(2):
                done(V_.tensor_tensor(der(D_NLAM + l), der(D_RED + 2 * l + 1), der(D_RED + 2 * l), ALU.subtract))
                done(V_.tensor_scalar(der(D_NLAM + l), der(D_NLAM + l), -LAM_INIT[l], None, ALU.add))

            def post(name):
                return {
                    "attn": post_attn,
                    "gate_a0": lambda g_, i, j: post_gate_a(g_, i, j, 0),
                    "gate_a1": lambda g_, i, j: post_gate_a(g_, i, j, 4),
                    "attn_out": post_attn_out, "x_r": post_x_r,
                    "x_r_last": lambda g_, i, j: post_x_r(g_, i, j, 20),
                    "gate_r": post_gate_r, "g_r": post_g_r,
                    "g_r_last": lambda g_, i, j: post_g_r(g_, i, j, 10),
                    "rnn_out": post_rnn_out, "w_o": lambda g_, i, j: residual(g_, i, j, 0.5),
                    "gu0": post_gu, "gu1": post_gu,
                    "gu_last0": lambda g_, i, j: post_gu(g_, i, j, 10),
                    "gu_last1": lambda g_, i, j: post_gu(g_, i, j, 10),
                    "down0": lambda g_, i, j: residual(g_, i, j, 1.0, False),
                    "down1": lambda g_, i, j: residual(g_, i, j, 1.0),
                    "ple_proj": post_ple_proj, "ple_gate": post_ple_gate,
                    "conf0": lambda g_, i, j: post_conf(g_, i, j, 0), "conf1": lambda g_, i, j: post_conf(g_, i, j, 1),
                    "diff0": lambda g_, i, j: post_diff(g_, i, j, 0), "diff1": lambda g_, i, j: post_diff(g_, i, j, 1),
                    "dil0": lambda g_, i, j: post_dil(g_, i, j, 0), "dil1": lambda g_, i, j: post_dil(g_, i, j, 1),
                    "pw0": post_pw, "pw1": post_pw, "out0": post_out, "out1": post_out,
                }[name]

            between = {"lru_gates": lru_gates, "tables": lambda: None, "norm_ffn": norm_ffn, "norm_ple": ple,
                       "pw_norm0": lambda: pw_norm(0), "pw_norm1": lambda: pw_norm(1),
                       "ln0": lambda: ln(0), "ln1": lambda: ln(1)}
            pending = [lambda: norm("g_mix")]
            for ph in phases:
                if ph.name in between:
                    pending.append(between[ph.name])
                    continue
                fn, J, B = post(ph.name), len(ph.body), ph.body
                for j, grp in enumerate(B):
                    split(grp)
                    for job in pending:
                        job()
                    pending = [lambda fn=fn, grp=grp, j=j: fn(grp, 0, j)]

                def turn(i):
                    for j, grp in enumerate(B):
                        split(grp)
                        fn(B[J - 1], i - 1, J - 1) if j == 0 else fn(B[j - 1], i, j - 1)
                c.loop(1, ph.n, turn)
                pending = [lambda fn=fn, B=B, n=ph.n, J=J: fn(B[J - 1], n - 1, J - 1)]
            for job in pending:
                job()
            for q in range(DC // 2):
                dve.wait_ge(s.tp, TP_OUT + q + 1)
                V_.tensor_copy(OUTV[:, :, COLS * q:COLS * q + COLS], PG[:, q % 4, :].rearrange(
                    "p (b n) -> p b n", b=NB)).then_inc(s.tpd, 1)
                dve.wait_ge(s.tpd, c.next("tpd"))

        @block.tensor
        def _(pe):
            c = Counts(pe, "pe", turns, real)
            mm = nc.tensor.matmul

            def group(grp, fresh):
                par = c.n.get("group", 0) % 2
                if c.n.get("group", 0) >= 2:
                    pe.wait_ge(s.evac, c.value("group", -1))
                if fresh == "all":
                    pe.wait_ge(s.op, c.next("op", 2))
                k = 0
                for k0, nk in grp.units():
                    slot = c.n.get("unit", 0) % SLOTS
                    pe.wait_ge(s.lo, c.value("unit", 1))
                    if fresh is True:
                        pe.wait_ge(s.op, c.next("op", nk // 2))
                    for kk in range(nk):
                        x = grp.X[:, grp.base + k, :]
                        for j in range(2):
                            b = 2 * par + j
                            cs = slice(P * j, P * j + P)
                            mm(PG[:, b, :], WH[:, slot, kk, cs], x, start=k == 0, stop=False)
                            last = mm(PG[:, b, T:2 * T], WL[:, slot, kk, cs], x[:, 0:T], start=False,
                                      stop=k == grp.K - 1)
                        k += 1
                    last.then_inc(s.unit, 1)
                    c.add("unit")
                c.add("group")

            def ready():
                pe.wait_ge(s.ready, c.next("ready"))

            def squares_in(m=1):
                pe.wait_ge(s.sq, c.next("sq", m))

            def sum_features(bank, src, first, last):
                return mm(PX[:, bank, 0:src.shape[-1]], ONES, src, start=first, stop=last)

            def v_transposes(par):
                for h in range(2):
                    for b in range(NB):
                        at = P * (2 * h + b)
                        last = nc.tensor.transpose(PX[:, 2, at:at + P], G[:, par, h, P * b:P * b + P], IDENT)
                return last

            def z_attn():
                ready()
                for h in range(2):
                    o = T * h
                    mm(PX[:, h, 0:T], QR[:, 1, o:o + P], QR[:, 0, o:o + T], start=True, stop=True)
                    mm(PX[:, h, T:T + P], QR[:, 1, o + P:o + T], QR[:, 0, o + P:o + T], start=True, stop=True)
                v_transposes(c.n["group"] % 2).then_inc(s.scores, 1)

            def e_attn():
                ready()
                for h in range(2):
                    mm(PX[:, 2 + h, T:T + P], AFTER, SP[:, h, T:T + P], start=True, stop=True)
                    mm(PX[:, 2 + h, 0:T], AFTER, SP[:, h, 0:T], start=True, stop=False)
                    last = mm(PX[:, 2 + h, P:T], ONES, SP[:, h, T:T + P], start=False, stop=True)
                last.then_inc(s.later, 1)

            def heads_out(tell):
                ready()
                for h in range(2):
                    o = T * h
                    mm(PX[:, 3, o:o + T], V[:, 2 * h, :], W[:, h, 0:T], start=True, stop=False)
                    last = mm(PX[:, 3, o + P:o + T], V[:, 2 * h + 1, :], W[:, h, T:T + P], start=False, stop=True)
                last.then_inc(tell, 1)

            def after_attn(i, j):
                m, what = divmod(j, 3)
                before = not (isinstance(i, int) and i == 0 and m == 0)
                if what == 0:
                    if before:
                        z_attn()
                elif what == 1:
                    if before:
                        e_attn()
                    squares_in()
                    sum_features(0, SQ2[:, 0, :], True, True)
                else:
                    if before:
                        heads_out(s.heads)
                    squares_in()
                    sum_features(1, SQ2[:, 1, :], True, True).then_inc(s.rms, 1)

            def after_gate_a0(i, j):
                if j == 0:
                    z_attn()
                elif j == 1:
                    e_attn()
                elif j == 2:
                    heads_out(s.heads)

            def lru_gates():
                for j in range(RC):
                    if j >= 4:
                        pe.wait_ge(s.bdd, j - 3)
                    for m in range(2):
                        for i in users[j]:
                            if m == 0:
                                pe.wait_ge(s.xc, i + 1)
                                pe.wait_ge(strip_sems[i % 4], strip_due[i])
                            at = P * (j - strips[i][0])
                            last = mm(PX[:, j % 4, T * m:T * m + T], BDS[:, i % 4, m, at:at + P], XC[:, i, :],
                                      start=i == users[j][0], stop=i == users[j][-1])
                    last.then_inc(s.bd, 1)

            def add_pair(src, q, bank, first, last):
                if src is XRES:
                    pe.wait_ge(s.sums, c.next("sums"))
                else:
                    squares_in()
                for e in range(2):
                    ch = 2 * q + e
                    x = src[:, ch, :] if isinstance(ch, int) else src[:, bass.ds(ch, 1), :].squeeze(1)
                    ins = sum_features(bank, x, first and e == 0, last and e == 1)
                return ins

            def after_sum(src):
                def after(i, j):
                    if j == 0 and isinstance(i, int) and i == 0:
                        return
                    g = 2 * i + j - 1
                    add_pair(src, g, 0, isinstance(g, int) and g == 0, False)
                return after

            def norm_ffn():
                add_pair(XC, 7, 0, False, True).then_inc(s.ss, 1)
                pe.wait_ge(s.tab, 48)
                mm(PX[0:HEADS2, 1, 0:384], MIXf[0:NBUCK, 3072:3072 + HEADS2], MIXf[0:NBUCK, 3100:3484],
                   start=True, stop=True).then_inc(s.tp, 1)

            def norm_ple():
                add_pair(XC, 7, 0, False, True).then_inc(s.ss, 1)
                pe.wait_ge(s.p_in, 16)
                for k in range(2):
                    for b in range(NB):
                        at = T * k + P * b
                        last = nc.tensor.transpose(PX[:, 1, at:at + P],
                                                   RT[:, 3072 + T * b + P * k:3072 + T * b + P * k + P], IDENT)
                last.then_inc(s.tp, 1)
                pe.wait_ge(s.tb, 16 * HEADS2)
                for h in range(HEADS2 // 2):
                    if h >= 2:
                        pe.wait_ge(s.flipped, h - 1)
                    mm(PX[:, 2 + h % 2, :], FLIP, MIXf[:, 512 * h:512 * h + 512], start=True, stop=True)\
                        .then_inc(s.flip, 1)

            def z_soft(comps):
                for h in range(2):
                    for x in range(comps):
                        r = slice(P // comps * x, P // comps * (x + 1))
                        bank, o = comps * h + x, T * h
                        mm(PX[:, bank, 0:P], QR[r, 0, o:o + P], QR[r, 1, o:o + P], start=True, stop=True)
                        last = mm(PX[:, bank, P:3 * P], QR[r, 0, o + P:o + T], QR[r, 1, o:o + T],
                                  start=True, stop=True)
                last.then_inc(s.scores2, 1)

            def pt_soft(comps):
                ready()
                for h in range(2):
                    x = S4[:, comps * h, :]
                    for to, frm in ((0, 0), (P, P), (2 * P, 2 * P)):
                        nc.tensor.transpose(PX[:, h, to:to + P], x[:, frm:frm + P], IDENT)
                v_transposes(c.n["group"] % 2).then_inc(s.turned, 1)

            def diff_sum():
                squares_in()
                sum_features(3, SQa, True, True).then_inc(s.rms, 1)

            def after_diff(i, j):
                m, what = divmod(j, 4)
                if what == 0 and m:
                    heads_out(s.heads2)
                elif what == 1 and m:
                    diff_sum()
                elif what == 2:
                    evac_of_k()
                    if m:
                        pe.wait_ge(s.op, c.value("op", m))
                    z_soft(2)
                elif what == 3:
                    pt_soft(2)

            def evac_of_k():
                pe.wait_ge(s.evac, c.value("group", -1))

            def after_dil(i, j):
                first = isinstance(i, int) and i == 0
                if j == 0:
                    heads_out(s.heads2)
                elif j == 1:
                    if first:
                        diff_sum()
                elif j == 2:
                    evac_of_k()
                    z_soft(1)
                else:
                    pt_soft(1)

            def pw_norm():
                heads_out(s.heads2)
                pe.wait_ge(s.op, c.next("op", 6))
                for ch in range(CONVC):
                    last = sum_features(0, CA[:, ch, :], ch == 0, ch == CONVC - 1)
                last.then_inc(s.sum, 1)
                squares_in()
                for ch in range(CONVC):
                    last = sum_features(1, SC_SQ[:, ch, :], ch == 0, ch == CONVC - 1)
                last.then_inc(s.sumsq, 1)

            def ln(l):
                add_pair(XRES, 7, 0, False, True).then_inc(s.sum, 1)
                for q in range(8):
                    last = add_pair(XC, q, 1, q == 0, q == 7)
                last.then_inc(s.sumsq, 1)

            after = {"attn": after_attn, "gate_a0": after_gate_a0, "w_o": after_sum(XC), "down1": after_sum(XC),
                     "diff0": after_diff, "diff1": after_diff, "dil0": after_dil, "dil1": after_dil,
                     "out0": after_sum(XRES), "out1": after_sum(XRES)}
            between = {"lru_gates": lru_gates, "tables": lambda: None, "norm_ffn": norm_ffn,
                       "norm_ple": norm_ple, "pw_norm0": pw_norm,
                       "pw_norm1": pw_norm, "ln0": lambda: ln(0), "ln1": lambda: ln(1)}

            pe.wait_ge(s.mats, 16)
            pe.wait_ge(s.x_in, 16)
            for q in range(DC // 2):
                if q >= 4:
                    pe.wait_ge(s.tpd, q - 3)
                for e in range(2):
                    for b in range(NB):
                        at = T * e + P * b
                        src = D * b + P * (2 * q + e)
                        last = nc.tensor.transpose(PG[:, q % 4, at:at + P], Fv[:, src:src + P], IDENT)
                last.then_inc(s.tp, 1)
            pe.wait_ge(s.vecs, 16 * VEC_DMAS)
            for t in range(VEC_TILES):
                m = min(P, VEC_N - P * t)
                last = nc.tensor.transpose(PX[:, 2 + t // 4, P * (t % 4):P * (t % 4) + m],
                                           RT[0:m, P * t:P * t + P], IDENT[0:m, 0:m])
            last.then_inc(s.tp, 1)
            for q in range(DC // 2):
                ins = add_pair(MIX, q, 0, q == 0, q == DC // 2 - 1)
            ins.then_inc(s.ss, 1)
            pe.wait_ge(s.tpd, DC // 2 + 1)

            for ph in phases:
                if ph.name in between:
                    between[ph.name]()
                    continue
                hook = after.get(ph.name)

                def turn(i):
                    for j, grp in enumerate(ph.body):
                        group(grp, ph.fresh if j == 0 and isinstance(i, int) and i == 0 else False)
                        if hook:
                            hook(i, j)
                turn(0)
                c.loop(1, ph.n, turn)
            for q in range(DC // 2):
                if not STOP:
                    pe.wait_ge(s.final, q + 1)
                if q >= 4:
                    pe.wait_ge(s.tpd, TPD_OUT + q - 3)
                for e in range(2):
                    for b in range(NB):
                        at = P * NB * 0 + T * b + P * e
                        last = nc.tensor.transpose(PG[:, q % 4, at:at + P], XRES[:, 2 * q + e, P * b:P * b + P],
                                                   IDENT)
                last.then_inc(s.tp, 1)


_INS = ["x", "p", "g_mix", "w_in", "conv_w", "conv_b", "w_rg_a", "b_rg_a", "w_rg_x", "b_rg_x", "lru_lambda",
        "q_gain", "k_gain", "w_rnn_out", "w_attn_out", "w_o", "g_ffn", "w_ffn_gu", "w_ffn_down", "g_ple",
        "w_ple_gate", "w_ple_proj", "w_in_2", "diff_lambda_2", "diff_head_gain_2", "conv_dw_2", "conv_b_2",
        "conv_ln_g_2", "conv_ln_b_2", "conv_pw_2", "w_out_2", "ln_g_2", "ln_b_2", "rel_bias_2"]


def kernel(**inputs):
    import concourse.bacc as _bacc
    from concourse.bass_utils import run_bass_kernel_spmd as _run

    data = {name: np.ascontiguousarray(inputs[name]) for name in _INS}
    data.update(zip(("c_mats", "c_keep", "c_onehot", "c_add"), shape_constants()))
    turns = {}
    for real in (False, True):
        nc = _bacc.Bacc("TRN2", target_bir_lowering=False, num_devices=1)
        arrays, A = {}, {}
        for name, a in data.items():
            arrays[f"in_{name}_dram"] = a
            A[name] = nc.dram_tensor(f"in_{name}_dram", a.shape, mybir.dt.from_np(a.dtype), kind="ExternalInput").ap()
        A["out"] = nc.dram_tensor("out_0_dram", (1, T, D), mybir.dt.float32, kind="ExternalOutput").ap()
        program(nc, A, turns, real)
    r = _run(nc, [arrays], core_ids=[0])
    return r.results[0]["out_0_dram"]
```

```python
import numpy as np
from contextlib import ExitStack
from collections import namedtuple
import concourse.bass as bass
from concourse import mybir

STOP = None

P = 128
T = 256
NB = T // P
D = 2048
DC = D // P
RNN = 2816
RC = RNN // P
RB = 176
TAPS = 4
FF = 5632
FF_PARTS = (16, 16, 12)
PLE = 256
TAPS2 = 31
COLS = 256
SLOTS = 4
UK = 4
NBUCK = 32
HEADS2 = 12
CONVC = 4
EPS = 1e-6
EPS2 = 1e-5
ALPHA = 4.0 ** 0.25
QSCALE = 128.0 ** -0.5
ASCALE = 64.0 ** -0.5
GELU_C = 0.044715
GELU_S = float(np.sqrt(2.0 / np.pi))
NEG = -1e30
LRU_HALF_C = 4.0
LAM_INIT = [0.8 - 0.6 * float(np.exp(-0.3 * layer)) for layer in range(2)]

VEC_ROWS = [("g_mix", 16), ("g_ffn", 16), ("g_ple", 16), ("conv_b", 22), ("conv_w", 88), ("b_rg_a", 22),
            ("b_rg_x", 22), ("lru_lambda", 22), ("q_gain", 1), ("k_gain", 1), ("diff_head_gain_2", 2),
            ("conv_dw_2", 248), ("conv_b_2", 8), ("conv_ln_g_2", 8), ("conv_ln_b_2", 8), ("ln_g_2", 32),
            ("ln_b_2", 32)]
VEC_AT, _n = {}, 0
for _name, _rows in VEC_ROWS:
    VEC_AT[_name] = _n
    _n += _rows
VEC_N = _n
VEC_TILES = (VEC_N + P - 1) // P


def t5_bucket_np(d):
    exact = NBUCK // 2
    df = np.maximum(d, 1).astype(np.float32)
    large = exact + (np.log(df / np.float32(exact)) / np.float32(np.log(2048 / exact))
                     * np.float32(NBUCK - exact)).astype(np.int32)
    return np.where(d < exact, d, np.minimum(large, NBUCK - 1))


def shape_constants():
    eye = np.eye(P, dtype=np.float32)
    after = np.tril(np.ones((P, P), np.float32), -1)
    ones = np.ones((P, P), np.float32)
    flip = np.ascontiguousarray(eye[:, ::-1])
    before = np.triu(np.ones((P, P), np.float32), 1)
    keep = np.concatenate([before, ones, before], 1)
    mats = np.concatenate([eye, after, ones, flip], 1)
    i = np.arange(384)
    dist = 255 - i
    onehot = (t5_bucket_np(np.maximum(dist, 0))[None] == np.arange(NBUCK)[:, None]).astype(np.float32)
    add = np.zeros((HEADS2, 384), np.float32)
    times = (dist <= 128).astype(int) + (dist % 4 == 0) + (dist % 16 == 0)
    add[4:] = np.where(times > 0, np.log(np.maximum(times, 1)), NEG)
    add[:, dist < 0] = NEG
    return mats, keep, onehot, add


class Counts:

    def __init__(self, eng, who, turns, real):
        self.eng, self.who, self.turns, self.real = eng, who, turns, real
        self.n, self.per, self.var, self.first, self.loops = {}, {}, None, 0, 0

    def add(self, key, m=1):
        self.n[key] = self.n.get(key, 0) + m

    def value(self, key, extra=0, div=1, mul=1):
        n = self.n.get(key, 0) + extra
        if self.var is None:
            return mul * (n // div)
        k = self.per.get(key, 0)
        if k == 0:
            return mul * (n // div)
        assert k % div == 0 or not self.real
        k //= div
        c = mul * (n // div - self.first * k)
        v = self.var * (mul * k) if mul * k != 1 else self.var
        return v + c if c >= 0 else v - (-c)

    def next(self, key, m=1, mul=1):
        self.add(key, m)
        return self.value(key, mul=mul)

    def loop(self, first, last, body):
        if last - first < 2:
            for i in range(first, last):
                body(i)
            return
        name = (self.who, self.loops)
        self.loops += 1
        start = dict(self.n)
        self.per = self.turns.get(name, {})
        self.first = first
        with self.eng.Fori(first, last) as i:
            self.var = i
            body(i)
        self.var = None
        met = {k: v - start.get(k, 0) for k, v in self.n.items()}
        assert not self.real or met == {k: self.per.get(k, 0) for k in met}, (name, met, self.per)
        self.turns[name] = met
        for k, v in met.items():
            self.n[k] = start.get(k, 0) + v * (last - first)


class Group:

    def __init__(self, W, K, col, step, X, base=0, turn=0):
        self.W, self.K, self.col, self.step, self.X, self.base, self.turn = W, K, col, step, X, base, turn

    def units(self):
        first = [(k, min(UK, self.K - k)) for k in range(0, self.K, UK)]
        return first[self.turn:] + first[:self.turn]


class Phase:

    def __init__(self, name, n, body, fresh=None):
        self.name, self.n, self.body, self.fresh = name, n, body, fresh or {}


def each_unit(K):
    return {0: [min(UK, K - k) // 2 for k in range(0, K, UK)]}


def gate_tiles():
    strips, users = [], [[] for _ in range(RC)]
    for i in range(RC):
        n0, n1 = P * i // RB, (P * i + P - 1) // RB
        j0 = RB * n0 // P
        pieces = [(n, max(P * i, RB * n), min(P * i + P, RB * (n + 1))) for n in range(n0, n1 + 1)]
        strips.append((j0, pieces))
        for j in range(RC):
            if any(RB * n < P * j + P and RB * (n + 1) > P * j for n in range(n0, n1 + 1)):
                users[j].append(i)
    return strips, users


def program(nc, A, turns, real):
    fp = mybir.dt.float32
    fr = mybir.dt.float32r
    ALU = mybir.AluOpType
    ACT = mybir.ActivationFunctionType
    AX = mybir.AxisListType.X
    ctx = ExitStack()
    with ctx:
        def sb(name, shape, dt=fp):
            return ctx.enter_context(nc.sbuf_tensor(name, shape, dt))

        RAW = sb("RAW", [P, SLOTS, UK, COLS])
        WH = sb("WH", [P, SLOTS, UK, COLS], fr)
        WL = sb("WL", [P, SLOTS, UK, COLS], fr)
        XRES = sb("XRES", [P, DC, T])
        XH = sb("XH", [P, DC, 2 * T], fr)
        with nc.sbuf_tensor("YH", [P, RC, 2 * T], fr) as YH:
            pass
        AL = sb("AL", [P, 2 * RC * T])
        MIX = sb("MIX", [P, DC, T])
        F = sb("F", [P, RC * T])
        RT = sb("RT", [P, 16 * T])
        G = sb("G", [P, 2, 2, T])
        TT = sb("TT", [P, 2, 2, T])
        MATS = sb("MATS", [P, 4 * P])
        VEC = sb("VEC", [P, VEC_TILES * P])
        DER = sb("DER", [P, 128])
        PG = ctx.enter_context(nc.psum_tensor("PG", [P, 4, 512], fp))
        PX = ctx.enter_context(nc.psum_tensor("PX", [P, 4, 512], fp))
        strip_dram = nc.dram_tensor("bias_strip", [HEADS2, 384], fp).ap()

        IDENT, AFTER, ONES, FLIP = (MATS[:, P * i:P * i + P] for i in range(4))
        Fv = F[:, :]
        XC = F[:, :].rearrange("p (c t) -> p c t", t=T)
        RTc = RT[:, :].rearrange("p (c t) -> p c t", t=T)
        Gf = G[:, :, :, :].rearrange("p a b t -> p a (b t)")
        Tf = TT[:, :, :, :].rearrange("p a b t -> p a (b t)")

        def vec(name, i=0, m=1):
            at = VEC_AT[name] + i
            return VEC[:, at:at + m] if isinstance(at, int) else VEC[:, bass.ds(at, m)]

        EPS_AP, EPS2_AP = EPS, EPS2
        VEC_DMAS = sum(1 + (at % P + rows - 1) // P for at, rows in
                       ((VEC_AT[n], r) for n, r in VEC_ROWS))
        TP_STRIP, TP_P, TP_OUT = DC // 2 + 3, DC // 2 + 2, DC // 2 + 3
        TPD_STRIP = TPD_OUT = DC // 2 + 2
        OPS_MIX = DC // 2 + DC // 2 + RC // 2 + DC // 2
        GATES_FROM = 8 * 3 + 8 + 8
        D_HBA, D_HBX, D_SP, D_NSP, D_QG, D_HG, D_NLAM, D_RED = 0, 22, 44, 66, 88, 89, 91, 93

        def der(at, m=1):
            return DER[:, at:at + m]

        QR = F[:, 0:1024].rearrange("p (a n) -> p a n", a=2)
        SQ2 = F[:, 1024:2048].rearrange("p (a n) -> p a n", a=2)
        V = F[:, 2048:2560].rearrange("p (a n) -> p a n", a=4)
        L = F[:, 2560:3328].rearrange("p (a n) -> p a n", a=2)
        SP = F[:, 3328:4096].rearrange("p (a n) -> p a n", a=2)
        T1 = F[:, 4096:4864].rearrange("p (a n) -> p a n", a=2)
        W = F[:, 4864:5632].rearrange("p (a n) -> p a n", a=2)
        KEEP = RT[:, 1024:1408]
        S4 = F[:, 2560:4096].rearrange("p (a n) -> p a n", a=4)
        PTS = W
        OA = F[:, 4096:4608]
        SG = F[:, 1024:1536]
        SQa = F[:, 1536:2048]
        HCW = 32 + T
        HC = MIX[:, 0:5, :].rearrange("p c t -> p (c t)")[:, 0:CONVC * HCW].rearrange("p (c t) -> p c t", t=HCW)
        CA = MIX[:, 6:10, :]
        SC = MIX[:, 10:14, :]
        SC_SQ = MIX[:, 0:CONVC, :]
        PN = MIX[:, 14:16, :].rearrange("p c t -> p (c t)")
        RR = F[:, 0:T]
        ACC = F[:, 512:1024]
        SQP = F[:, 1024:1536]
        MSQ = F[:, 1536:1536 + T]
        NW = F[:, 1792:1792 + T]
        BDS = AL[:, 0:8 * 1024].rearrange("p (s m n) -> p s m n", s=8, m=2)
        TA, TX, AA, TE = (AL[:, 8192 + 768 * q:8192 + 768 * q + 768].rearrange("p (c t) -> p c t", t=T)
                          for q in range(4))
        MIXf = MIX[:, :, :].rearrange("p c t -> p (c t)")
        OUTV = MIXf.rearrange("p (b d) -> p b d", b=NB)
        AB = RT[:, 0:HEADS2 * T].rearrange("p (h t) -> p h t", t=T)

        def wv(ap):
            return ap.rearrange("(c p) n -> p c n", p=P)

        w_in = wv(A["w_in"][0])
        w_rnn, w_att, w_o = wv(A["w_rnn_out"][0]), wv(A["w_attn_out"][0]), wv(A["w_o"][0])
        w_gu, w_dn = wv(A["w_ffn_gu"][0]), wv(A["w_ffn_down"][0])
        w_pg, w_pp = wv(A["w_ple_gate"][0]), wv(A["w_ple_proj"][0])
        QO = 2 * RNN
        KO, VO = QO + D, QO + 2 * D
        GR, GA = QO + 3 * D, QO + 4 * D

        def seq(w, K, col, X, width=2, base=0):
            return [Group(w, K, col + COLS * j, COLS * width, X, base) for j in range(width)]

        phases = []
        body = []
        for m in range(2):
            for off in (QO, KO, VO):
                body.append(Group(w_in, DC, off + COLS * m, 2 * COLS, XH))
        phases.append(Phase("attn", 4, body, each_unit(DC)))
        phases.append(Phase("gate_a0", 1, seq(w_in, DC, GA, XH, 4)))
        phases.append(Phase("gate_a1", 2, seq(w_in, DC, GA + 4 * COLS, XH)))
        phases.append(Phase("attn_out", 4, seq(w_att, DC, 0, YH), each_unit(DC)))
        phases.append(Phase("x_r", 5, seq(w_in, DC, 0, XH)))
        phases.append(Phase("x_r_last", 1, seq(w_in, DC, 10 * COLS, XH, 1)))
        phases.append(Phase("gate_r", 1, seq(w_in, DC, GR, XH, 8)))
        phases.append(Phase("g_r", 5, seq(w_in, DC, RNN, XH)))
        phases.append(Phase("g_r_last", 1, seq(w_in, DC, RNN + 10 * COLS, XH, 1)))
        phases.append(Phase("rnn_out", 4, seq(w_rnn, RC, 0, YH), each_unit(RC)))
        phases.append(Phase("tables", 0, []))
        phases.append(Phase("w_o", 4, seq(w_o, DC, 0, XH), each_unit(DC)))
        at = 0
        for h, K in enumerate(FF_PARTS):
            gu = []
            for m in range(2):
                gu.append(Group(w_gu, DC, P * at + COLS * m, 2 * COLS, YH))
                gu.append(Group(w_gu, DC, FF + P * at + COLS * m, 2 * COLS, YH))
            phases.append(Phase(f"gu{h}", K // 4, gu, each_unit(DC) if h == 0 else None))
            width = 2 if K // UK % 2 == 0 else 4
            phases.append(Phase(f"down{h}", 8 // width, seq(w_dn[:, at:at + K, :], K, 0, XH, width), each_unit(K)))
            at += K
        pl = []
        for m in range(4):
            pl.append(Group(w_pg, DC, COLS * m, 4 * COLS, YH))
            pl.append(Group(w_pp, 2, COLS * m, 4 * COLS, YH, base=DC))
        phases.append(Phase("ple", 2, pl, each_unit(DC)))
        for l in range(2):
            w2, wp, wo = wv(A["w_in_2"][l]), wv(A["conv_pw_2"][l]), wv(A["w_out_2"][l])
            A0, B0, C0 = 0, 2048, 6144
            cb = [C0, C0 + 512, C0 + COLS, C0 + 512 + COLS, C0 + 1024, C0 + 1024 + COLS]
            diff = [[Group(w2, DC, A0 + 512 * o + COLS * m, 0, XH) for o in range(4)] for m in range(2)]
            pw = seq(wp, CONVC, 0, YH, 2, base=DC)
            phases.append(Phase(f"conf{l}", 1, [Group(w2, DC, c, 0, XH) for c in cb], each_unit(DC)))
            phases.append(Phase(f"dil{l}", 4, [Group(w2, DC, B0 + 1024 * o, COLS, XH) for o in range(4)]))
            phases.append(Phase(f"diffa{l}", 1, diff[0]))
            q, k, v, g = diff[1]
            phases.append(Phase(f"diffb{l}", 1, [q, pw[0], k, pw[1], v, g], {1: [6]}))
            phases.append(Phase(f"tail{l}", 0, []))
            out = [Group(wo, DC, 0, 0, YH, turn=1), Group(wo, DC, COLS, 0, YH)]
            phases.append(Phase(f"outa{l}", 1, out, {0: [0, 0, 3, 1]}))
            phases.append(Phase(f"outb{l}", 3, seq(wo, DC, 2 * COLS, YH)))
            phases.append(Phase(f"ln{l}", 0, []))
        if STOP:
            names = [p.name for p in phases]
            phases = phases[:names.index(STOP) + 1]

        NAMES = ["raw0", "raw1", "raw2", "raw3",
                 "hi", "lo",
                 "unit",
                 "evac",
                 "op",
                 "x_in", "mats", "vecs", "lam", "keep", "p_in", "tab", "strip", "tb", "out",
                 "tp",
                 "tpd",
                 "sq",
                 "ss",
                 "act",
                 "dve",
                 "scores",
                 "later",
                 "rms",
                 "heads",
                 "scores2", "turned", "heads2",
                 "flip", "flipped",
                 "sum", "sumsq",
                 "final",
                 "chain",
                 "achain",
                 "ready",
                 "strip0", "strip1", "strip2", "strip3", "strip4", "strip5", "strip6", "strip7",
                 "conv",
                 "wiped",
                 "xc",
                 "bd",
                 "bdd",
                 ]
        Semaphores = namedtuple("Semaphores", NAMES)
        s = Semaphores(*(ctx.enter_context(nc.semaphore("s_" + name)) for name in NAMES))
        raw_sems = [s.raw0, s.raw1, s.raw2, s.raw3]
        strip_sems = [s.strip0, s.strip1, s.strip2, s.strip3, s.strip4, s.strip5, s.strip6, s.strip7]
        strips, users = gate_tiles()
        last_user = [max(j for j in range(RC) if i in users[j]) for i in range(RC)]
        block = ctx.enter_context(nc.Block())

        def pair(X, i):
            return X[:, 2 * i:2 * i + 2, :] if isinstance(i, int) else X[:, bass.ds(2 * i, 2), :]

        def hi2(X, i, base=0):
            if isinstance(i, int):
                return X[:, base + 2 * i:base + 2 * i + 2, 0:T]
            return X[:, bass.ds(2 * i + base, 2), 0:T]

        def lo2(X, i, base=0):
            if isinstance(i, int):
                return X[:, base + 2 * i:base + 2 * i + 2, T:2 * T]
            return X[:, bass.ds(2 * i + base, 2), T:2 * T]

        @block.sync
        def _(sp):
            c = Counts(sp, "sp", turns, real)

            def load(grp, i):
                col = grp.col + grp.step * i if grp.step else grp.col
                cols = slice(col, col + COLS) if isinstance(col, int) else bass.ds(col, COLS)
                for k, nk in grp.units():
                    u = c.n.get("unit", 0)
                    if u >= SLOTS:
                        sp.wait_ge(s.lo, c.value("unit", 1 - SLOTS))
                    sp.dma_start(RAW[:, u % SLOTS, 0:nk, :], grp.W[:, k:k + nk, cols])\
                        .then_inc(raw_sems[u % SLOTS], 16)
                    c.add("unit")

            for ph in phases:
                def turn(i):
                    for grp in ph.body:
                        load(grp, i)
                if ph.n:
                    turn(0)
                    c.loop(1, ph.n, turn)
            for g in range(DC // 2):
                sp.wait_ge(s.tpd, 8 + 1 + 1 + g + 1)
                sp.dma_start(A["out"][0].rearrange("(b p) d -> p b d", p=P)[:, :, COLS * g:COLS * g + COLS],
                             OUTV[:, :, COLS * g:COLS * g + COLS]).then_inc(s.out, 16)
            sp.wait_ge(s.out, 16 * (DC // 2))

        @block.gpsimd
        def _(pool):
            n = 0
            for i, (j0, pieces) in enumerate(strips):
                if i == 0:
                    pool.wait_ge(s.evac, GATES_FROM)
                if i >= 8:
                    pool.wait_ge(s.bd, last_user[i - 8] + 1)
                nc.gpsimd.memset(BDS[:, i % 8, :, :], 0.0).then_inc(s.wiped, 1)
                pool.wait_ge(s.wiped, i + 1)
                for n, r0, r1 in pieces:
                    at = RB * n - P * j0
                    for m, w in enumerate((A["w_rg_a"], A["w_rg_x"])):
                        pool.dma_start(BDS[r0 - P * i:r1 - P * i, i % 8, m, at:at + RB],
                                       w[0, n, r0 - RB * n:r1 - RB * n, :]).then_inc(strip_sems[i % 8], 16)

        strip_due = []
        _c = [0] * 8
        for i, (j0, pieces) in enumerate(strips):
            _c[i % 8] += 32 * len(pieces)
            strip_due.append(_c[i % 8])

        @block.scalar
        def _(act):
            c = Counts(act, "act", turns, real)

            def done(ins):
                ins.then_inc(s.achain, 1)
                act.wait_ge(s.achain, c.next("achain"))

            def split(grp):
                for k, nk in grp.units():
                    u = c.n.get("unit", 0)
                    act.wait_ge(raw_sems[u % SLOTS], c.value("unit", SLOTS, div=SLOTS, mul=16))
                    if u >= SLOTS:
                        act.wait_ge(s.unit, c.value("unit", 1 - SLOTS))
                    nc.scalar.activation(WH[:, u % SLOTS, 0:nk, :], RAW[:, u % SLOTS, 0:nk, :], ACT.Copy)\
                        .then_inc(s.hi, 1)
                    c.add("unit")

            def evacuated():
                act.wait_ge(s.evac, c.next("evac"))

            def from_dve():
                act.wait_ge(s.dve, c.next("dve"))

            def g(n=None):
                return Gf[:, (c.n["evac"] - 1) % 2, :]

            def a_q(i):
                evacuated()
                nc.scalar.activation(SQ2[:, 0, :], QR[:, 0, :], ACT.Square).then_inc(s.sq, 1)
                act.wait_ge(s.sq, c.next("sq"))

            def rms_inverse(m):
                act.wait_ge(s.rms, c.next("rms"))
                done(nc.scalar.activation(SQ2[:, m, :], PX[:, m, :], ACT.Ln, scale=1.0 / P, bias=EPS_AP))
                nc.scalar.activation(SQ2[:, m, :], SQ2[:, m, :], ACT.Exp, scale=-0.5).then_inc(s.act, 1)
                act.wait_ge(s.act, c.next("act"))

            def a_k(i):
                evacuated()
                nc.scalar.activation(SQ2[:, 1, :], QR[:, 1, :], ACT.Square).then_inc(s.sq, 1)
                act.wait_ge(s.sq, c.next("sq"))
                rms_inverse(0)

            def a_v(i):
                evacuated()
                rms_inverse(1)

            def a_soft():
                act.wait_ge(s.scores, c.next("scores"))
                done(nc.scalar.activation(L, PX[:, 0:2, 0:384], ACT.Abs))
                done(nc.scalar.activation(L, L, ACT.Exp, scale=-1.0))
                nc.scalar.activation(L, L, ACT.Ln, bias=1.0).then_inc(s.act, 1)
                act.wait_ge(s.act, c.next("act"))

            def a_w():
                from_dve()
                nc.scalar.activation(W, T1, ACT.Exp).then_inc(s.act, 1)
                act.wait_ge(s.act, c.next("act"))

            def a_o(i):
                act.wait_ge(s.heads, c.next("heads"))
                nc.scalar.activation(hi2(YH, i), PX[:, 3, :].rearrange("p (c t) -> p c t", t=T), ACT.Copy)\
                    .then_inc(s.act, 1)
                act.wait_ge(s.act, c.next("act"))

            def post_attn(i, j):
                m, what = divmod(j, 3)
                now = 2 * i + m
                before = not (isinstance(i, int) and now == 0)
                if what == 0:
                    a_q(now)
                    if before:
                        a_soft()
                elif what == 1:
                    a_k(now)
                    if before:
                        a_w()
                else:
                    a_v(now)
                    if before:
                        a_o(now - 1)

            def tanh_half(dst):
                evacuated()
                nc.scalar.activation(dst, g().rearrange("p (c t) -> p c t", t=T), ACT.Tanh, scale=0.5)\
                    .then_inc(s.act, 1)
                act.wait_ge(s.act, c.next("act"))

            def post_gate_a(i, j, at):
                if at == 0 and j == 0:
                    a_soft()
                if at == 0 and j == 1:
                    a_w()
                if at == 0 and j == 2:
                    a_o(7)
                tanh_half(pair(MIX, at + 2 * i + j))

            def post_plain(i, j):
                evacuated()

            def split_pair(X, i, src=None, base=0):
                from_dve()
                nc.scalar.activation(hi2(X, i, base), TT[:, 0, :, :] if src is None else src, ACT.Copy)\
                    .then_inc(s.act, 1)
                act.wait_ge(s.act, c.next("act"))

            def lru_step(j):
                chunks = list(range(3 * j, min(3 * j + 3, RC)))
                if j:
                    from_dve()
                for n in chunks:
                    e, b = n % 3, n % 4
                    act.wait_ge(s.bd, n + 1)
                    nc.scalar.activation(TA[:, e, :], PX[:, b, 0:T], ACT.Tanh, scale=0.5, bias=der(D_HBA + n))
                    nc.scalar.activation(TX[:, e, :], PX[:, b, T:2 * T], ACT.Tanh, scale=0.5, bias=der(D_HBX + n))\
                        .then_inc(s.bdd, 1)
                    act.wait_ge(s.bdd, c.next("bdd"))
                for n in chunks:
                    e = n % 3
                    nc.scalar.activation(AA[:, e, :], TA[:, e, :], ACT.Exp, scale=der(D_NSP + n),
                                         bias=der(D_NSP + n))
                    last = nc.scalar.activation(TE[:, e, :], TA[:, e, :], ACT.Tanh, scale=der(D_SP + n),
                                                bias=der(D_SP + n))
                last.then_inc(s.act, 1)
                act.wait_ge(s.act, c.next("act"))
                from_dve()
                m = len(chunks)
                nc.scalar.activation(TE[:, 0:m, :], TE[:, 0:m, :], ACT.Sqrt, scale=0.25).then_inc(s.act, 1)
                act.wait_ge(s.act, c.next("act"))

            def post_gate_r(i, j):
                tanh_half(pair(RTc, j))
                lru_step(j)

            def post_g_r(i, j, at=0):
                evacuated()
                nc.scalar.activation(Tf[:, 0, :], g(), ACT.Square, scale=float(np.sqrt(GELU_C))).then_inc(s.act, 1)
                act.wait_ge(s.act, c.next("act"))
                from_dve()
                nc.scalar.activation(Tf[:, 1, :], Tf[:, 0, :], ACT.Tanh, scale=GELU_S).then_inc(s.act, 1)
                act.wait_ge(s.act, c.next("act"))
                split_pair(YH, at + 2 * i + j)

            def post_rnn_out(i, j):
                evacuated()
                from_dve()
                nc.scalar.activation(hi2(XH, 2 * i + j), pair(MIX, 2 * i + j), ACT.Copy).then_inc(s.act, 1)
                act.wait_ge(s.act, c.next("act"))

            def post_fold(n):
                evacuated()
                from_dve()
                nc.scalar.activation(two(SQP), pair(XRES, n), ACT.Square).then_inc(s.act, 1)
                act.wait_ge(s.act, c.next("act"))
                split_pair(YH, n)

            def two(ap):
                return ap.rearrange("p (c t) -> p c t", t=T)

            def inverse_rms(ms, r, ss, width, eps):
                done(nc.scalar.activation(ms, ss, ACT.Identity, scale=1.0 / width, bias=eps))
                done(nc.scalar.activation(r, ms, ACT.Ln))
                nc.scalar.activation(r, r, ACT.Exp, scale=-0.5).then_inc(s.act, 1)
                act.wait_ge(s.act, c.next("act"))

            def norm():
                act.wait_ge(s.ss, c.next("ss"))
                inverse_rms(Gf[:, 0, 0:T], Gf[:, 0, T:2 * T], PX[:, 0, 0:T], D, EPS)
                for q in range(DC // 2):
                    from_dve()
                    nc.scalar.activation(hi2(XH, q), TT[:, q % 2, :, :], ACT.Copy).then_inc(s.act, 1)
                    act.wait_ge(s.act, c.next("act"))

            def fold():
                act.wait_ge(s.ss, c.next("ss"))
                inverse_rms(MSQ, RR, PX[:, 0, 0:T], D, EPS)

            def tables():
                act.wait_ge(s.op, OPS_MIX)
                act.dma_start(MIXf[0:NBUCK, 3072:3072 + HEADS2], A["rel_bias_2"]).then_inc(s.tab, 16)
                act.dma_start(MIXf[0:NBUCK, 3100:3484], A["c_onehot"]).then_inc(s.tab, 16)
                act.dma_start(MIXf[0:HEADS2, 3500:3884], A["c_add"]).then_inc(s.tab, 16)
                act.dma_start(RT[:, 3072:3584].rearrange("p (b d) -> p b d", b=NB),
                              A["p"][0, 0].rearrange("(b p) d -> p b d", p=P)).then_inc(s.p_in, 16)

            def p_high():
                act.wait_ge(s.tp, TP_P)
                nc.scalar.activation(hi2(YH, 0, base=DC), two(PX[:, 1, :]), ACT.Copy).then_inc(s.act, 1)
                act.wait_ge(s.act, c.next("act"))

            def strip_around():
                act.wait_ge(s.tpd, TPD_STRIP)
                act.dma_start(strip_dram, MIXf[0:HEADS2, 3500:3884]).then_inc(s.strip, 16)
                act.wait_ge(s.strip, 16)
                for h in range(HEADS2):
                    rows = strip_dram[h, :]
                    toeplitz = bass.AP(tensor=rows.tensor, offset=rows.offset, ap=[[1, P], [1, T]])
                    act.dma_start(MIXf[:, T * h:T * h + T], toeplitz).then_inc(s.tb, 16)

            def post_gu(i, j, h):
                evacuated()
                first = h == 0 and isinstance(i, int) and i == 0
                if first and j == 0:
                    fold()
                    p_high()
                if j % 2 == 0:
                    from_dve()
                    nc.scalar.activation(Tf[:, 0, :], g(), ACT.Tanh, scale=0.5).then_inc(s.act, 1)
                    act.wait_ge(s.act, c.next("act"))
                else:
                    split_pair(XH, 2 * i + j // 2, TT[:, 1, :, :])
                if first and j == 1:
                    strip_around()

            def post_ple(i, j):
                evacuated()
                if j % 2 == 0:
                    if isinstance(i, int) and i == 0 and j == 0:
                        fold()
                    from_dve()
                    nc.scalar.activation(Tf[:, 0, :], g(), ACT.Tanh, scale=0.5).then_inc(s.act, 1)
                    act.wait_ge(s.act, c.next("act"))
                else:
                    n = 4 * i + j // 2
                    from_dve()
                    nc.scalar.activation(hi2(XH, n), pair(XRES, n), ACT.Copy).then_inc(s.act, 1)
                    act.wait_ge(s.act, c.next("act"))

            def post_conf(i, j):
                evacuated()
                if j in (1, 3):
                    nc.scalar.activation(Tf[:, 0, :], g(), ACT.Tanh, scale=0.5).then_inc(s.act, 1)
                    act.wait_ge(s.act, c.next("act"))
                if j in (4, 5):
                    nc.scalar.activation(Tf[:, 0, :], g(), ACT.Tanh, scale=0.5).then_inc(s.act, 1)
                    act.wait_ge(s.act, c.next("act"))

            def soft(n):
                for x in range(n):
                    from_dve()
                    for b, (lo, up) in enumerate(((0, P), (P, 3 * P))):
                        last = nc.scalar.activation(S4[:, x, lo:up], S4[:, x, lo:up], ACT.Exp,
                                                    bias=der(D_RED + 2 * x + b),
                                                    accum_out=der(D_RED + 8 + 2 * x + b))
                        last.then_inc(s.act, 1)
                        act.wait_ge(s.act, c.next("act"))

            def silu_gate():
                evacuated()
                nc.scalar.activation(Tf[:, 0, :], g(), ACT.Tanh, scale=0.5).then_inc(s.act, 1)
                act.wait_ge(s.act, c.next("act"))

            def diff_squares():
                from_dve()
                nc.scalar.activation(SQa, OA, ACT.Square).then_inc(s.sq, 1)
                act.wait_ge(s.sq, c.next("sq"))

            def diff_out(m):
                act.wait_ge(s.rms, c.next("rms"))
                done(nc.scalar.activation(Tf[:, 1, :], PX[:, 3, :], ACT.Ln, scale=1.0 / P, bias=EPS2_AP))
                nc.scalar.activation(Tf[:, 1, :], Tf[:, 1, :], ACT.Exp, scale=-0.5).then_inc(s.act, 1)
                act.wait_ge(s.act, c.next("act"))
                from_dve()
                nc.scalar.activation(hi2(YH, m), two(OA), ACT.Copy).then_inc(s.act, 1)
                act.wait_ge(s.act, c.next("act"))

            def dil_out(i):
                from_dve()
                nc.scalar.activation(hi2(YH, i, base=4), two(OA), ACT.Copy).then_inc(s.act, 1)
                act.wait_ge(s.act, c.next("act"))

            def post_diffa(i, j):
                if j == 0:
                    evacuated()
                    dil_out(3)
                    from_dve()
                    nc.scalar.activation(SC_SQ, CA, ACT.Square).then_inc(s.sq, 1)
                    act.wait_ge(s.sq, c.next("sq"))
                elif j == 1:
                    evacuated()
                    act.wait_ge(s.sumsq, c.next("sumsq"))
                    inverse_rms(PN[:, 0:T], PN[:, T:2 * T], PX[:, 1, 0:T], 512, EPS2)
                elif j == 2:
                    evacuated()
                    soft(4)
                else:
                    silu_gate()
                    from_dve()
                    nc.scalar.activation(SC_SQ, CA, ACT.Tanh, scale=0.5).then_inc(s.act, 1)
                    act.wait_ge(s.act, c.next("act"))
                    from_dve()
                    for q in range(2):
                        nc.scalar.activation(hi2(YH, q, base=DC), CA[:, 2 * q:2 * q + 2, :], ACT.Copy)\
                            .then_inc(s.act, 1)
                        act.wait_ge(s.act, c.next("act"))

            def post_diffb(i, j):
                if j == 0:
                    evacuated()
                    diff_squares()
                elif j == 1:
                    evacuated()
                    split_pair(YH, 0, base=12)
                elif j == 2:
                    evacuated()
                    diff_out(0)
                elif j == 3:
                    evacuated()
                    split_pair(YH, 1, base=12)
                elif j == 4:
                    evacuated()
                    soft(4)
                else:
                    silu_gate()

            def tail():
                diff_squares()
                diff_out(1)

            def post_dil(i, j):
                before = not (isinstance(i, int) and i == 0)
                if j < 3:
                    evacuated()
                if j == 0 and before:
                    dil_out(i - 1)
                elif j == 2:
                    soft(2)
                elif j == 3:
                    silu_gate()

            def ln(l):
                for q in range(8):
                    from_dve()
                    nc.scalar.activation(pair(XC, q), pair(XRES, q), ACT.Square).then_inc(s.sq, 1)
                    act.wait_ge(s.sq, c.next("sq"))
                act.wait_ge(s.sumsq, c.next("sumsq"))
                inverse_rms(Gf[:, 0, 0:T], Gf[:, 0, T:2 * T], PX[:, 1, 0:T], D, EPS2)
                for q in range(8):
                    from_dve()
                    for e in range(2):
                        ch = 2 * q + e
                        last = nc.scalar.activation(XRES[:, ch, :], TT[:, q % 2, e, :], ACT.Identity,
                                                    bias=vec("ln_b_2", 16 * l + ch))
                    if l == 0:
                        done(last)
                        nc.scalar.activation(hi2(XH, q), pair(XRES, q), ACT.Copy).then_inc(s.act, 1)
                        act.wait_ge(s.act, c.next("act"))
                    else:
                        last.then_inc(s.final, 1)
                        act.wait_ge(s.final, c.next("final"))

            act.dma_start(MATS[:, :], A["c_mats"]).then_inc(s.mats, 16)
            act.dma_start(F[:, 0:NB * D].rearrange("p (b d) -> p b d", b=NB),
                          A["x"][0].rearrange("(b p) d -> p b d", p=P)).then_inc(s.x_in, 16)
            row = 0
            for name, rows in VEC_ROWS:
                src = A[name].rearrange("a k (c p) -> (a k c) p", p=P) if len(A[name].shape) == 3 else \
                    A[name].rearrange("a (c p) -> (a c) p", p=P)
                at = 0
                while at < rows:
                    r = (row + at) % P
                    m = min(rows - at, P - r)
                    t = (row + at) // P
                    act.dma_start(RT[r:r + m, P * t:P * t + P], src[at:at + m, :]).then_inc(s.vecs, 16)
                    at += m
                row += rows
            act.dma_start(KEEP, A["c_keep"]).then_inc(s.keep, 16)
            act.dma_start(Fv[:, NB * D:NB * D + 512],
                          A["diff_lambda_2"].rearrange("l a d -> (l a d)").partition_broadcast(P)).then_inc(s.lam, 16)

            for q in range(DC // 2):
                act.wait_ge(s.tpd, q + 1)
                nc.scalar.activation(pair(MIX, q), pair(XRES, q), ACT.Square).then_inc(s.sq, 1)
                act.wait_ge(s.sq, c.next("sq"))
            act.wait_ge(s.tpd, DC // 2 + 1)
            for half, src in ((D_HBA, "b_rg_a"), (D_HBX, "b_rg_x")):
                nc.scalar.activation(der(half, RC), vec(src, 0, RC), ACT.Copy, scale=0.5)
            nc.scalar.activation(der(D_QG), vec("q_gain"), ACT.Copy, scale=QSCALE)
            for l in range(2):
                nc.scalar.activation(der(D_HG + l), vec("diff_head_gain_2", l), ACT.Copy, scale=1.0 - LAM_INIT[l])
            done(nc.scalar.activation(der(D_SP, RC), vec("lru_lambda", 0, RC), ACT.Abs))
            done(nc.scalar.activation(der(D_SP, RC), der(D_SP, RC), ACT.Exp, scale=-1.0))
            nc.scalar.activation(der(D_SP, RC), der(D_SP, RC), ACT.Ln, bias=1.0).then_inc(s.act, 1)
            act.wait_ge(s.act, c.next("act"))
            from_dve()
            nc.scalar.activation(der(D_RED, 4), der(D_RED, 4), ACT.Exp).then_inc(s.act, 1)
            act.wait_ge(s.act, c.next("act"))

            def post(name):
                return {
                    "attn": post_attn,
                    "gate_a0": lambda i, j: post_gate_a(i, j, 0),
                    "gate_a1": lambda i, j: post_gate_a(i, j, 4),
                    "attn_out": post_plain, "x_r": post_plain, "x_r_last": post_plain,
                    "gate_r": post_gate_r, "g_r": post_g_r,
                    "g_r_last": lambda i, j: post_g_r(i, j, 10),
                    "rnn_out": post_rnn_out, "w_o": lambda i, j: post_fold(2 * i + j),
                    "gu0": lambda i, j: post_gu(i, j, 0), "gu1": lambda i, j: post_gu(i, j, 1),
                    "gu2": lambda i, j: post_gu(i, j, 2),
                    "down0": post_plain, "down1": post_plain, "down2": lambda i, j: post_fold(4 * i + j), "ple": post_ple,
                    "conf": post_conf, "dil": post_dil, "diffa": post_diffa, "diffb": post_diffb,
                    "outa": post_plain, "outb": post_plain,
                }.get(name) or post(name[:-1])

            between = {"tables": tables, "tail0": tail, "tail1": tail,
                       "ln0": lambda: ln(0), "ln1": lambda: ln(1)}
            pending = [norm]
            for ph in phases:
                if ph.name in between:
                    pending.append(between[ph.name])
                    continue
                fn, J = post(ph.name), len(ph.body)
                for j, grp in enumerate(ph.body):
                    split(grp)
                    for job in pending:
                        job()
                    pending = [lambda fn=fn, j=j: fn(0, j)]

                def turn(i):
                    for j, grp in enumerate(ph.body):
                        split(grp)
                        fn(i - 1, J - 1) if j == 0 else fn(i, j - 1)
                c.loop(1, ph.n, turn)
                pending = [lambda fn=fn, n=ph.n, J=J: fn(n - 1, J - 1)]
            for job in pending:
                job()

        @block.vector
        def _(dve):
            c = Counts(dve, "dve", turns, real)
            V_ = nc.vector

            def done(ins):
                ins.then_inc(s.chain, 1)
                dve.wait_ge(s.chain, c.next("chain"))

            def split(grp):
                for k, nk in grp.units():
                    u = c.n.get("unit", 0)
                    dve.wait_ge(s.hi, c.value("unit", 1))
                    V_.tensor_tensor(WL[:, u % SLOTS, 0:nk, :], RAW[:, u % SLOTS, 0:nk, :],
                                     WH[:, u % SLOTS, 0:nk, :].bitcast(fp), ALU.subtract).then_inc(s.lo, 1)
                    c.add("unit")

            def from_act(m=1):
                dve.wait_ge(s.act, c.next("act", m))

            def evacuate(grp, dst=None):
                par = c.n.get("group", 0) % 2
                dve.wait_ge(s.unit, c.next("seen", len(grp.units())))
                out = G[:, par, :, :] if dst is None else dst
                V_.reduce_sum(out, PG[:, 2 * par:2 * par + 2, :].rearrange("p b (h t) -> p b t h", h=2), AX)\
                    .then_inc(s.evac, 1)
                c.add("group")
                dve.wait_ge(s.evac, c.value("group"))
                return Gf[:, par, :]

            def two(ap):
                return ap.rearrange("p (c t) -> p c t", t=T)

            def low(X, i, src, base=0):
                from_act()
                V_.tensor_tensor(lo2(X, i, base), src, hi2(X, i, base).bitcast(fp), ALU.subtract).then_inc(s.op, 1)
                dve.wait_ge(s.op, c.next("op"))

            def newton(ms, r, tmp, tell=None):
                done(V_.scalar_tensor_tensor(tmp, ms, -0.5, r, ALU.mult, ALU.mult))
                done(V_.tensor_tensor(tmp, tmp, r, ALU.mult))
                done(V_.scalar_tensor_tensor(r, tmp, 1.5, r, ALU.add, ALU.mult))

            def a_q(grp, i):
                evacuate(grp, two(QR[:, 0, :]))

            def a_k(grp, i):
                evacuate(grp, two(QR[:, 1, :]))
                from_act()
                done(V_.scalar_tensor_tensor(QR[:, 0, :], QR[:, 0, :], der(D_QG), SQ2[:, 0, :], ALU.mult, ALU.mult))

            def a_v(grp, i):
                evacuate(grp)
                from_act()
                V_.scalar_tensor_tensor(QR[:, 1, :], QR[:, 1, :], vec("k_gain"), SQ2[:, 1, :], ALU.mult, ALU.mult)\
                    .then_inc(s.ready, 1)
                dve.wait_ge(s.ready, c.next("ready"))

            def a_soft():
                V_.tensor_copy(V, PX[:, 2, :].rearrange("p (a n) -> p a n", a=4))
                from_act()
                z = PX[:, 0:2, 0:384]
                done(V_.scalar_tensor_tensor(SP, z, 0.0, L, ALU.max, ALU.add))
                V_.tensor_tensor(T1, z, SP, ALU.subtract)
                V_.tensor_tensor(SP, SP, KEEP.unsqueeze(1).broadcast_to([P, 2, 384]), ALU.mult).then_inc(s.ready, 1)
                dve.wait_ge(s.ready, c.next("ready"))

            def a_w():
                dve.wait_ge(s.later, c.next("later"))
                V_.tensor_tensor(T1, T1, PX[:, 2:4, 0:384], ALU.subtract).then_inc(s.dve, 1)
                dve.wait_ge(s.dve, c.next("dve"))
                from_act()
                V_.tensor_tensor(W, W, KEEP.unsqueeze(1).broadcast_to([P, 2, 384]), ALU.mult).then_inc(s.ready, 1)
                dve.wait_ge(s.ready, c.next("ready"))

            def a_o(i):
                dve.wait_ge(s.heads, c.next("heads"))
                low(YH, i, two(PX[:, 3, :]))

            def post_attn(grp, i, j):
                m, what = divmod(j, 3)
                now = 2 * i + m
                before = not (isinstance(i, int) and now == 0)
                if what == 0:
                    if before:
                        dve.wait_ge(s.scores, c.next("scores"))
                    a_q(grp, now)
                    if before:
                        a_soft()
                elif what == 1:
                    a_k(grp, now)
                    if before:
                        a_w()
                else:
                    a_v(grp, now)
                    if before:
                        a_o(now - 1)

            def post_gate_a(grp, i, j, at):
                if at == 0 and j == 0:
                    dve.wait_ge(s.scores, c.next("scores"))
                    evacuate(grp)
                    a_soft()
                elif at == 0 and j == 1:
                    evacuate(grp)
                    a_w()
                elif at == 0 and j == 2:
                    evacuate(grp)
                    a_o(7)
                else:
                    evacuate(grp)
                from_act()

            def post_attn_out(grp, i, j):
                x = evacuate(grp)
                m = pair(MIX, 2 * i + j)
                V_.scalar_tensor_tensor(m, m, 1.0, two(x), ALU.add, ALU.mult)

            def post_x_r(grp, i, j, at=0):
                x = evacuate(grp)
                for e in range(2):
                    ch = 4 * i + 2 * j + e + at
                    src = x[:, e * T:e * T + T]
                    dst = XC[:, ch, :] if isinstance(ch, int) else XC[:, bass.ds(ch, 1), :].squeeze(1)
                    done(V_.tensor_scalar(dst, src, vec("conv_w", 3 * RC + ch), vec("conv_b", ch),
                                          ALU.mult, ALU.add))
                    for k in (2, 1, 0):
                        d = TAPS - 1 - k
                        part = dst[:, d:T]
                        ins = V_.scalar_tensor_tensor(part, src[:, 0:T - d], vec("conv_w", k * RC + ch), part,
                                                      ALU.mult, ALU.add)
                        if k:
                            done(ins)
                        else:
                            ins.then_inc(s.xc, 1)
                            dve.wait_ge(s.xc, c.next("xc"))

            def lru_step(j):
                first, m = 3 * j, min(3, RC - 3 * j)
                dve.wait_ge(s.bd, first + m)
                if j:
                    V_.tensor_copy(XC[:, first - 3:first, :], TE).then_inc(s.dve, 1)
                    dve.wait_ge(s.dve, c.next("dve"))
                a, t, x, e = AA[:, 0:m, :], TA[:, 0:m, :], TX[:, 0:m, :], TE[:, 0:m, :]
                from_act()
                done(V_.tensor_tensor(t, a, a, ALU.mult))
                V_.scalar_tensor_tensor(e, t, 1.0, e, ALU.add, ALU.mult).then_inc(s.dve, 1)
                dve.wait_ge(s.dve, c.next("dve"))
                done(V_.scalar_tensor_tensor(x, x, 1.0, XC[:, first:first + m, :], ALU.add, ALU.mult))
                from_act()
                done(V_.tensor_tensor(x, x, e, ALU.mult))
                for q in range(m):
                    ins = V_.tensor_tensor_scan(TE[:, q, :], AA[:, q, :], TX[:, q, :], 0.0, ALU.mult, ALU.add)
                done(ins)
                if first + m == RC:
                    done(V_.tensor_copy(XC[:, first:RC, :], e))

            def post_gate_r(grp, i, j):
                evacuate(grp)
                from_act()
                lru_step(j)

            def post_g_r(grp, i, j, at=0):
                x = evacuate(grp)
                n = at + 2 * i + j
                from_act()
                V_.scalar_tensor_tensor(Tf[:, 0, :], Tf[:, 0, :], 1.0, x, ALU.add, ALU.mult).then_inc(s.dve, 1)
                dve.wait_ge(s.dve, c.next("dve"))
                from_act()
                done(V_.scalar_tensor_tensor(Tf[:, 1, :], Tf[:, 1, :], 1.0, x, ALU.add, ALU.mult))
                V_.tensor_tensor(TT[:, 0, :, :], TT[:, 1, :, :], pair(XC, n), ALU.mult).then_inc(s.dve, 1)
                dve.wait_ge(s.dve, c.next("dve"))
                low(YH, n, TT[:, 0, :, :])

            def post_rnn_out(grp, i, j):
                x = evacuate(grp)
                n = 2 * i + j
                r, m = pair(RTc, n), pair(MIX, n)
                done(V_.scalar_tensor_tensor(r, r, 1.0, two(x), ALU.add, ALU.mult))
                V_.scalar_tensor_tensor(m, r, 0.5, m, ALU.mult, ALU.add).then_inc(s.dve, 1)
                dve.wait_ge(s.dve, c.next("dve"))
                low(XH, n, m)

            def accumulate(n, src):
                if isinstance(n, int) and n == 0:
                    done(V_.tensor_copy(two(ACC), src))
                elif isinstance(n, int) and n == DC // 2 - 1:
                    V_.tensor_tensor(two(ACC), two(ACC), src, ALU.add).then_inc(s.ready, 1)
                    dve.wait_ge(s.ready, c.next("ready"))
                else:
                    done(V_.tensor_tensor(two(ACC), two(ACC), src, ALU.add))

            def residual(grp, i, j):
                x = evacuate(grp)
                m = pair(XRES, 2 * i + j)
                V_.tensor_tensor(m, two(x), m, ALU.add)

            def post_fold(grp, n, scale, gain):
                x = evacuate(grp)
                m = pair(XRES, n)
                V_.scalar_tensor_tensor(m, two(x), scale, m, ALU.mult, ALU.add).then_inc(s.dve, 1)
                dve.wait_ge(s.dve, c.next("dve"))
                V_.tensor_tensor(TT[:, 0, :, :], m, vec(gain, 2 * n, 2).unsqueeze(2).broadcast_to([P, 2, T]),
                                 ALU.mult).then_inc(s.dve, 1)
                dve.wait_ge(s.dve, c.next("dve"))
                from_act()
                accumulate(n, two(SQP))
                low(YH, n, TT[:, 0, :, :])

            def fold():
                from_act()
                newton(MSQ, RR, NW)

            def over_rms(x):
                V_.tensor_tensor(two(x), two(x), RR.unsqueeze(1).broadcast_to([P, 2, T]), ALU.mult).then_inc(s.dve, 1)
                dve.wait_ge(s.dve, c.next("dve"))

            def norm(gain):
                from_act()
                newton(Gf[:, 0, 0:T], Gf[:, 0, T:2 * T], Gf[:, 1, 0:T])
                for q in range(DC // 2):
                    for e in range(2):
                        ins = V_.scalar_tensor_tensor(TT[:, q % 2, e, :], XRES[:, 2 * q + e, :],
                                                      vec(gain, 2 * q + e), Gf[:, 0, T:2 * T], ALU.mult, ALU.mult)
                    ins.then_inc(s.dve, 1)
                    dve.wait_ge(s.dve, c.next("dve"))
                    if q:
                        low(XH, q - 1, TT[:, (q - 1) % 2, :, :])
                low(XH, DC // 2 - 1, TT[:, (DC // 2 - 1) % 2, :, :])

            def bias_strip():
                dve.wait_ge(s.tab, 48)
                dve.wait_ge(s.tp, TP_STRIP)
                V_.tensor_tensor(MIXf[0:HEADS2, 3500:3884], PX[0:HEADS2, 2, 0:384], MIXf[0:HEADS2, 3500:3884],
                                 ALU.add).then_inc(s.tpd, 1)
                dve.wait_ge(s.tpd, c.next("tpd"))

            def bias_tiles(j):
                for h in (2 * j, 2 * j + 1):
                    dve.wait_ge(s.flip, h + 1)
                    V_.tensor_copy(AB[:, 2 * h:2 * h + 2, :], two(PX[:, 2 + h % 2, :])).then_inc(s.flipped, 1)
                    dve.wait_ge(s.flipped, c.next("flipped"))

            def post_gu(grp, i, j, h):
                x = evacuate(grp)
                first = isinstance(i, int) and i == 0
                if h == 0 and first and j == 0:
                    fold()
                    dve.wait_ge(s.tp, TP_P)
                    low(YH, 0, two(PX[:, 1, :]), base=DC)
                if j % 2 == 0:
                    over_rms(x)
                    from_act()
                    done(V_.scalar_tensor_tensor(Tf[:, 1, :], Tf[:, 0, :], 1.0, x, ALU.add, ALU.mult))
                else:
                    done(V_.scalar_tensor_tensor(Tf[:, 1, :], Tf[:, 1, :], 0.5, x, ALU.mult, ALU.mult))
                    over_rms(Tf[:, 1, :])
                    low(XH, 2 * i + j // 2, TT[:, 1, :, :])
                if h == 0 and first and j == 1:
                    bias_strip()
                if h == 1 and first and j < 3:
                    bias_tiles(j)

            def post_ple(grp, i, j):
                x = evacuate(grp)
                if j % 2 == 0:
                    if isinstance(i, int) and i == 0 and j == 0:
                        fold()
                    over_rms(x)
                    from_act()
                else:
                    n = 4 * i + j // 2
                    done(V_.scalar_tensor_tensor(Tf[:, 1, :], Tf[:, 0, :], 1.0, x, ALU.add, ALU.mult))
                    m = pair(XRES, n)
                    V_.scalar_tensor_tensor(m, TT[:, 1, :, :], 0.5, m, ALU.mult, ALU.add).then_inc(s.dve, 1)
                    dve.wait_ge(s.dve, c.next("dve"))
                    low(XH, n, m)

            def post_conf(grp, i, j, l):
                h = 2 * (j // 2)
                if j == 0:
                    done(V_.memset(HC[:, :, 0:32], 0.0))
                if j in (0, 2):
                    evacuate(grp, HC[:, h:h + 2, 32:32 + T])
                elif j in (1, 3):
                    evacuate(grp)
                    from_act()
                    done(V_.tensor_scalar(Tf[:, 1, :], Tf[:, 0, :], 0.5, 0.5, ALU.mult, ALU.add))
                    x = HC[:, h:h + 2, 32:32 + T]
                    done(V_.tensor_tensor(x, x, TT[:, 1, :, :], ALU.mult))
                else:
                    x = evacuate(grp)
                    from_act()
                    V_.scalar_tensor_tensor(SC[:, 2 * (j - 4):2 * (j - 4) + 2, :], TT[:, 0, :, :], 1.0, two(x),
                                            ALU.add, ALU.mult)
                if j == 5:
                    taps(0, 3, l)

            def taps(k, m, l):
                for t in range(m):
                    tap = k + t
                    for ch in range(CONVC):
                        row = (l * TAPS2) * CONVC + ch
                        at = tap * CONVC + row
                        off = tap + 2
                        src = HC[:, ch, off:off + T] if isinstance(tap, int) else \
                            HC[:, ch, bass.ds(off, T)]
                        if isinstance(tap, int) and tap == 0:
                            ins = V_.tensor_scalar(CA[:, ch, :], src, vec("conv_dw_2", at),
                                                   vec("conv_b_2", CONVC * l + ch), ALU.mult, ALU.add)
                        else:
                            ins = V_.scalar_tensor_tensor(CA[:, ch, :], src, vec("conv_dw_2", at), CA[:, ch, :],
                                                          ALU.mult, ALU.add)
                    if isinstance(tap, int) and tap == TAPS2 - 1:
                        ins.then_inc(s.conv, 1)
                        dve.wait_ge(s.conv, c.next("conv"))
                    else:
                        done(ins)

            def scores(n, scale, head):
                for x in range(n):
                    h = head(x)
                    ab = AB[:, h, :] if isinstance(h, int) else AB[:, bass.ds(h, 1), :].squeeze(1)
                    V_.scalar_tensor_tensor(S4[:, x, 0:P], PX[:, x, 0:P], scale, ab[:, P:2 * P], ALU.mult, ALU.add)
                    done(V_.scalar_tensor_tensor(S4[:, x, P:3 * P], PX[:, x, P:3 * P], scale, ab, ALU.mult, ALU.add))
                    V_.tensor_reduce(der(D_RED + 2 * x), S4[:, x, 0:P], AX, ALU.max, negate=True)
                    V_.tensor_reduce(der(D_RED + 2 * x + 1), S4[:, x, P:3 * P], AX, ALU.max, negate=True)\
                        .then_inc(s.dve, 1)
                    dve.wait_ge(s.dve, c.next("dve"))

            def inverse_sums(n):
                from_act(2 * n)
                done(V_.reciprocal(der(D_RED + 16, 2 * n), der(D_RED + 8, 2 * n)))

            def transposed():
                dve.wait_ge(s.turned, c.next("turned"))
                V_.tensor_copy(V, PX[:, 2, :].rearrange("p (a n) -> p a n", a=4))
                V_.tensor_copy(PTS, PX[:, 0:2, 0:384]).then_inc(s.ready, 1)
                dve.wait_ge(s.ready, c.next("ready"))

            def gate(grp, tell=False):
                x = evacuate(grp)
                from_act()
                ins = V_.scalar_tensor_tensor(SG, Tf[:, 0, :], 1.0, x, ALU.add, ALU.mult)
                if tell:
                    ins.then_inc(s.dve, 1)
                    dve.wait_ge(s.dve, c.next("dve"))
                transposed()

            def gated():
                dve.wait_ge(s.heads2, c.next("heads2"))
                V_.scalar_tensor_tensor(OA, PX[:, 3, :], 0.5, SG, ALU.mult, ALU.mult).then_inc(s.dve, 1)
                dve.wait_ge(s.dve, c.next("dve"))

            def diff_gated():
                dve.wait_ge(s.heads2, c.next("heads2"))
                V_.tensor_copy(OA, PX[:, 3, :]).then_inc(s.dve, 1)
                dve.wait_ge(s.dve, c.next("dve"))

            def diff_out(m, l):
                from_act()
                done(V_.scalar_tensor_tensor(OA, OA, der(D_HG + l), Tf[:, 1, :], ALU.mult, ALU.mult))
                V_.scalar_tensor_tensor(OA, OA, 0.5, SG, ALU.mult, ALU.mult).then_inc(s.dve, 1)
                dve.wait_ge(s.dve, c.next("dve"))
                low(YH, m, two(OA))

            def diff_softmax(m, l):
                dve.wait_ge(s.scores2, c.next("scores2"))
                scores(4, ASCALE, lambda x: 2 * m + x // 2)
                inverse_sums(4)
                for h in range(2):
                    done(V_.tensor_scalar(der(D_RED + 16 + 4 * h + 2, 2), der(D_RED + 16 + 4 * h + 2, 2),
                                          der(D_NLAM + l), None, ALU.mult))
                    for b, (lo, up) in enumerate(((0, P), (P, 3 * P))):
                        x = S4[:, 2 * h, lo:up]
                        done(V_.tensor_scalar(x, x, der(D_RED + 16 + 4 * h + b), None, ALU.mult))
                        ins = V_.scalar_tensor_tensor(x, S4[:, 2 * h + 1, lo:up],
                                                      der(D_RED + 16 + 4 * h + 2 + b), x, ALU.mult, ALU.add)
                ins.then_inc(s.ready, 1)
                dve.wait_ge(s.ready, c.next("ready"))

            def post_dil(grp, i, j, l):
                if j == 0:
                    evacuate(grp, two(QR[:, 0, :]))
                    if not (isinstance(i, int) and i == 0):
                        gated()
                        low(YH, i - 1, two(OA), base=4)
                elif j == 1:
                    evacuate(grp, two(QR[:, 1, :]))
                elif j == 2:
                    evacuate(grp)
                    dve.wait_ge(s.scores2, c.next("scores2"))
                    scores(2, QSCALE, lambda x: 2 * i + (4 + x))
                    inverse_sums(2)
                    for h in range(2):
                        for b, (lo, up) in enumerate(((0, P), (P, 3 * P))):
                            x = S4[:, h, lo:up]
                            ins = V_.tensor_scalar(x, x, der(D_RED + 16 + 2 * h + b), None, ALU.mult)
                    ins.then_inc(s.ready, 1)
                    dve.wait_ge(s.ready, c.next("ready"))
                else:
                    gate(grp)
                at, m = ((0, 2), (2, 2), (4, 2), (6, 1))[j]
                taps(7 * i + (3 + at), m, l)

            def post_diffa(grp, i, j, l):
                if j == 0:
                    evacuate(grp, two(QR[:, 0, :]))
                    gated()
                    low(YH, 3, two(OA), base=4)
                    dve.wait_ge(s.sum, c.next("sum"))
                    done(V_.tensor_scalar(PN[:, T:2 * T], PX[:, 0, 0:T], -1.0 / 512, None, ALU.mult))
                    V_.tensor_tensor(CA, CA, PN[:, T:2 * T].unsqueeze(1).broadcast_to([P, CONVC, T]), ALU.add)\
                        .then_inc(s.dve, 1)
                    dve.wait_ge(s.dve, c.next("dve"))
                elif j == 1:
                    evacuate(grp, two(QR[:, 1, :]))
                    from_act()
                    V_.scalar_tensor_tensor(NW, PN[:, 0:T], -0.5, PN[:, T:2 * T], ALU.mult, ALU.mult)\
                        .then_inc(s.ready, 1)
                    dve.wait_ge(s.ready, c.next("ready"))
                    done(V_.tensor_tensor(NW, NW, PN[:, T:2 * T], ALU.mult))
                    done(V_.scalar_tensor_tensor(PN[:, T:2 * T], NW, 1.5, PN[:, T:2 * T], ALU.add, ALU.mult))
                    for ch in range(CONVC):
                        ins = V_.scalar_tensor_tensor(CA[:, ch, :], CA[:, ch, :], vec("conv_ln_g_2", CONVC * l + ch),
                                                      PN[:, T:2 * T], ALU.mult, ALU.mult)
                    done(ins)
                    for ch in range(CONVC):
                        ins = V_.tensor_scalar(CA[:, ch, :], CA[:, ch, :], vec("conv_ln_b_2", CONVC * l + ch), None,
                                               ALU.add)
                    done(ins)
                elif j == 2:
                    evacuate(grp)
                    diff_softmax(0, l)
                else:
                    gate(grp, tell=True)
                    from_act()
                    done(V_.scalar_tensor_tensor(CA, SC_SQ, 1.0, CA, ALU.add, ALU.mult))
                    V_.tensor_scalar(CA, CA, 0.5, None, ALU.mult).then_inc(s.dve, 1)
                    dve.wait_ge(s.dve, c.next("dve"))
                    for q in range(2):
                        low(YH, q, CA[:, 2 * q:2 * q + 2, :], base=DC)

            def post_pw(grp, j):
                x = evacuate(grp)
                V_.scalar_tensor_tensor(TT[:, 0, :, :], two(x), 0.5, SC[:, 2 * j:2 * j + 2, :], ALU.mult, ALU.mult)\
                    .then_inc(s.dve, 1)
                dve.wait_ge(s.dve, c.next("dve"))
                low(YH, j, TT[:, 0, :, :], base=12)

            def post_diffb(grp, i, j, l):
                if j == 0:
                    evacuate(grp, two(QR[:, 0, :]))
                    diff_gated()
                elif j in (1, 3):
                    post_pw(grp, j // 2)
                elif j == 2:
                    evacuate(grp, two(QR[:, 1, :]))
                    diff_out(0, l)
                elif j == 4:
                    evacuate(grp)
                    diff_softmax(1, l)
                else:
                    gate(grp)

            def tail(l):
                diff_gated()
                diff_out(1, l)

            def post_out(grp, i, j, at=0):
                x = evacuate(grp)
                n = 2 * i + (j + at)
                m = pair(XRES, n)
                done(V_.scalar_tensor_tensor(m, m, ALPHA, two(x), ALU.mult, ALU.add))
                accumulate(n, m)

            def ln(l):
                dve.wait_ge(s.sum, c.next("sum"))
                mean = Gf[:, 0, T:2 * T]
                done(V_.tensor_scalar(mean, PX[:, 0, 0:T], -1.0 / D, None, ALU.mult))
                for q in range(DC // 2):
                    V_.tensor_tensor(pair(XRES, q), pair(XRES, q), mean.unsqueeze(1).broadcast_to([P, 2, T]), ALU.add)\
                        .then_inc(s.dve, 1)
                    dve.wait_ge(s.dve, c.next("dve"))
                from_act()
                newton(Gf[:, 0, 0:T], Gf[:, 0, T:2 * T], Gf[:, 1, 0:T])
                for q in range(DC // 2):
                    if q >= 2:
                        if l == 0:
                            low(XH, q - 2, pair(XRES, q - 2))
                        else:
                            dve.wait_ge(s.final, q - 1)
                    for e in range(2):
                        ins = V_.scalar_tensor_tensor(TT[:, q % 2, e, :], XRES[:, 2 * q + e, :],
                                                      vec("ln_g_2", DC * l + 2 * q + e), Gf[:, 0, T:2 * T],
                                                      ALU.mult, ALU.mult)
                    ins.then_inc(s.dve, 1)
                    dve.wait_ge(s.dve, c.next("dve"))
                for q in (6, 7):
                    if l == 0:
                        low(XH, q, pair(XRES, q))

            for q in range(DC // 2):
                dve.wait_ge(s.tp, q + 1)
                V_.tensor_copy(pair(XRES, q), two(PG[:, q % 4, :])).then_inc(s.tpd, 1)
                dve.wait_ge(s.tpd, c.next("tpd"))
            dve.wait_ge(s.tp, DC // 2 + 1)
            V_.tensor_copy(VEC[:, 0:512], PX[:, 2, :])
            V_.tensor_copy(VEC[:, 512:VEC_N], PX[:, 3, 0:VEC_N - 512]).then_inc(s.tpd, 1)
            dve.wait_ge(s.tpd, DC // 2 + 1)
            from_act()
            done(V_.tensor_scalar(Tf[:, 0, 0:RC], vec("lru_lambda", 0, RC), 0.0, None, ALU.min))
            done(V_.tensor_tensor(der(D_SP, RC), der(D_SP, RC), Tf[:, 0, 0:RC], ALU.subtract))
            done(V_.tensor_scalar(der(D_SP, RC), der(D_SP, RC), LRU_HALF_C, None, ALU.mult))
            V_.tensor_scalar(der(D_NSP, RC), der(D_SP, RC), -1.0, None, ALU.mult)
            dve.wait_ge(s.lam, 16)
            lam = Fv[:, NB * D:NB * D + 512].rearrange("p (g two d) -> p g two d", two=2, d=64)
            done(V_.tensor_tensor(Tf[:, 1, 0:256].rearrange("p (g d) -> p g d", d=64), lam[:, :, 0, :],
                                  lam[:, :, 1, :], ALU.mult))
            V_.reduce_sum(der(D_RED, 4), Tf[:, 1, 0:256].rearrange("p (g d) -> p g d", d=64), AX).then_inc(s.dve, 1)
            dve.wait_ge(s.dve, c.next("dve"))
            from_act()
            for l in range(2):
                done(V_.tensor_tensor(der(D_NLAM + l), der(D_RED + 2 * l + 1), der(D_RED + 2 * l), ALU.subtract))
                done(V_.tensor_scalar(der(D_NLAM + l), der(D_NLAM + l), -LAM_INIT[l], None, ALU.add))

            def post(name):
                return {
                    "attn": post_attn,
                    "gate_a0": lambda g_, i, j: post_gate_a(g_, i, j, 0),
                    "gate_a1": lambda g_, i, j: post_gate_a(g_, i, j, 4),
                    "attn_out": post_attn_out, "x_r": post_x_r,
                    "x_r_last": lambda g_, i, j: post_x_r(g_, i, j, 20),
                    "gate_r": post_gate_r, "g_r": post_g_r,
                    "g_r_last": lambda g_, i, j: post_g_r(g_, i, j, 10),
                    "rnn_out": post_rnn_out, "w_o": lambda g_, i, j: post_fold(g_, 2 * i + j, 0.5, "g_ffn"),
                    "gu0": lambda g_, i, j: post_gu(g_, i, j, 0), "gu1": lambda g_, i, j: post_gu(g_, i, j, 1),
                    "gu2": lambda g_, i, j: post_gu(g_, i, j, 2),
                    "down0": residual, "down1": residual,
                    "down2": lambda g_, i, j: post_fold(g_, 4 * i + j, 1.0, "g_ple"),
                    "ple": post_ple,
                    "conf0": lambda g_, i, j: post_conf(g_, i, j, 0), "conf1": lambda g_, i, j: post_conf(g_, i, j, 1),
                    "dil0": lambda g_, i, j: post_dil(g_, i, j, 0), "dil1": lambda g_, i, j: post_dil(g_, i, j, 1),
                    "diffa0": lambda g_, i, j: post_diffa(g_, i, j, 0),
                    "diffa1": lambda g_, i, j: post_diffa(g_, i, j, 1),
                    "diffb0": lambda g_, i, j: post_diffb(g_, i, j, 0),
                    "diffb1": lambda g_, i, j: post_diffb(g_, i, j, 1),
                    "outa0": post_out, "outa1": post_out,
                    "outb0": lambda g_, i, j: post_out(g_, i, j, 2), "outb1": lambda g_, i, j: post_out(g_, i, j, 2),
                }[name]

            between = {"tables": lambda: None, "tail0": lambda: tail(0), "tail1": lambda: tail(1),
                       "ln0": lambda: ln(0), "ln1": lambda: ln(1)}
            pending = [lambda: norm("g_mix")]
            for ph in phases:
                if ph.name in between:
                    pending.append(between[ph.name])
                    continue
                fn, J, B = post(ph.name), len(ph.body), ph.body
                for j, grp in enumerate(B):
                    split(grp)
                    for job in pending:
                        job()
                    pending = [lambda fn=fn, grp=grp, j=j: fn(grp, 0, j)]

                def turn(i):
                    for j, grp in enumerate(B):
                        split(grp)
                        fn(B[J - 1], i - 1, J - 1) if j == 0 else fn(B[j - 1], i, j - 1)
                c.loop(1, ph.n, turn)
                pending = [lambda fn=fn, B=B, n=ph.n, J=J: fn(B[J - 1], n - 1, J - 1)]
            for job in pending:
                job()
            for q in range(DC // 2):
                dve.wait_ge(s.tp, TP_OUT + q + 1)
                V_.tensor_copy(OUTV[:, :, COLS * q:COLS * q + COLS], PG[:, q % 4, :].rearrange(
                    "p (b n) -> p b n", b=NB)).then_inc(s.tpd, 1)
                dve.wait_ge(s.tpd, c.next("tpd"))

        @block.tensor
        def _(pe):
            c = Counts(pe, "pe", turns, real)
            mm = nc.tensor.matmul

            def group(grp, fresh=(), mid=None):
                par = c.n.get("group", 0) % 2
                if c.n.get("group", 0) >= 2:
                    pe.wait_ge(s.evac, c.value("group", -1))
                units = grp.units()
                for n, (k0, nk) in enumerate(units):
                    slot = c.n.get("unit", 0) % SLOTS
                    pe.wait_ge(s.lo, c.value("unit", 1))
                    if n < len(fresh) and fresh[n]:
                        pe.wait_ge(s.op, c.next("op", fresh[n]))
                    for kk in range(nk):
                        x = grp.X[:, grp.base + k0 + kk, :]
                        for j in range(2):
                            b = 2 * par + j
                            cs = slice(P * j, P * j + P)
                            mm(PG[:, b, :], WH[:, slot, kk, cs], x, start=n == 0 and kk == 0, stop=False)
                            last = mm(PG[:, b, T:2 * T], WL[:, slot, kk, cs], x[:, 0:T], start=False,
                                      stop=n == len(units) - 1 and kk == nk - 1)
                    last.then_inc(s.unit, 1)
                    c.add("unit")
                    if mid and n in mid:
                        mid[n]()
                c.add("group")

            def ready():
                pe.wait_ge(s.ready, c.next("ready"))

            def squares_in(m=1):
                pe.wait_ge(s.sq, c.next("sq", m))

            def sum_features(bank, src, first, last):
                return mm(PX[:, bank, 0:src.shape[-1]], ONES, src, start=first, stop=last)

            def v_transposes(par):
                for h in range(2):
                    for b in range(NB):
                        at = P * (2 * h + b)
                        last = nc.tensor.transpose(PX[:, 2, at:at + P], G[:, par, h, P * b:P * b + P], IDENT)
                return last

            def z_attn():
                ready()
                for h in range(2):
                    o = T * h
                    mm(PX[:, h, 0:T], QR[:, 1, o:o + P], QR[:, 0, o:o + T], start=True, stop=True)
                    mm(PX[:, h, T:T + P], QR[:, 1, o + P:o + T], QR[:, 0, o + P:o + T], start=True, stop=True)
                v_transposes(c.n["group"] % 2).then_inc(s.scores, 1)

            def e_attn():
                ready()
                for h in range(2):
                    mm(PX[:, 2 + h, T:T + P], AFTER, SP[:, h, T:T + P], start=True, stop=True)
                    mm(PX[:, 2 + h, 0:T], AFTER, SP[:, h, 0:T], start=True, stop=False)
                    last = mm(PX[:, 2 + h, P:T], ONES, SP[:, h, T:T + P], start=False, stop=True)
                last.then_inc(s.later, 1)

            def heads_out(tell):
                ready()
                for h in range(2):
                    o = T * h
                    mm(PX[:, 3, o:o + T], V[:, 2 * h, :], W[:, h, 0:T], start=True, stop=False)
                    last = mm(PX[:, 3, o + P:o + T], V[:, 2 * h + 1, :], W[:, h, T:T + P], start=False, stop=True)
                last.then_inc(tell, 1)

            def after_attn(i, j):
                m, what = divmod(j, 3)
                before = not (isinstance(i, int) and i == 0 and m == 0)
                if what == 0:
                    if before:
                        z_attn()
                else:
                    if before:
                        e_attn() if what == 1 else heads_out(s.heads)
                    squares_in()
                    sum_features(what - 1, SQ2[:, what - 1, :], True, True).then_inc(s.rms, 1)

            def after_gate_a0(i, j):
                if j == 0:
                    z_attn()
                elif j == 1:
                    e_attn()
                elif j == 2:
                    heads_out(s.heads)

            def after_gate_r(i, g):
                for j in range(3 * g, min(3 * g + 3, RC)):
                    if j >= 4:
                        pe.wait_ge(s.bdd, j - 3)
                    for m in range(2):
                        for i in users[j]:
                            if m == 0:
                                pe.wait_ge(s.xc, i + 1)
                                pe.wait_ge(strip_sems[i % 8], strip_due[i])
                            at = P * (j - strips[i][0])
                            last = mm(PX[:, j % 4, T * m:T * m + T], BDS[:, i % 8, m, at:at + P], XC[:, i, :],
                                      start=i == users[j][0], stop=i == users[j][-1])
                    last.then_inc(s.bd, 1)

            def add_pair(src, q, bank, first, last):
                squares_in()
                for e in range(2):
                    ins = sum_features(bank, src[:, 2 * q + e, :], first and e == 0, last and e == 1)
                return ins

            def sum_acc(tell):
                ready()
                sum_features(0, ACC[:, 0:T], True, False)
                sum_features(0, ACC[:, T:2 * T], False, True).then_inc(tell, 1)

            def after_gu0(i, j):
                if not (isinstance(i, int) and i == 0):
                    return
                if j == 0:
                    sum_acc(s.ss)
                    pe.wait_ge(s.p_in, 16)
                    for k in range(2):
                        for b in range(NB):
                            at = T * k + P * b
                            last = nc.tensor.transpose(PX[:, 1, at:at + P],
                                                       RT[:, 3072 + T * b + P * k:3072 + T * b + P * k + P], IDENT)
                    last.then_inc(s.tp, 1)
                    c.add("op")
                elif j == 1:
                    pe.wait_ge(s.tab, 48)
                    mm(PX[0:HEADS2, 2, 0:384], MIXf[0:NBUCK, 3072:3072 + HEADS2], MIXf[0:NBUCK, 3100:3484],
                       start=True, stop=True).then_inc(s.tp, 1)

            def after_gu1(i, j):
                if isinstance(i, int) and i == 0 and j < 3:
                    pe.wait_ge(s.tb, 16 * HEADS2)
                    if j:
                        pe.wait_ge(s.flipped, 2 * j)
                    for h in (2 * j, 2 * j + 1):
                        mm(PX[:, 2 + h % 2, :], FLIP, MIXf[:, 512 * h:512 * h + 512], start=True, stop=True)\
                            .then_inc(s.flip, 1)

            def after_ple(i, j):
                if isinstance(i, int) and i == 0 and j == 0:
                    sum_acc(s.ss)

            def z_soft(comps):
                for h in range(2):
                    for x in range(comps):
                        r = slice(P // comps * x, P // comps * (x + 1))
                        bank, o = comps * h + x, T * h
                        mm(PX[:, bank, 0:P], QR[r, 0, o:o + P], QR[r, 1, o:o + P], start=True, stop=True)
                        last = mm(PX[:, bank, P:3 * P], QR[r, 0, o + P:o + T], QR[r, 1, o:o + T],
                                  start=True, stop=True)
                last.then_inc(s.scores2, 1)

            def pt_soft(comps):
                ready()
                for h in range(2):
                    x = S4[:, comps * h, :]
                    for to, frm in ((0, 0), (P, P), (2 * P, 2 * P)):
                        nc.tensor.transpose(PX[:, h, to:to + P], x[:, frm:frm + P], IDENT)
                v_transposes(c.n["group"] % 2).then_inc(s.turned, 1)

            def diff_sum():
                squares_in()
                sum_features(3, SQa, True, True).then_inc(s.rms, 1)

            def evac_of_k():
                pe.wait_ge(s.evac, c.value("group", -1))

            def after_dil(i, j):
                if j == 0:
                    if not (isinstance(i, int) and i == 0):
                        heads_out(s.heads2)
                elif j == 2:
                    evac_of_k()
                    z_soft(1)
                elif j == 3:
                    pt_soft(1)

            def after_diffa(i, j):
                if j == 0:
                    heads_out(s.heads2)
                    pe.wait_ge(s.conv, c.next("conv"))
                    for ch in range(CONVC):
                        last = sum_features(0, CA[:, ch, :], ch == 0, ch == CONVC - 1)
                    last.then_inc(s.sum, 1)
                elif j == 1:
                    squares_in()
                    for ch in range(CONVC):
                        last = sum_features(1, SC_SQ[:, ch, :], ch == 0, ch == CONVC - 1)
                    last.then_inc(s.sumsq, 1)
                elif j == 2:
                    evac_of_k()
                    ready()
                    z_soft(2)
                else:
                    pt_soft(2)

            def after_diffb(i, j):
                if j == 0:
                    heads_out(s.heads2)
                elif j == 2:
                    diff_sum()
                elif j == 4:
                    evac_of_k()
                    pe.wait_ge(s.op, c.value("op", 2))
                    z_soft(2)
                elif j == 5:
                    pt_soft(2)

            tail_mid = {1: lambda: heads_out(s.heads2), 2: diff_sum}

            def ln():
                sum_acc(s.sum)
                for q in range(8):
                    last = add_pair(XC, q, 1, q == 0, q == 7)
                last.then_inc(s.sumsq, 1)

            after = {"attn": after_attn, "gate_a0": after_gate_a0, "gate_r": after_gate_r, "gu0": after_gu0,
                     "gu1": after_gu1, "ple": after_ple, "dil0": after_dil, "dil1": after_dil,
                     "diffa0": after_diffa, "diffa1": after_diffa, "diffb0": after_diffb, "diffb1": after_diffb}
            between = {"tables": lambda: None, "tail0": lambda: None, "tail1": lambda: None, "ln0": ln, "ln1": ln}

            pe.wait_ge(s.mats, 16)
            pe.wait_ge(s.x_in, 16)
            for q in range(DC // 2):
                if q >= 4:
                    pe.wait_ge(s.tpd, q - 3)
                for e in range(2):
                    for b in range(NB):
                        at = T * e + P * b
                        src = D * b + P * (2 * q + e)
                        last = nc.tensor.transpose(PG[:, q % 4, at:at + P], Fv[:, src:src + P], IDENT)
                last.then_inc(s.tp, 1)
            pe.wait_ge(s.vecs, 16 * VEC_DMAS)
            for t in range(VEC_TILES):
                m = min(P, VEC_N - P * t)
                last = nc.tensor.transpose(PX[:, 2 + t // 4, P * (t % 4):P * (t % 4) + m],
                                           RT[0:m, P * t:P * t + P], IDENT[0:m, 0:m])
            last.then_inc(s.tp, 1)
            for q in range(DC // 2):
                ins = add_pair(MIX, q, 0, q == 0, q == DC // 2 - 1)
            ins.then_inc(s.ss, 1)
            pe.wait_ge(s.tpd, DC // 2 + 1)

            for ph in phases:
                if ph.name in between:
                    between[ph.name]()
                    continue
                hook = after.get(ph.name)

                def turn(i):
                    for j, grp in enumerate(ph.body):
                        first = isinstance(i, int) and i == 0
                        group(grp, ph.fresh.get(j, ()) if first else (),
                              tail_mid if first and j == 0 and ph.name[:4] == "outa" else None)
                        if hook:
                            hook(i, j)
                turn(0)
                c.loop(1, ph.n, turn)
            for q in range(DC // 2):
                if not STOP:
                    pe.wait_ge(s.final, q + 1)
                if q >= 4:
                    pe.wait_ge(s.tpd, TPD_OUT + q - 3)
                for e in range(2):
                    for b in range(NB):
                        at = P * NB * 0 + T * b + P * e
                        last = nc.tensor.transpose(PG[:, q % 4, at:at + P], XRES[:, 2 * q + e, P * b:P * b + P],
                                                   IDENT)
                last.then_inc(s.tp, 1)


_INS = ["x", "p", "g_mix", "w_in", "conv_w", "conv_b", "w_rg_a", "b_rg_a", "w_rg_x", "b_rg_x", "lru_lambda",
        "q_gain", "k_gain", "w_rnn_out", "w_attn_out", "w_o", "g_ffn", "w_ffn_gu", "w_ffn_down", "g_ple",
        "w_ple_gate", "w_ple_proj", "w_in_2", "diff_lambda_2", "diff_head_gain_2", "conv_dw_2", "conv_b_2",
        "conv_ln_g_2", "conv_ln_b_2", "conv_pw_2", "w_out_2", "ln_g_2", "ln_b_2", "rel_bias_2"]


def kernel(**inputs):
    import concourse.bacc as _bacc
    from concourse.bass_utils import run_bass_kernel_spmd as _run

    data = {name: np.ascontiguousarray(inputs[name]) for name in _INS}
    data.update(zip(("c_mats", "c_keep", "c_onehot", "c_add"), shape_constants()))
    turns = {}
    for real in (False, True):
        nc = _bacc.Bacc("TRN2", target_bir_lowering=False, num_devices=1)
        arrays, A = {}, {}
        for name, a in data.items():
            arrays[f"in_{name}_dram"] = a
            A[name] = nc.dram_tensor(f"in_{name}_dram", a.shape, mybir.dt.from_np(a.dtype), kind="ExternalInput").ap()
        A["out"] = nc.dram_tensor("out_0_dram", (1, T, D), mybir.dt.float32, kind="ExternalOutput").ap()
        program(nc, A, turns, real)
    r = _run(nc, [arrays], core_ids=[0])
    return r.results[0]["out_0_dram"]
```

```python
import numpy as np
from contextlib import ExitStack
from collections import namedtuple
import concourse.bass as bass
from concourse import mybir

STOP = None

P = 128
T = 256
NB = T // P
D = 2048
DC = D // P
RNN = 2816
RC = RNN // P
RB = 176
TAPS = 4
FF = 5632
FF_PARTS = (16, 16, 12)
PLE = 256
TAPS2 = 31
COLS = 256
SLOTS = 4
UK = 4
NBUCK = 32
HEADS2 = 12
CONVC = 4
EPS = 1e-6
EPS2 = 1e-5
ALPHA = 4.0 ** 0.25
QSCALE = 128.0 ** -0.5
ASCALE = 64.0 ** -0.5
GELU_C = 0.044715
GELU_S = float(np.sqrt(2.0 / np.pi))
NEG = -1e30
LRU_HALF_C = 4.0
LAM_INIT = [0.8 - 0.6 * float(np.exp(-0.3 * layer)) for layer in range(2)]

VEC_ROWS = [("g_mix", 16), ("g_ffn", 16), ("g_ple", 16), ("conv_b", 22), ("conv_w", 88), ("b_rg_a", 22),
            ("b_rg_x", 22), ("lru_lambda", 22), ("q_gain", 1), ("k_gain", 1), ("diff_head_gain_2", 2),
            ("conv_dw_2", 248), ("conv_b_2", 8), ("conv_ln_g_2", 8), ("conv_ln_b_2", 8), ("ln_g_2", 32),
            ("ln_b_2", 32)]
VEC_AT, _n = {}, 0
for _name, _rows in VEC_ROWS:
    VEC_AT[_name] = _n
    _n += _rows
VEC_N = _n
VEC_TILES = (VEC_N + P - 1) // P


def t5_bucket_np(d):
    exact = NBUCK // 2
    df = np.maximum(d, 1).astype(np.float32)
    large = exact + (np.log(df / np.float32(exact)) / np.float32(np.log(2048 / exact))
                     * np.float32(NBUCK - exact)).astype(np.int32)
    return np.where(d < exact, d, np.minimum(large, NBUCK - 1))


def shape_constants():
    eye = np.eye(P, dtype=np.float32)
    after = np.tril(np.ones((P, P), np.float32), -1)
    ones = np.ones((P, P), np.float32)
    flip = np.ascontiguousarray(eye[:, ::-1])
    before = np.triu(np.ones((P, P), np.float32), 1)
    keep = np.concatenate([before, ones, before], 1)
    mats = np.concatenate([eye, after, ones, flip], 1)
    i = np.arange(384)
    dist = 255 - i
    onehot = (t5_bucket_np(np.maximum(dist, 0))[None] == np.arange(NBUCK)[:, None]).astype(np.float32)
    add = np.zeros((HEADS2, 384), np.float32)
    times = (dist <= 128).astype(int) + (dist % 4 == 0) + (dist % 16 == 0)
    add[4:] = np.where(times > 0, np.log(np.maximum(times, 1)), NEG)
    add[:, dist < 0] = NEG
    return mats, keep, onehot, add


class Counts:

    def __init__(self, eng, who, turns, real):
        self.eng, self.who, self.turns, self.real = eng, who, turns, real
        self.n, self.per, self.var, self.first, self.loops = {}, {}, None, 0, 0

    def add(self, key, m=1):
        self.n[key] = self.n.get(key, 0) + m

    def value(self, key, extra=0, div=1, mul=1):
        n = self.n.get(key, 0) + extra
        if self.var is None:
            return mul * (n // div)
        k = self.per.get(key, 0)
        if k == 0:
            return mul * (n // div)
        assert k % div == 0 or not self.real
        k //= div
        c = mul * (n // div - self.first * k)
        v = self.var * (mul * k) if mul * k != 1 else self.var
        return v + c if c >= 0 else v - (-c)

    def next(self, key, m=1, mul=1):
        self.add(key, m)
        return self.value(key, mul=mul)

    def loop(self, first, last, body):
        if last - first < 2:
            for i in range(first, last):
                body(i)
            return
        name = (self.who, self.loops)
        self.loops += 1
        start = dict(self.n)
        self.per = self.turns.get(name, {})
        self.first = first
        with self.eng.Fori(first, last) as i:
            self.var = i
            body(i)
        self.var = None
        met = {k: v - start.get(k, 0) for k, v in self.n.items()}
        assert not self.real or met == {k: self.per.get(k, 0) for k in met}, (name, met, self.per)
        self.turns[name] = met
        for k, v in met.items():
            self.n[k] = start.get(k, 0) + v * (last - first)


class Group:

    def __init__(self, W, K, col, step, X, base=0, part=None, opens=True, closes=True, ahead=0, seen=None):
        self.W, self.K, self.col, self.step, self.X, self.base = W, K, col, step, X, base
        self.part, self.opens, self.closes, self.ahead = part or slice(None), opens, closes, ahead
        self.seen = seen or len(self.units())

    def units(self):
        return [(k, min(UK, self.K - k)) for k in range(0, self.K, UK)][self.part]


class Phase:

    def __init__(self, name, n, body, fresh=None):
        self.name, self.n, self.body, self.fresh = name, n, body, fresh or {}


def each_unit(K):
    return {0: [min(UK, K - k) // 2 for k in range(0, K, UK)]}


def gate_tiles():
    strips, users = [], [[] for _ in range(RC)]
    for i in range(RC):
        n0, n1 = P * i // RB, (P * i + P - 1) // RB
        j0 = RB * n0 // P
        pieces = [(n, max(P * i, RB * n), min(P * i + P, RB * (n + 1))) for n in range(n0, n1 + 1)]
        strips.append((j0, pieces))
        for j in range(RC):
            if any(RB * n < P * j + P and RB * (n + 1) > P * j for n in range(n0, n1 + 1)):
                users[j].append(i)
    return strips, users


def program(nc, A, turns, real):
    fp = mybir.dt.float32
    fr = mybir.dt.float32r
    ALU = mybir.AluOpType
    ACT = mybir.ActivationFunctionType
    AX = mybir.AxisListType.X
    ctx = ExitStack()
    with ctx:
        def sb(name, shape, dt=fp):
            return ctx.enter_context(nc.sbuf_tensor(name, shape, dt))

        RAW = sb("RAW", [P, SLOTS, UK, COLS])
        WH = sb("WH", [P, SLOTS, UK, COLS], fr)
        WL = sb("WL", [P, SLOTS, UK, COLS], fr)
        XRES = sb("XRES", [P, DC, T])
        XH = sb("XH", [P, DC, 2 * T], fr)
        with nc.sbuf_tensor("YH", [P, RC, 2 * T], fr) as YH:
            pass
        AL = sb("AL", [P, 2 * RC * T])
        MIX = sb("MIX", [P, DC, T])
        F = sb("F", [P, RC * T])
        RT = sb("RT", [P, 16 * T])
        G = sb("G", [P, 2, 2, T])
        TT = sb("TT", [P, 2, 2, T])
        MATS = sb("MATS", [P, 4 * P])
        VEC = sb("VEC", [P, VEC_TILES * P])
        DER = sb("DER", [P, 128])
        PG = ctx.enter_context(nc.psum_tensor("PG", [P, 4, 512], fp))
        PX = ctx.enter_context(nc.psum_tensor("PX", [P, 4, 512], fp))
        strip_dram = nc.dram_tensor("bias_strip", [HEADS2, 384], fp).ap()

        IDENT, AFTER, ONES, FLIP = (MATS[:, P * i:P * i + P] for i in range(4))
        Fv = F[:, :]
        XC = F[:, :].rearrange("p (c t) -> p c t", t=T)
        RTc = RT[:, :].rearrange("p (c t) -> p c t", t=T)
        Gf = G[:, :, :, :].rearrange("p a b t -> p a (b t)")
        Tf = TT[:, :, :, :].rearrange("p a b t -> p a (b t)")

        def vec(name, i=0, m=1):
            at = VEC_AT[name] + i
            return VEC[:, at:at + m] if isinstance(at, int) else VEC[:, bass.ds(at, m)]

        EPS_AP, EPS2_AP = EPS, EPS2
        VEC_DMAS = sum(1 + (at % P + rows - 1) // P for at, rows in
                       ((VEC_AT[n], r) for n, r in VEC_ROWS[1:]))
        TP_STRIP, TP_P, TP_OUT = DC // 2 + 3, DC // 2 + 2, DC // 2 + 3
        TPD_STRIP = TPD_OUT = DC // 2 + 2
        OPS_MIX = DC // 2 + DC // 2 + RC // 2 + DC // 2
        GATES_FROM = 8 * 3 + 8 + 8
        GROUPS_BEFORE_G_R = GATES_FROM + 11 + 8
        POOL_TAPS = 15
        CB = RT[:, 12 * T:16 * T].rearrange("p (c t) -> p c t", t=T)
        D_HBA, D_HBX, D_SP, D_NSP, D_QG, D_HG, D_NLAM, D_RED = 0, 22, 44, 66, 88, 89, 91, 93
        D_SS, D_MS, D_R, D_LN = 118, 120, 122, 124

        def der(at, m=1):
            return DER[:, at:at + m]

        QR = F[:, 0:1024].rearrange("p (a n) -> p a n", a=2)
        SQ2 = F[:, 1024:2048].rearrange("p (a n) -> p a n", a=2)
        V = F[:, 2048:2560].rearrange("p (a n) -> p a n", a=4)
        L = F[:, 2560:3328].rearrange("p (a n) -> p a n", a=2)
        SP = F[:, 3328:4096].rearrange("p (a n) -> p a n", a=2)
        T1 = F[:, 4096:4864].rearrange("p (a n) -> p a n", a=2)
        W = F[:, 4864:5632].rearrange("p (a n) -> p a n", a=2)
        KEEP = RT[:, 1024:1408]
        PT = (MIX[:, 5, :], F[:, 4608:4608 + T])
        S4 = F[:, 2560:4096].rearrange("p (a n) -> p a n", a=4)
        PTS = W
        OA = F[:, 4096:4608]
        SG = F[:, 1024:1536]
        SQa = F[:, 1536:2048]
        HCW = 32 + T
        HC = MIX[:, 0:5, :].rearrange("p c t -> p (c t)")[:, 0:CONVC * HCW].rearrange("p (c t) -> p c t", t=HCW)
        CA = MIX[:, 6:10, :]
        SC = MIX[:, 10:14, :]
        SC_SQ = MIX[:, 0:CONVC, :]
        PN = MIX[:, 14:16, :].rearrange("p c t -> p (c t)")
        RR = F[:, 0:T]
        ACC = F[:, 512:1024]
        SQP = F[:, 1024:1536]
        MSQ = F[:, 1536:1536 + T]
        NW = F[:, 1792:1792 + T]
        ACC2 = F[:, 2048:2560]
        PILOT = F[:, 2560:2560 + T]
        SQ6 = F[:, 2816:2816 + 6 * T].rearrange("p (c t) -> p c t", t=T)
        BDS = AL[:, 0:8 * 1024].rearrange("p (s m n) -> p s m n", s=8, m=2)
        TA, TX, AA, TE = (AL[:, 8192 + 768 * q:8192 + 768 * q + 768].rearrange("p (c t) -> p c t", t=T)
                          for q in range(4))
        MIXf = MIX[:, :, :].rearrange("p c t -> p (c t)")
        OUTV = MIXf.rearrange("p (b d) -> p b d", b=NB)
        AB = RT[:, 0:HEADS2 * T].rearrange("p (h t) -> p h t", t=T)

        def wv(ap):
            return ap.rearrange("(c p) n -> p c n", p=P)

        w_in = wv(A["w_in"][0])
        w_rnn, w_att, w_o = wv(A["w_rnn_out"][0]), wv(A["w_attn_out"][0]), wv(A["w_o"][0])
        w_gu, w_dn = wv(A["w_ffn_gu"][0]), wv(A["w_ffn_down"][0])
        w_pg, w_pp = wv(A["w_ple_gate"][0]), wv(A["w_ple_proj"][0])
        QO = 2 * RNN
        KO, VO = QO + D, QO + 2 * D
        GR, GA = QO + 3 * D, QO + 4 * D

        def seq(w, K, col, X, width=2, base=0):
            return [Group(w, K, col + COLS * j, COLS * width, X, base) for j in range(width)]

        phases = []
        body = []
        for m in range(2):
            for off in (QO, KO, VO):
                body.append(Group(w_in, DC, off + COLS * m, 2 * COLS, XH))
        phases.append(Phase("attn", 4, body, each_unit(DC)))
        phases.append(Phase("gate_a0", 1, seq(w_in, DC, GA, XH, 4)))
        phases.append(Phase("gate_a1", 2, seq(w_in, DC, GA + 4 * COLS, XH)))
        phases.append(Phase("attn_out", 4, seq(w_att, DC, 0, YH), each_unit(DC)))
        phases.append(Phase("x_r", 5, seq(w_in, DC, 0, XH)))
        phases.append(Phase("x_r_last", 1, seq(w_in, DC, 10 * COLS, XH, 1)))
        phases.append(Phase("gate_r", 1, seq(w_in, DC, GR, XH, 8)))
        phases.append(Phase("g_r", 5, seq(w_in, DC, RNN, XH)))
        phases.append(Phase("g_r_last", 1, seq(w_in, DC, RNN + 10 * COLS, XH, 1)))
        phases.append(Phase("rnn_out", 4, seq(w_rnn, RC, 0, YH), each_unit(RC)))
        phases.append(Phase("tables", 0, []))
        phases.append(Phase("w_o", 4, seq(w_o, DC, 0, XH), each_unit(DC)))
        at = 0
        for h, K in enumerate(FF_PARTS):
            gu = []
            for m in range(2):
                gu.append(Group(w_gu, DC, P * at + COLS * m, 2 * COLS, YH))
                gu.append(Group(w_gu, DC, FF + P * at + COLS * m, 2 * COLS, YH))
            phases.append(Phase(f"gu{h}", K // 4, gu, each_unit(DC) if h == 0 else None))
            width = 2 if K // UK % 2 == 0 else 4
            phases.append(Phase(f"down{h}", 8 // width, seq(w_dn[:, at:at + K, :], K, 0, XH, width), each_unit(K)))
            at += K
        phases.append(Phase("proj", 1, seq(w_pp, 2, 0, YH, 8, base=DC)))
        phases.append(Phase("ple", 4, seq(w_pg, DC, 0, YH), each_unit(DC)))
        for l in range(2):
            w2, wp, wo = wv(A["w_in_2"][l]), wv(A["conv_pw_2"][l]), wv(A["w_out_2"][l])
            A0, B0, C0 = 0, 2048, 6144
            cb = [C0, C0 + 512, C0 + COLS, C0 + 512 + COLS, C0 + 1024, C0 + 1024 + COLS]
            diff = [[Group(w2, DC, A0 + 512 * o + COLS * m, 0, XH) for o in range(4)] for m in range(2)]
            pw = seq(wp, CONVC, 0, YH, 2, base=DC)
            phases.append(Phase(f"conf{l}", 1, [Group(w2, DC, c, 0, XH) for c in cb], each_unit(DC)))
            phases.append(Phase(f"dil{l}", 4, [Group(w2, DC, B0 + 1024 * o, COLS, XH) for o in range(4)]))
            phases.append(Phase(f"diffa{l}", 1, diff[0]))
            q, k, v, g = diff[1]
            phases.append(Phase(f"diffb{l}", 1, [q, pw[0], k, pw[1], v, g], {1: [6]}))
            U = DC // UK
            out = [Group(wo, DC, 0, 0, YH, part=slice(1, U), closes=False),
                   Group(wo, DC, COLS, 0, YH, part=slice(1, U), closes=False, ahead=1),
                   Group(wo, DC, 0, 0, YH, part=slice(0, 1), opens=False, seen=2 * U - 1),
                   Group(wo, DC, COLS, 0, YH, part=slice(0, 1), opens=False)]
            phases.append(Phase(f"outa{l}", 1, out, {0: [0, 0, 3], 2: [1]}))
            phases.append(Phase(f"outb{l}", 3, seq(wo, DC, 2 * COLS, YH)))
            phases.append(Phase(f"ln{l}", 0, []))
        if STOP:
            names = [p.name for p in phases]
            phases = phases[:names.index(STOP) + 1]

        NAMES = ["raw0", "raw1", "raw2", "raw3",
                 "hi", "lo",
                 "unit",
                 "evac",
                 "op",
                 "x_in0", "x_in1", "mats", "g_in", "vecs", "lam", "keep", "p_in", "tab", "strip", "tb", "out",
                 "tp",
                 "tpd",
                 "sq",
                 "ss",
                 "act",
                 "dve",
                 "scores",
                 "later",
                 "rms",
                 "heads",
                 "scores2", "turned", "heads2",
                 "flip", "flipped",
                 "sum", "sumsq",
                 "final",
                 "chain",
                 "achain",
                 "ready",
                 "strip0", "strip1", "strip2", "strip3", "strip4", "strip5", "strip6", "strip7",
                 "gh",
                 "acc",
                 "glu",
                 "taps",
                 "conv",
                 "wiped",
                 "xc",
                 "bd",
                 "bdd",
                 ]
        Semaphores = namedtuple("Semaphores", NAMES)
        s = Semaphores(*(ctx.enter_context(nc.semaphore("s_" + name)) for name in NAMES))
        raw_sems = [s.raw0, s.raw1, s.raw2, s.raw3]
        strip_sems = [s.strip0, s.strip1, s.strip2, s.strip3, s.strip4, s.strip5, s.strip6, s.strip7]
        strips, users = gate_tiles()
        last_user = [max(j for j in range(RC) if i in users[j]) for i in range(RC)]
        block = ctx.enter_context(nc.Block())

        def pair(X, i):
            return X[:, 2 * i:2 * i + 2, :] if isinstance(i, int) else X[:, bass.ds(2 * i, 2), :]

        def hi2(X, i, base=0):
            if isinstance(i, int):
                return X[:, base + 2 * i:base + 2 * i + 2, 0:T]
            return X[:, bass.ds(2 * i + base, 2), 0:T]

        def lo2(X, i, base=0):
            if isinstance(i, int):
                return X[:, base + 2 * i:base + 2 * i + 2, T:2 * T]
            return X[:, bass.ds(2 * i + base, 2), T:2 * T]

        def load_vectors(sp):
            row = VEC_ROWS[0][1]
            for name, rows in VEC_ROWS[1:]:
                src = A[name].rearrange("a k (c p) -> (a k c) p", p=P) if len(A[name].shape) == 3 else \
                    A[name].rearrange("a (c p) -> (a c) p", p=P)
                at = 0
                while at < rows:
                    r = (row + at) % P
                    m = min(rows - at, P - r)
                    t = (row + at) // P
                    sp.dma_start(RT[r:r + m, P * t:P * t + P], src[at:at + m, :]).then_inc(s.vecs, 16)
                    at += m
                row += rows
            sp.dma_start(KEEP, A["c_keep"]).then_inc(s.keep, 16)
            sp.dma_start(Fv[:, NB * D:NB * D + 512],
                         A["diff_lambda_2"].rearrange("l a d -> (l a d)").partition_broadcast(P)).then_inc(s.lam, 16)

        @block.sync
        def _(sp):
            c = Counts(sp, "sp", turns, real)
            sp.dma_start(RT[0:DC, 0:P], A["g_mix"].rearrange("a (c p) -> (a c) p", p=P)).then_inc(s.g_in, 16)
            sp.wait_ge(s.x_in0, 16)

            def load(grp, i):
                col = grp.col + grp.step * i if grp.step else grp.col
                cols = slice(col, col + COLS) if isinstance(col, int) else bass.ds(col, COLS)
                for k, nk in grp.units():
                    u = c.n.get("unit", 0)
                    if u >= SLOTS:
                        sp.wait_ge(s.lo, c.value("unit", 1 - SLOTS))
                    sp.dma_start(RAW[:, u % SLOTS, 0:nk, :], grp.W[:, k:k + nk, cols])\
                        .then_inc(raw_sems[u % SLOTS], 16)
                    c.add("unit")

            for ph in phases:
                def turn(i):
                    for grp in ph.body:
                        load(grp, i)
                        if c.n["unit"] == SLOTS:
                            load_vectors(sp)
                if ph.n:
                    turn(0)
                    c.loop(1, ph.n, turn)
            for g in range(DC // 2):
                sp.wait_ge(s.tpd, 8 + 1 + 1 + g + 1)
                sp.dma_start(A["out"][0].rearrange("(b p) d -> p b d", p=P)[:, :, COLS * g:COLS * g + COLS],
                             OUTV[:, :, COLS * g:COLS * g + COLS]).then_inc(s.out, 16)
            sp.wait_ge(s.out, 16 * (DC // 2))

        @block.gpsimd
        def _(pool):
            for u in range(SLOTS):
                pool.wait_ge(s.hi, u + 1)
                nc.gpsimd.tensor_tensor(WL[:, u, :, :], RAW[:, u, :, :], WH[:, u, :, :].bitcast(fp), ALU.subtract)\
                    .then_inc(s.lo, 1)
            pool.wait_ge(s.lo, SLOTS)
            n = 0
            for i, (j0, pieces) in enumerate(strips):
                if i == 0:
                    pool.wait_ge(s.evac, GATES_FROM)
                if i >= 8:
                    pool.wait_ge(s.bd, last_user[i - 8] + 1)
                nc.gpsimd.memset(BDS[:, i % 8, :, :], 0.0).then_inc(s.wiped, 1)
                pool.wait_ge(s.wiped, i + 1)
                for n, r0, r1 in pieces:
                    at = RB * n - P * j0
                    for m, w in enumerate((A["w_rg_a"], A["w_rg_x"])):
                        pool.dma_start(BDS[r0 - P * i:r1 - P * i, i % 8, m, at:at + RB],
                                       w[0, n, r0 - RB * n:r1 - RB * n, :]).then_inc(strip_sems[i % 8], 16)

            for n in range(RC // 2):
                pool.wait_ge(s.evac, GROUPS_BEFORE_G_R + n + 1)
                par = (GROUPS_BEFORE_G_R + n) % 2
                nc.gpsimd.tensor_tensor(pair(XC, n), pair(XC, n), G[:, par, :, :], ALU.mult).then_inc(s.gh, 1)
                pool.wait_ge(s.gh, n + 1)
            pool.wait_ge(s.tpd, TPD_STRIP)
            pool.dma_start(strip_dram, MIXf[0:HEADS2, 3500:3884]).then_inc(s.strip, 16)
            pool.wait_ge(s.strip, 16)
            for h in range(HEADS2):
                rows = strip_dram[h, :]
                toeplitz = bass.AP(tensor=rows.tensor, offset=rows.offset, ap=[[1, P], [1, T]])
                pool.dma_start(MIXf[:, T * h:T * h + T], toeplitz).then_inc(s.tb, 16)

            n = 0
            for l in range(2 if not STOP else 0):
                pool.wait_ge(s.glu, l + 1)
                for tap in range(TAPS2 - POOL_TAPS, TAPS2):
                    for h in range(2):
                        opening = tap == TAPS2 - POOL_TAPS
                        for ch in (2 * h, 2 * h + 1):
                            to = CB[:, ch, :] if opening else PT[ch % 2]
                            ins = nc.gpsimd.tensor_scalar(to, HC[:, ch, tap + 2:tap + 2 + T],
                                                          vec("conv_dw_2", (l * TAPS2 + tap) * CONVC + ch), None,
                                                          ALU.mult)
                        n += 1
                        ins.then_inc(s.taps, 1)
                        pool.wait_ge(s.taps, n)
                        if not opening:
                            for ch in (2 * h, 2 * h + 1):
                                ins = nc.gpsimd.tensor_tensor(CB[:, ch, :], CB[:, ch, :], PT[ch % 2], ALU.add)
                            n += 1
                            ins.then_inc(s.taps, 1)
                            pool.wait_ge(s.taps, n)

        strip_due = []
        _c = [0] * 8
        for i, (j0, pieces) in enumerate(strips):
            _c[i % 8] += 32 * len(pieces)
            strip_due.append(_c[i % 8])

        @block.scalar
        def _(act):
            c = Counts(act, "act", turns, real)

            def done(ins):
                ins.then_inc(s.achain, 1)
                act.wait_ge(s.achain, c.next("achain"))

            def split(grp, some=slice(None)):
                for k, nk in grp.units()[some]:
                    u = c.n.get("unit", 0)
                    act.wait_ge(raw_sems[u % SLOTS], c.value("unit", SLOTS, div=SLOTS, mul=16))
                    if u >= SLOTS:
                        act.wait_ge(s.unit, c.value("unit", 1 - SLOTS))
                    nc.scalar.activation(WH[:, u % SLOTS, 0:nk, :], RAW[:, u % SLOTS, 0:nk, :], ACT.Copy)\
                        .then_inc(s.hi, 1)
                    c.add("unit")

            def evacuated():
                act.wait_ge(s.evac, c.next("evac"))

            def from_dve():
                act.wait_ge(s.dve, c.next("dve"))

            def g(n=None):
                return Gf[:, (c.n["evac"] - 1) % 2, :]

            def a_q(i):
                evacuated()
                nc.scalar.activation(SQ2[:, 0, :], QR[:, 0, :], ACT.Square).then_inc(s.sq, 1)
                act.wait_ge(s.sq, c.next("sq"))

            def rms_inverse(m):
                act.wait_ge(s.rms, c.next("rms"))
                done(nc.scalar.activation(SQ2[:, m, :], PX[:, m, :], ACT.Ln, scale=1.0 / P, bias=EPS_AP))
                nc.scalar.activation(SQ2[:, m, :], SQ2[:, m, :], ACT.Exp, scale=-0.5).then_inc(s.act, 1)
                act.wait_ge(s.act, c.next("act"))

            def a_k(i):
                evacuated()
                nc.scalar.activation(SQ2[:, 1, :], QR[:, 1, :], ACT.Square).then_inc(s.sq, 1)
                act.wait_ge(s.sq, c.next("sq"))
                rms_inverse(0)

            def a_v(i):
                evacuated()
                rms_inverse(1)

            def a_soft():
                act.wait_ge(s.scores, c.next("scores"))
                done(nc.scalar.activation(L, PX[:, 0:2, 0:384], ACT.Abs))
                done(nc.scalar.activation(L, L, ACT.Exp, scale=-1.0))
                nc.scalar.activation(L, L, ACT.Ln, bias=1.0).then_inc(s.act, 1)
                act.wait_ge(s.act, c.next("act"))

            def a_w():
                from_dve()
                nc.scalar.activation(W, T1, ACT.Exp).then_inc(s.act, 1)
                act.wait_ge(s.act, c.next("act"))

            def a_o(i):
                act.wait_ge(s.heads, c.next("heads"))
                nc.scalar.activation(hi2(YH, i), PX[:, 3, :].rearrange("p (c t) -> p c t", t=T), ACT.Copy)\
                    .then_inc(s.act, 1)
                act.wait_ge(s.act, c.next("act"))

            def post_attn(i, j):
                m, what = divmod(j, 3)
                now = 2 * i + m
                before = not (isinstance(i, int) and now == 0)
                if what == 0:
                    a_q(now)
                    if before:
                        a_soft()
                elif what == 1:
                    a_k(now)
                    if before:
                        a_w()
                else:
                    a_v(now)
                    if before:
                        a_o(now - 1)

            def tanh_half(dst):
                evacuated()
                nc.scalar.activation(dst, g().rearrange("p (c t) -> p c t", t=T), ACT.Tanh, scale=0.5)\
                    .then_inc(s.act, 1)
                act.wait_ge(s.act, c.next("act"))

            def post_gate_a(i, j, at):
                if at == 0 and j == 0:
                    a_soft()
                if at == 0 and j == 1:
                    a_w()
                if at == 0 and j == 2:
                    a_o(7)
                tanh_half(pair(MIX, at + 2 * i + j))

            def post_plain(i, j):
                evacuated()

            def split_pair(X, i, src=None, base=0):
                from_dve()
                nc.scalar.activation(hi2(X, i, base), TT[:, 0, :, :] if src is None else src, ACT.Copy)\
                    .then_inc(s.act, 1)
                act.wait_ge(s.act, c.next("act"))

            def lru_step(j):
                chunks = list(range(3 * j, min(3 * j + 3, RC)))
                if j:
                    from_dve()
                for n in chunks:
                    e, b = n % 3, n % 4
                    act.wait_ge(s.bd, n + 1)
                    nc.scalar.activation(TA[:, e, :], PX[:, b, 0:T], ACT.Tanh, scale=0.5, bias=der(D_HBA + n))
                    nc.scalar.activation(TX[:, e, :], PX[:, b, T:2 * T], ACT.Tanh, scale=0.5, bias=der(D_HBX + n))\
                        .then_inc(s.bdd, 1)
                    act.wait_ge(s.bdd, c.next("bdd"))
                for n in chunks:
                    e = n % 3
                    nc.scalar.activation(AA[:, e, :], TA[:, e, :], ACT.Exp, scale=der(D_NSP + n),
                                         bias=der(D_NSP + n))
                    last = nc.scalar.activation(TE[:, e, :], TA[:, e, :], ACT.Tanh, scale=der(D_SP + n),
                                                bias=der(D_SP + n))
                last.then_inc(s.act, 1)
                act.wait_ge(s.act, c.next("act"))
                from_dve()
                m = len(chunks)
                nc.scalar.activation(TE[:, 0:m, :], TE[:, 0:m, :], ACT.Sqrt, scale=0.25).then_inc(s.act, 1)
                act.wait_ge(s.act, c.next("act"))

            def post_gate_r(i, j):
                tanh_half(pair(RTc, j))
                lru_step(j)

            def post_g_r(i, j, at=0):
                evacuated()
                nc.scalar.activation(Tf[:, 0, :], g(), ACT.Square, scale=float(np.sqrt(GELU_C))).then_inc(s.act, 1)
                act.wait_ge(s.act, c.next("act"))
                from_dve()
                nc.scalar.activation(Tf[:, 1, :], Tf[:, 0, :], ACT.Tanh, scale=GELU_S).then_inc(s.act, 1)
                act.wait_ge(s.act, c.next("act"))
                split_pair(YH, at + 2 * i + j)

            def post_rnn_out(i, j):
                evacuated()
                from_dve()
                nc.scalar.activation(hi2(XH, 2 * i + j), pair(MIX, 2 * i + j), ACT.Copy).then_inc(s.act, 1)
                act.wait_ge(s.act, c.next("act"))

            def post_fold(n):
                evacuated()
                from_dve()
                nc.scalar.activation(two(SQP), pair(XRES, n), ACT.Square).then_inc(s.act, 1)
                act.wait_ge(s.act, c.next("act"))
                split_pair(YH, n)

            def two(ap):
                return ap.rearrange("p (c t) -> p c t", t=T)

            def preload_ln():
                nc.scalar.activation(der(D_LN), ONES[:, 0:1], ACT.Ln)

            def inverse_rms(ms, r, ss, width, eps):
                done(nc.scalar.activation(r, ss, ACT.Ln, scale=1.0 / width, bias=eps))
                nc.scalar.activation(ms, ss, ACT.Identity, scale=1.0 / width, bias=eps)
                nc.scalar.activation(r, r, ACT.Exp, scale=-0.5).then_inc(s.act, 1)
                act.wait_ge(s.act, c.next("act"))

            def norm(h):
                for q in (2 * h, 2 * h + 1):
                    from_dve()
                    nc.scalar.activation(hi2(XH, q), TT[:, q % 2, :, :], ACT.Copy).then_inc(s.act, 1)
                    act.wait_ge(s.act, c.next("act"))

            def fold():
                preload_ln()
                act.wait_ge(s.ss, c.next("ss"))
                inverse_rms(MSQ, RR, PX[:, 0, 0:T], D, EPS)

            def tables():
                act.wait_ge(s.op, OPS_MIX)
                act.dma_start(MIXf[0:NBUCK, 3072:3072 + HEADS2], A["rel_bias_2"]).then_inc(s.tab, 16)
                act.dma_start(MIXf[0:NBUCK, 3100:3484], A["c_onehot"]).then_inc(s.tab, 16)
                act.dma_start(MIXf[0:HEADS2, 3500:3884], A["c_add"]).then_inc(s.tab, 16)
                act.dma_start(RT[:, 3072:3584].rearrange("p (b d) -> p b d", b=NB),
                              A["p"][0, 0].rearrange("(b p) d -> p b d", p=P)).then_inc(s.p_in, 16)

            def p_high():
                act.wait_ge(s.tp, TP_P)
                nc.scalar.activation(hi2(YH, 0, base=DC), two(PX[:, 1, :]), ACT.Copy).then_inc(s.act, 1)
                act.wait_ge(s.act, c.next("act"))

            def post_gu(i, j, h):
                evacuated()
                first = h == 0 and isinstance(i, int) and i == 0
                if first and j == 0:
                    fold()
                    p_high()
                if j % 2 == 0:
                    from_dve()
                    nc.scalar.activation(Tf[:, 0, :], g(), ACT.Tanh, scale=0.5).then_inc(s.act, 1)
                    act.wait_ge(s.act, c.next("act"))
                else:
                    split_pair(XH, 2 * i + j // 2, TT[:, 1, :, :])

            def post_ple(i, j):
                evacuated()
                if isinstance(i, int) and i == 0 and j == 0:
                    fold()
                from_dve()
                nc.scalar.activation(Tf[:, 0, :], g(), ACT.Tanh, scale=0.5).then_inc(s.act, 1)
                act.wait_ge(s.act, c.next("act"))
                from_dve()
                nc.scalar.activation(hi2(XH, 2 * i + j), pair(XRES, 2 * i + j), ACT.Copy).then_inc(s.act, 1)
                act.wait_ge(s.act, c.next("act"))

            def post_conf(i, j):
                evacuated()
                if j in (1, 3):
                    nc.scalar.activation(Tf[:, 0, :], g(), ACT.Tanh, scale=0.5).then_inc(s.act, 1)
                    act.wait_ge(s.act, c.next("act"))
                if j in (4, 5):
                    nc.scalar.activation(Tf[:, 0, :], g(), ACT.Tanh, scale=0.5).then_inc(s.act, 1)
                    act.wait_ge(s.act, c.next("act"))

            def soft(n):
                for x in range(n):
                    from_dve()
                    for b, (lo, up) in enumerate(((0, P), (P, 3 * P))):
                        last = nc.scalar.activation(S4[:, x, lo:up], S4[:, x, lo:up], ACT.Exp,
                                                    bias=der(D_RED + 2 * x + b),
                                                    accum_out=der(D_RED + 8 + 2 * x + b))
                        last.then_inc(s.act, 1)
                        act.wait_ge(s.act, c.next("act"))

            def silu_gate():
                evacuated()
                nc.scalar.activation(Tf[:, 0, :], g(), ACT.Tanh, scale=0.5).then_inc(s.act, 1)
                act.wait_ge(s.act, c.next("act"))

            def diff_squares():
                from_dve()
                nc.scalar.activation(SQa, OA, ACT.Square).then_inc(s.sq, 1)
                act.wait_ge(s.sq, c.next("sq"))

            def diff_rms():
                preload_ln()
                act.wait_ge(s.rms, c.next("rms"))
                done(nc.scalar.activation(Tf[:, 1, :], PX[:, 3, :], ACT.Ln, scale=1.0 / P, bias=EPS2_AP))
                nc.scalar.activation(Tf[:, 1, :], Tf[:, 1, :], ACT.Exp, scale=-0.5).then_inc(s.act, 1)
                act.wait_ge(s.act, c.next("act"))

            def diff_high(m):
                from_dve()
                nc.scalar.activation(hi2(YH, m), two(OA), ACT.Copy).then_inc(s.act, 1)
                act.wait_ge(s.act, c.next("act"))

            def dil_out(i):
                from_dve()
                nc.scalar.activation(hi2(YH, i, base=4), two(OA), ACT.Copy).then_inc(s.act, 1)
                act.wait_ge(s.act, c.next("act"))

            def post_diffa(i, j):
                if j == 0:
                    evacuated()
                    dil_out(3)
                    from_dve()
                    nc.scalar.activation(SC_SQ, CA, ACT.Square).then_inc(s.sq, 1)
                    act.wait_ge(s.sq, c.next("sq"))
                elif j == 1:
                    evacuated()
                    act.wait_ge(s.sumsq, c.next("sumsq"))
                    inverse_rms(PN[:, 0:T], PN[:, T:2 * T], PX[:, 1, 0:T], 512, EPS2)
                elif j == 2:
                    evacuated()
                    soft(4)
                else:
                    silu_gate()
                    from_dve()
                    nc.scalar.activation(SC_SQ, CA, ACT.Tanh, scale=0.5).then_inc(s.act, 1)
                    act.wait_ge(s.act, c.next("act"))
                    from_dve()
                    for q in range(2):
                        nc.scalar.activation(hi2(YH, q, base=DC), CA[:, 2 * q:2 * q + 2, :], ACT.Copy)\
                            .then_inc(s.act, 1)
                        act.wait_ge(s.act, c.next("act"))

            def post_diffb(i, j):
                if j == 0:
                    evacuated()
                    diff_squares()
                elif j == 1:
                    evacuated()
                    split_pair(YH, 0, base=12)
                    diff_rms()
                elif j == 2:
                    evacuated()
                elif j == 3:
                    evacuated()
                    split_pair(YH, 1, base=12)
                    diff_high(0)
                elif j == 4:
                    evacuated()
                    soft(4)
                else:
                    silu_gate()

            def post_dil(i, j):
                before = not (isinstance(i, int) and i == 0)
                if j < 3:
                    evacuated()
                if j == 0 and before:
                    dil_out(i - 1)
                elif j == 2:
                    soft(2)
                elif j == 3:
                    silu_gate()

            def post_outa(i, j):
                if j == 0:
                    diff_squares()
                elif j == 2:
                    diff_rms()
                    diff_high(1)
                if j >= 2:
                    evacuated()

            def post_out(n):
                evacuated()
                from_dve()
                if isinstance(n, int) and n == 2:
                    nc.scalar.activation(SQ6, XRES[:, 0:6, :], ACT.Square).then_inc(s.act, 1)
                    act.wait_ge(s.act, c.next("act"))
                elif isinstance(n, int) and n == DC // 2 - 1:
                    nc.scalar.activation(two(SQP), pair(XRES, n), ACT.Square).then_inc(s.sq, 1)
                    act.wait_ge(s.sq, c.next("sq"))
                else:
                    nc.scalar.activation(two(SQP), pair(XRES, n), ACT.Square).then_inc(s.act, 1)
                    act.wait_ge(s.act, c.next("act"))

            def ln(l):
                preload_ln()
                from_dve()
                inverse_rms(MSQ, Gf[:, 0, T:2 * T], Gf[:, 0, 0:T], 1, EPS2)
                for q in range(8):
                    from_dve()
                    for e in range(2):
                        ch = 2 * q + e
                        last = nc.scalar.activation(XRES[:, ch, :], TT[:, q % 2, e, :], ACT.Identity,
                                                    bias=vec("ln_b_2", 16 * l + ch))
                    if l == 0:
                        done(last)
                        nc.scalar.activation(hi2(XH, q), pair(XRES, q), ACT.Copy).then_inc(s.act, 1)
                        act.wait_ge(s.act, c.next("act"))
                    else:
                        last.then_inc(s.final, 1)
                        act.wait_ge(s.final, c.next("final"))

            act.dma_start(MATS[:, :], A["c_mats"]).then_inc(s.mats, 16)
            half = slice(0, D // 2), slice(D // 2, D)
            for h in range(2):
                act.dma_start(F[:, 0:NB * D].rearrange("p (b d) -> p b d", b=NB)[:, :, half[h]],
                              A["x"][0].rearrange("(b p) d -> p b d", p=P)[:, :, half[h]])\
                    .then_inc((s.x_in0, s.x_in1)[h], 16)
            act.wait_ge(s.mats, 16)
            preload_ln()
            for h in range(2):
                act.wait_ge((s.x_in0, s.x_in1)[h], 16)
                for b in range(NB):
                    at = D * b + D // 2 * h
                    last = nc.scalar.activation(MIXf[:, at:at + D // 2], Fv[:, at:at + D // 2], ACT.Square,
                                                accum_out=der((D_SS, D_R)[h] + b))
            done(last)
            for b in range(NB):
                last = nc.scalar.activation(der(D_SS + b), der(D_SS + b), ACT.Identity, bias=der(D_R + b))
            done(last)
            done(nc.scalar.activation(der(D_R, NB), der(D_SS, NB), ACT.Ln, scale=1.0 / D, bias=EPS))
            nc.scalar.activation(der(D_MS, NB), der(D_SS, NB), ACT.Identity, scale=1.0 / D, bias=EPS)
            nc.scalar.activation(der(D_R, NB), der(D_R, NB), ACT.Exp, scale=-0.5).then_inc(s.act, 1)
            act.wait_ge(s.act, c.next("act"))
            c.add("ss")
            def derive():
                act.wait_ge(s.tpd, DC // 2 + 1)
                for half, src in ((D_HBA, "b_rg_a"), (D_HBX, "b_rg_x")):
                    nc.scalar.activation(der(half, RC), vec(src, 0, RC), ACT.Copy, scale=0.5)
                nc.scalar.activation(der(D_QG), vec("q_gain"), ACT.Copy, scale=QSCALE)
                for l in range(2):
                    nc.scalar.activation(der(D_HG + l), vec("diff_head_gain_2", l), ACT.Copy, scale=1.0 - LAM_INIT[l])
                done(nc.scalar.activation(der(D_SP, RC), vec("lru_lambda", 0, RC), ACT.Abs))
                done(nc.scalar.activation(der(D_SP, RC), der(D_SP, RC), ACT.Exp, scale=-1.0))
                nc.scalar.activation(der(D_SP, RC), der(D_SP, RC), ACT.Ln, bias=1.0).then_inc(s.act, 1)
                act.wait_ge(s.act, c.next("act"))
                from_dve()
                nc.scalar.activation(der(D_RED, 4), der(D_RED, 4), ACT.Exp).then_inc(s.act, 1)
                act.wait_ge(s.act, c.next("act"))

            def post(name):
                return {
                    "attn": post_attn,
                    "gate_a0": lambda i, j: post_gate_a(i, j, 0),
                    "gate_a1": lambda i, j: post_gate_a(i, j, 4),
                    "attn_out": post_plain, "x_r": post_plain, "x_r_last": post_plain,
                    "gate_r": post_gate_r, "g_r": post_g_r,
                    "g_r_last": lambda i, j: post_g_r(i, j, 10),
                    "rnn_out": post_rnn_out, "w_o": lambda i, j: post_fold(2 * i + j),
                    "gu0": lambda i, j: post_gu(i, j, 0), "gu1": lambda i, j: post_gu(i, j, 1),
                    "gu2": lambda i, j: post_gu(i, j, 2),
                    "down0": post_plain, "down1": post_plain, "down2": lambda i, j: post_fold(4 * i + j), "proj": post_plain,
                    "ple": post_ple, "conf": post_conf, "dil": post_dil, "diffa": post_diffa, "diffb": post_diffb,
                    "outa": post_outa, "outb": lambda i, j: post_out(2 * i + (j + 2)),
                }.get(name) or post(name[:-1])

            between = {"tables": tables, "ln0": lambda: ln(0), "ln1": lambda: ln(1)}
            pending, later = [], [derive]
            for ph in phases:
                if ph.name in between:
                    pending.append(between[ph.name])
                    continue
                fn, J = post(ph.name), len(ph.body)
                for j, grp in enumerate(ph.body):
                    if later:
                        split(grp)
                        for h in range(DC // UK):
                            norm(h)
                    elif ph.name == "conf1" and j == 0:
                        split(grp, slice(0, UK - 1))
                    else:
                        split(grp)
                    for job in pending:
                        job()
                    if ph.name == "conf1" and j == 0:
                        split(grp, slice(UK - 1, UK))
                    pending = [lambda fn=fn, j=j: fn(0, j)] + later
                    later = []

                def turn(i):
                    for j, grp in enumerate(ph.body):
                        split(grp)
                        fn(i - 1, J - 1) if j == 0 else fn(i, j - 1)
                c.loop(1, ph.n, turn)
                pending = [lambda fn=fn, n=ph.n, J=J: fn(n - 1, J - 1)]
            for job in pending:
                job()

        @block.vector
        def _(dve):
            c = Counts(dve, "dve", turns, real)
            V_ = nc.vector

            def done(ins):
                ins.then_inc(s.chain, 1)
                dve.wait_ge(s.chain, c.next("chain"))

            def split(grp, some=slice(None)):
                for k, nk in grp.units()[some]:
                    u = c.n.get("unit", 0)
                    dve.wait_ge(s.hi, c.value("unit", 1))
                    V_.tensor_tensor(WL[:, u % SLOTS, 0:nk, :], RAW[:, u % SLOTS, 0:nk, :],
                                     WH[:, u % SLOTS, 0:nk, :].bitcast(fp), ALU.subtract).then_inc(s.lo, 1)
                    c.add("unit")

            def from_act(m=1):
                dve.wait_ge(s.act, c.next("act", m))

            def evacuate(grp, dst=None):
                par = c.n.get("group", 0) % 2
                dve.wait_ge(s.unit, c.next("seen", grp.seen))
                out = G[:, par, :, :] if dst is None else dst
                V_.reduce_sum(out, PG[:, 2 * par:2 * par + 2, :].rearrange("p b (h t) -> p b t h", h=2), AX)\
                    .then_inc(s.evac, 1)
                c.add("group")
                dve.wait_ge(s.evac, c.value("group"))
                return Gf[:, par, :]

            def two(ap):
                return ap.rearrange("p (c t) -> p c t", t=T)

            def low(X, i, src, base=0):
                from_act()
                V_.tensor_tensor(lo2(X, i, base), src, hi2(X, i, base).bitcast(fp), ALU.subtract).then_inc(s.op, 1)
                dve.wait_ge(s.op, c.next("op"))

            def inverse_root(ms, r, tmp, told=None):
                from_act()
                if told:
                    told()
                done(V_.scalar_tensor_tensor(tmp, ms, -0.5, r, ALU.mult, ALU.mult))
                done(V_.tensor_tensor(tmp, tmp, r, ALU.mult))
                done(V_.scalar_tensor_tensor(r, tmp, 1.5, r, ALU.add, ALU.mult))

            def a_q(grp, i):
                evacuate(grp, two(QR[:, 0, :]))

            def a_k(grp, i):
                evacuate(grp, two(QR[:, 1, :]))
                from_act()
                done(V_.scalar_tensor_tensor(QR[:, 0, :], QR[:, 0, :], der(D_QG), SQ2[:, 0, :], ALU.mult, ALU.mult))

            def a_v(grp, i):
                evacuate(grp)
                from_act()
                V_.scalar_tensor_tensor(QR[:, 1, :], QR[:, 1, :], vec("k_gain"), SQ2[:, 1, :], ALU.mult, ALU.mult)\
                    .then_inc(s.ready, 1)
                dve.wait_ge(s.ready, c.next("ready"))

            def a_soft():
                V_.tensor_copy(V, PX[:, 2, :].rearrange("p (a n) -> p a n", a=4))
                from_act()
                z = PX[:, 0:2, 0:384]
                done(V_.scalar_tensor_tensor(SP, z, 0.0, L, ALU.max, ALU.add))
                V_.tensor_tensor(T1, z, SP, ALU.subtract)
                V_.tensor_tensor(SP, SP, KEEP.unsqueeze(1).broadcast_to([P, 2, 384]), ALU.mult).then_inc(s.ready, 1)
                dve.wait_ge(s.ready, c.next("ready"))

            def a_w():
                dve.wait_ge(s.later, c.next("later"))
                V_.tensor_tensor(T1, T1, PX[:, 2:4, 0:384], ALU.subtract).then_inc(s.dve, 1)
                dve.wait_ge(s.dve, c.next("dve"))
                from_act()
                V_.tensor_tensor(W, W, KEEP.unsqueeze(1).broadcast_to([P, 2, 384]), ALU.mult).then_inc(s.ready, 1)
                dve.wait_ge(s.ready, c.next("ready"))

            def a_o(i):
                dve.wait_ge(s.heads, c.next("heads"))
                low(YH, i, two(PX[:, 3, :]))

            def post_attn(grp, i, j):
                m, what = divmod(j, 3)
                now = 2 * i + m
                before = not (isinstance(i, int) and now == 0)
                if what == 0:
                    if before:
                        dve.wait_ge(s.scores, c.next("scores"))
                    a_q(grp, now)
                    if before:
                        a_soft()
                elif what == 1:
                    a_k(grp, now)
                    if before:
                        a_w()
                else:
                    a_v(grp, now)
                    if before:
                        a_o(now - 1)

            def post_gate_a(grp, i, j, at):
                if at == 0 and j == 0:
                    dve.wait_ge(s.scores, c.next("scores"))
                    evacuate(grp)
                    a_soft()
                elif at == 0 and j == 1:
                    evacuate(grp)
                    a_w()
                elif at == 0 and j == 2:
                    evacuate(grp)
                    a_o(7)
                else:
                    evacuate(grp)
                from_act()

            def post_attn_out(grp, i, j):
                x = evacuate(grp)
                m = pair(MIX, 2 * i + j)
                V_.scalar_tensor_tensor(m, m, 1.0, two(x), ALU.add, ALU.mult)

            def post_x_r(grp, i, j, at=0):
                x = evacuate(grp)
                rows = [4 * i + 2 * j + e + at for e in range(2)]
                src = [x[:, e * T:e * T + T] for e in range(2)]
                dst = [XC[:, ch, :] if isinstance(ch, int) else XC[:, bass.ds(ch, 1), :].squeeze(1) for ch in rows]
                for k in range(TAPS - 1, -1, -1):
                    d = TAPS - 1 - k
                    for e in range(2):
                        w = vec("conv_w", k * RC + rows[e])
                        if d == 0:
                            ins = V_.tensor_scalar(dst[e], src[e], w, vec("conv_b", rows[e]), ALU.mult, ALU.add)
                        else:
                            ins = V_.scalar_tensor_tensor(dst[e][:, d:T], src[e][:, 0:T - d], w, dst[e][:, d:T],
                                                          ALU.mult, ALU.add)
                    if k:
                        done(ins)
                ins.then_inc(s.xc, 1)
                dve.wait_ge(s.xc, c.next("xc"))

            def lru_step(j):
                first, m = 3 * j, min(3, RC - 3 * j)
                dve.wait_ge(s.bd, first + m)
                for ch in range(max(0, first - 3), first):
                    if last_user[ch] >= first:
                        ins = V_.tensor_copy(XC[:, ch, :], TE[:, ch % 3, :])
                if j:
                    ins.then_inc(s.dve, 1)
                    dve.wait_ge(s.dve, c.next("dve"))
                a, t, x, e = AA[:, 0:m, :], TA[:, 0:m, :], TX[:, 0:m, :], TE[:, 0:m, :]
                from_act()
                done(V_.tensor_tensor(t, a, a, ALU.mult))
                V_.scalar_tensor_tensor(e, t, 1.0, e, ALU.add, ALU.mult).then_inc(s.dve, 1)
                dve.wait_ge(s.dve, c.next("dve"))
                done(V_.scalar_tensor_tensor(x, x, 1.0, XC[:, first:first + m, :], ALU.add, ALU.mult))
                from_act()
                done(V_.tensor_tensor(x, x, e, ALU.mult))
                for q in range(m):
                    ch = first + q
                    to = XC[:, ch, :] if last_user[ch] < first + m else TE[:, q, :]
                    ins = V_.tensor_tensor_scan(to, AA[:, q, :], TX[:, q, :], 0.0, ALU.mult, ALU.add)
                done(ins)

            def post_gate_r(grp, i, j):
                evacuate(grp)
                from_act()
                lru_step(j)

            def post_g_r(grp, i, j, at=0):
                x = evacuate(grp)
                n = at + 2 * i + j
                from_act()
                V_.scalar_tensor_tensor(Tf[:, 0, :], Tf[:, 0, :], 1.0, x, ALU.add, ALU.mult).then_inc(s.dve, 1)
                dve.wait_ge(s.dve, c.next("dve"))
                from_act()
                dve.wait_ge(s.gh, c.next("gh"))
                V_.scalar_tensor_tensor(TT[:, 0, :, :], TT[:, 1, :, :], 1.0, pair(XC, n), ALU.add, ALU.mult)\
                    .then_inc(s.dve, 1)
                dve.wait_ge(s.dve, c.next("dve"))
                low(YH, n, TT[:, 0, :, :])

            def post_rnn_out(grp, i, j):
                x = evacuate(grp)
                n = 2 * i + j
                r, m = pair(RTc, n), pair(MIX, n)
                done(V_.scalar_tensor_tensor(r, r, 1.0, two(x), ALU.add, ALU.mult))
                V_.scalar_tensor_tensor(m, r, 0.5, m, ALU.mult, ALU.add).then_inc(s.dve, 1)
                dve.wait_ge(s.dve, c.next("dve"))
                low(XH, n, m)

            def accumulate(n, src):
                if isinstance(n, int) and n == 0:
                    done(V_.tensor_copy(two(ACC), src))
                elif isinstance(n, int) and n == DC // 2 - 1:
                    V_.tensor_tensor(two(ACC), two(ACC), src, ALU.add).then_inc(s.ready, 1)
                    dve.wait_ge(s.ready, c.next("ready"))
                else:
                    done(V_.tensor_tensor(two(ACC), two(ACC), src, ALU.add))

            def residual(grp, i, j):
                x = evacuate(grp)
                m = pair(XRES, 2 * i + j)
                V_.tensor_tensor(m, two(x), m, ALU.add)

            def post_fold(grp, n, scale, gain):
                x = evacuate(grp)
                m = pair(XRES, n)
                V_.scalar_tensor_tensor(m, two(x), scale, m, ALU.mult, ALU.add).then_inc(s.dve, 1)
                dve.wait_ge(s.dve, c.next("dve"))
                V_.tensor_tensor(TT[:, 0, :, :], m, vec(gain, 2 * n, 2).unsqueeze(2).broadcast_to([P, 2, T]),
                                 ALU.mult).then_inc(s.dve, 1)
                dve.wait_ge(s.dve, c.next("dve"))
                from_act()
                accumulate(n, two(SQP))
                low(YH, n, TT[:, 0, :, :])

            def fold():
                inverse_root(MSQ, RR, NW)

            def over_rms(x):
                V_.tensor_tensor(two(x), two(x), RR.unsqueeze(1).broadcast_to([P, 2, T]), ALU.mult).then_inc(s.dve, 1)
                dve.wait_ge(s.dve, c.next("dve"))

            def norm(h):
                if h == 0:
                    dve.wait_ge(s.ss, c.next("ss"))
                    done(V_.tensor_copy(Gf[:, 0, T:2 * T], PX[:, 0, 0:T]))
                for q in (2 * h, 2 * h + 1):
                    for e in range(2):
                        ins = V_.scalar_tensor_tensor(TT[:, q % 2, e, :], XRES[:, 2 * q + e, :],
                                                      vec("g_mix", 2 * q + e), Gf[:, 0, T:2 * T], ALU.mult, ALU.mult)
                    ins.then_inc(s.dve, 1)
                    dve.wait_ge(s.dve, c.next("dve"))
                    if q % 2:
                        low(XH, q - 1, TT[:, 0, :, :])
                low(XH, 2 * h + 1, TT[:, 1, :, :])

            def bias_strip():
                dve.wait_ge(s.tab, 48)
                dve.wait_ge(s.tp, TP_STRIP)
                V_.tensor_tensor(MIXf[0:HEADS2, 3500:3884], PX[0:HEADS2, 2, 0:384], MIXf[0:HEADS2, 3500:3884],
                                 ALU.add).then_inc(s.tpd, 1)
                dve.wait_ge(s.tpd, c.next("tpd"))

            def bias_tiles(j):
                for h in (2 * j, 2 * j + 1):
                    dve.wait_ge(s.flip, h + 1)
                    V_.tensor_copy(AB[:, 2 * h:2 * h + 2, :], two(PX[:, 2 + h % 2, :])).then_inc(s.flipped, 1)
                    dve.wait_ge(s.flipped, c.next("flipped"))

            def post_gu(grp, i, j, h):
                x = evacuate(grp)
                first = isinstance(i, int) and i == 0
                if h == 0 and first and j == 0:
                    fold()
                    dve.wait_ge(s.tp, TP_P)
                    low(YH, 0, two(PX[:, 1, :]), base=DC)
                if j % 2 == 0:
                    over_rms(x)
                    from_act()
                    done(V_.scalar_tensor_tensor(Tf[:, 1, :], Tf[:, 0, :], 1.0, x, ALU.add, ALU.mult))
                else:
                    done(V_.scalar_tensor_tensor(Tf[:, 1, :], Tf[:, 1, :], 0.5, x, ALU.mult, ALU.mult))
                    over_rms(Tf[:, 1, :])
                    low(XH, 2 * i + j // 2, TT[:, 1, :, :])
                if h == 0 and first and j == 1:
                    bias_strip()
                if h == 1 and first and j < 3:
                    bias_tiles(j)

            def post_proj(grp, i, j):
                evacuate(grp, pair(MIX, j))

            def post_ple(grp, i, j):
                x = evacuate(grp)
                n = 2 * i + j
                if isinstance(i, int) and i == 0 and j == 0:
                    fold()
                over_rms(x)
                from_act()
                done(V_.scalar_tensor_tensor(TT[:, 1, :, :], TT[:, 0, :, :], 1.0, pair(MIX, n), ALU.add, ALU.mult))
                m = pair(XRES, n)
                V_.scalar_tensor_tensor(m, TT[:, 1, :, :], 0.5, m, ALU.mult, ALU.add).then_inc(s.dve, 1)
                dve.wait_ge(s.dve, c.next("dve"))
                low(XH, n, m)

            def post_conf(grp, i, j, l):
                h = 2 * (j // 2)
                if j == 0:
                    done(V_.memset(HC[:, :, 0:32], 0.0))
                if j in (0, 2):
                    evacuate(grp, HC[:, h:h + 2, 32:32 + T])
                elif j in (1, 3):
                    evacuate(grp)
                    from_act()
                    done(V_.tensor_scalar(Tf[:, 1, :], Tf[:, 0, :], 0.5, 0.5, ALU.mult, ALU.add))
                    x = HC[:, h:h + 2, 32:32 + T]
                    V_.tensor_tensor(x, x, TT[:, 1, :, :], ALU.mult).then_inc(s.glu if j == 3 else s.chain, 1)
                    dve.wait_ge(s.glu if j == 3 else s.chain, c.next("glu" if j == 3 else "chain"))
                else:
                    x = evacuate(grp)
                    from_act()
                    V_.scalar_tensor_tensor(SC[:, 2 * (j - 4):2 * (j - 4) + 2, :], TT[:, 0, :, :], 1.0, two(x),
                                            ALU.add, ALU.mult)

            def taps(k, m, l):
                for t in range(m):
                    tap = k + t
                    for ch in range(CONVC):
                        row = (l * TAPS2) * CONVC + ch
                        at = tap * CONVC + row
                        off = tap + 2
                        src = HC[:, ch, off:off + T] if isinstance(tap, int) else \
                            HC[:, ch, bass.ds(off, T)]
                        if isinstance(tap, int) and tap == 0:
                            ins = V_.tensor_scalar(CA[:, ch, :], src, vec("conv_dw_2", at),
                                                   vec("conv_b_2", CONVC * l + ch), ALU.mult, ALU.add)
                        else:
                            ins = V_.scalar_tensor_tensor(CA[:, ch, :], src, vec("conv_dw_2", at), CA[:, ch, :],
                                                          ALU.mult, ALU.add)
                    done(ins)
                    if isinstance(tap, int) and tap == TAPS2 - POOL_TAPS - 1:
                        dve.wait_ge(s.taps, (4 * POOL_TAPS - 2) * (l + 1))
                        V_.tensor_tensor(CA, CA, CB, ALU.add).then_inc(s.conv, 1)
                        dve.wait_ge(s.conv, c.next("conv"))

            def scores(n, scale, head):
                for x in range(n):
                    h = head(x)
                    ab = AB[:, h, :] if isinstance(h, int) else AB[:, bass.ds(h, 1), :].squeeze(1)
                    V_.scalar_tensor_tensor(S4[:, x, 0:P], PX[:, x, 0:P], scale, ab[:, P:2 * P], ALU.mult, ALU.add)
                    done(V_.scalar_tensor_tensor(S4[:, x, P:3 * P], PX[:, x, P:3 * P], scale, ab, ALU.mult, ALU.add))
                    V_.tensor_reduce(der(D_RED + 2 * x), S4[:, x, 0:P], AX, ALU.max, negate=True)
                    V_.tensor_reduce(der(D_RED + 2 * x + 1), S4[:, x, P:3 * P], AX, ALU.max, negate=True)\
                        .then_inc(s.dve, 1)
                    dve.wait_ge(s.dve, c.next("dve"))

            def inverse_sums(n):
                from_act(2 * n)
                done(V_.reciprocal(der(D_RED + 16, 2 * n), der(D_RED + 8, 2 * n)))

            def transposed():
                dve.wait_ge(s.turned, c.next("turned"))
                V_.tensor_copy(V, PX[:, 2, :].rearrange("p (a n) -> p a n", a=4))
                V_.tensor_copy(PTS, PX[:, 0:2, 0:384]).then_inc(s.ready, 1)
                dve.wait_ge(s.ready, c.next("ready"))

            def gate(grp, tell=False):
                x = evacuate(grp)
                from_act()
                ins = V_.scalar_tensor_tensor(SG, Tf[:, 0, :], 1.0, x, ALU.add, ALU.mult)
                if tell:
                    ins.then_inc(s.dve, 1)
                    dve.wait_ge(s.dve, c.next("dve"))
                transposed()

            def gated():
                dve.wait_ge(s.heads2, c.next("heads2"))
                V_.scalar_tensor_tensor(OA, PX[:, 3, :], 0.5, SG, ALU.mult, ALU.mult).then_inc(s.dve, 1)
                dve.wait_ge(s.dve, c.next("dve"))

            def diff_gated():
                dve.wait_ge(s.heads2, c.next("heads2"))
                V_.tensor_copy(OA, PX[:, 3, :]).then_inc(s.dve, 1)
                dve.wait_ge(s.dve, c.next("dve"))

            def diff_out(m, l):
                done(V_.scalar_tensor_tensor(OA, OA, der(D_HG + l), Tf[:, 1, :], ALU.mult, ALU.mult))
                V_.scalar_tensor_tensor(OA, OA, 0.5, SG, ALU.mult, ALU.mult).then_inc(s.dve, 1)
                dve.wait_ge(s.dve, c.next("dve"))
                low(YH, m, two(OA))

            def diff_softmax(m, l):
                dve.wait_ge(s.scores2, c.next("scores2"))
                scores(4, ASCALE, lambda x: 2 * m + x // 2)
                inverse_sums(4)
                for h in range(2):
                    done(V_.tensor_scalar(der(D_RED + 16 + 4 * h + 2, 2), der(D_RED + 16 + 4 * h + 2, 2),
                                          der(D_NLAM + l), None, ALU.mult))
                    for b, (lo, up) in enumerate(((0, P), (P, 3 * P))):
                        x = S4[:, 2 * h, lo:up]
                        done(V_.tensor_scalar(x, x, der(D_RED + 16 + 4 * h + b), None, ALU.mult))
                        ins = V_.scalar_tensor_tensor(x, S4[:, 2 * h + 1, lo:up],
                                                      der(D_RED + 16 + 4 * h + 2 + b), x, ALU.mult, ALU.add)
                ins.then_inc(s.ready, 1)
                dve.wait_ge(s.ready, c.next("ready"))

            def post_dil(grp, i, j, l):
                if j == 0:
                    evacuate(grp, two(QR[:, 0, :]))
                    if not (isinstance(i, int) and i == 0):
                        gated()
                        low(YH, i - 1, two(OA), base=4)
                elif j == 1:
                    evacuate(grp, two(QR[:, 1, :]))
                elif j == 2:
                    evacuate(grp)
                    dve.wait_ge(s.scores2, c.next("scores2"))
                    scores(2, QSCALE, lambda x: 2 * i + (4 + x))
                    inverse_sums(2)
                    for h in range(2):
                        for b, (lo, up) in enumerate(((0, P), (P, 3 * P))):
                            x = S4[:, h, lo:up]
                            ins = V_.tensor_scalar(x, x, der(D_RED + 16 + 2 * h + b), None, ALU.mult)
                    ins.then_inc(s.ready, 1)
                    dve.wait_ge(s.ready, c.next("ready"))
                else:
                    gate(grp)
                at, m = ((0, 1), (1, 2), (3, 0), (3, 1))[j]
                taps(4 * i + at, m, l)

            def sums_read():
                V_.tensor_copy(NW[:, 0:1], PN[:, 0:1]).then_inc(s.ready, 1)
                dve.wait_ge(s.ready, c.next("ready"))

            def post_diffa(grp, i, j, l):
                if j == 0:
                    evacuate(grp, two(QR[:, 0, :]))
                    gated()
                    low(YH, 3, two(OA), base=4)
                    dve.wait_ge(s.sum, c.next("sum"))
                    done(V_.tensor_scalar(PN[:, T:2 * T], PX[:, 0, 0:T], -1.0 / 512, None, ALU.mult))
                    V_.tensor_tensor(CA, CA, PN[:, T:2 * T].unsqueeze(1).broadcast_to([P, CONVC, T]), ALU.add)\
                        .then_inc(s.dve, 1)
                    dve.wait_ge(s.dve, c.next("dve"))
                elif j == 1:
                    evacuate(grp, two(QR[:, 1, :]))
                    inverse_root(PN[:, 0:T], PN[:, T:2 * T], NW, sums_read)
                    for ch in range(CONVC):
                        ins = V_.scalar_tensor_tensor(CA[:, ch, :], CA[:, ch, :], vec("conv_ln_g_2", CONVC * l + ch),
                                                      PN[:, T:2 * T], ALU.mult, ALU.mult)
                    done(ins)
                    for ch in range(CONVC):
                        ins = V_.tensor_scalar(CA[:, ch, :], CA[:, ch, :], vec("conv_ln_b_2", CONVC * l + ch), None,
                                               ALU.add)
                    done(ins)
                elif j == 2:
                    evacuate(grp)
                    diff_softmax(0, l)
                else:
                    gate(grp, tell=True)
                    from_act()
                    done(V_.scalar_tensor_tensor(CA, SC_SQ, 1.0, CA, ALU.add, ALU.mult))
                    V_.tensor_scalar(CA, CA, 0.5, None, ALU.mult).then_inc(s.dve, 1)
                    dve.wait_ge(s.dve, c.next("dve"))
                    for q in range(2):
                        low(YH, q, CA[:, 2 * q:2 * q + 2, :], base=DC)

            def post_pw(grp, j):
                x = evacuate(grp)
                V_.scalar_tensor_tensor(TT[:, 0, :, :], two(x), 0.5, SC[:, 2 * j:2 * j + 2, :], ALU.mult, ALU.mult)\
                    .then_inc(s.dve, 1)
                dve.wait_ge(s.dve, c.next("dve"))
                low(YH, j, TT[:, 0, :, :], base=12)

            def post_diffb(grp, i, j, l):
                if j == 0:
                    evacuate(grp, two(QR[:, 0, :]))
                    diff_gated()
                elif j in (1, 3):
                    post_pw(grp, j // 2)
                    if j == 1:
                        c.add("act")
                    else:
                        diff_out(0, l)
                elif j == 2:
                    evacuate(grp, two(QR[:, 1, :]))
                elif j == 4:
                    evacuate(grp)
                    diff_softmax(1, l)
                else:
                    gate(grp)

            def post_outa(grp, j, l):
                if j == 0:
                    diff_gated()
                elif j == 2:
                    from_act()
                    diff_out(1, l)
                if j >= 2:
                    x = evacuate(grp)
                    m = pair(XRES, j - 2)
                    done(V_.scalar_tensor_tensor(m, m, ALPHA, two(x), ALU.mult, ALU.add))
                    if j == 2:
                        V_.tensor_copy(two(ACC), m).then_inc(s.ready, 1)
                        dve.wait_ge(s.ready, c.next("ready"))

            def post_out(grp, n):
                x = evacuate(grp)
                m = pair(XRES, n)
                done(V_.scalar_tensor_tensor(m, m, ALPHA, two(x), ALU.mult, ALU.add))
                if isinstance(n, int) and n == 2:
                    dve.wait_ge(s.sum, c.next("sum"))
                    done(V_.tensor_scalar(PILOT, PX[:, 0, 0:T], -1.0 / (2 * P), None, ALU.mult))
                    V_.tensor_tensor(XRES[:, 0:6, :], XRES[:, 0:6, :],
                                     PILOT.unsqueeze(1).broadcast_to([P, 6, T]), ALU.add).then_inc(s.dve, 1)
                    dve.wait_ge(s.dve, c.next("dve"))
                    done(V_.tensor_tensor(two(ACC), pair(XRES, 0), pair(XRES, 1), ALU.add))
                    done(V_.tensor_tensor(two(ACC), two(ACC), m, ALU.add))
                    from_act()
                    done(V_.tensor_tensor(two(ACC2), pair(SQ6, 0), pair(SQ6, 1), ALU.add))
                    done(V_.tensor_tensor(two(ACC2), two(ACC2), pair(SQ6, 2), ALU.add))
                elif isinstance(n, int) and n == DC // 2 - 1:
                    V_.tensor_tensor(m, m, PILOT.unsqueeze(1).broadcast_to([P, 2, T]), ALU.add).then_inc(s.dve, 1)
                    dve.wait_ge(s.dve, c.next("dve"))
                    V_.tensor_copy(NW[:, 0:1], PILOT[:, 0:1]).then_inc(s.ready, 1)
                    dve.wait_ge(s.ready, c.next("ready"))
                else:
                    V_.tensor_tensor(m, m, PILOT.unsqueeze(1).broadcast_to([P, 2, T]), ALU.add).then_inc(s.dve, 1)
                    dve.wait_ge(s.dve, c.next("dve"))
                    done(V_.tensor_tensor(two(ACC), two(ACC), m, ALU.add))
                    from_act()
                    V_.tensor_tensor(two(ACC2), two(ACC2), two(SQP), ALU.add).then_inc(s.acc, 1)
                    dve.wait_ge(s.acc, c.next("acc"))

            def ln(l):
                v, r, mean, tmp = Gf[:, 0, 0:T], Gf[:, 0, T:2 * T], Gf[:, 1, 0:T], Gf[:, 1, T:2 * T]
                dve.wait_ge(s.sum, c.next("sum"))
                done(V_.tensor_scalar(mean, PX[:, 0, 0:T], -1.0 / D, None, ALU.mult))
                done(V_.tensor_tensor(tmp, mean, mean, ALU.mult))
                V_.scalar_tensor_tensor(v, PX[:, 1, 0:T], 1.0 / D, tmp, ALU.mult, ALU.subtract).then_inc(s.dve, 1)
                dve.wait_ge(s.dve, c.next("dve"))

                def centre(q):
                    m = pair(XRES, q)
                    done(V_.tensor_tensor(m, m, mean.unsqueeze(1).broadcast_to([P, 2, T]), ALU.add))
                EARLY = 4
                for q in range(EARLY):
                    centre(q)
                inverse_root(MSQ, r, tmp)
                for q in range(DC // 2):
                    if q >= EARLY:
                        centre(q)
                    if q >= 2 and l == 1:
                        dve.wait_ge(s.final, q - 1)
                    for e in range(2):
                        ins = V_.scalar_tensor_tensor(TT[:, q % 2, e, :], XRES[:, 2 * q + e, :],
                                                      vec("ln_g_2", DC * l + 2 * q + e), r, ALU.mult, ALU.mult)
                    ins.then_inc(s.dve, 1)
                    dve.wait_ge(s.dve, c.next("dve"))
                    if q and l == 0:
                        low(XH, q - 1, pair(XRES, q - 1))
                if l == 0:
                    low(XH, 7, pair(XRES, 7))

            for q in range(DC // 2):
                if q == 6:
                    inverse_root(der(D_MS, NB), der(D_R, NB), der(D_SS, NB))
                    for b in range(NB):
                        ins = V_.tensor_scalar(Gf[:, 1, P * b:P * b + P], IDENT, der(D_R + b), None, ALU.mult)
                    ins.then_inc(s.ready, 1)
                    dve.wait_ge(s.ready, c.next("ready"))
                dve.wait_ge(s.tp, q + 1)
                V_.tensor_copy(pair(XRES, q), two(PG[:, q % 4, :])).then_inc(s.tpd, 1)
                dve.wait_ge(s.tpd, c.next("tpd"))
            done(V_.tensor_copy(VEC[:, 0:DC], PX[:, 2, 0:DC]))
            def derive():
                dve.wait_ge(s.tp, DC // 2 + 1)
                V_.tensor_copy(VEC[:, 0:512], PX[:, 2, :])
                V_.tensor_copy(VEC[:, 512:VEC_N], PX[:, 3, 0:VEC_N - 512]).then_inc(s.tpd, 1)
                dve.wait_ge(s.tpd, c.next("tpd"))
                from_act()
                done(V_.tensor_scalar(Tf[:, 0, 0:RC], vec("lru_lambda", 0, RC), 0.0, None, ALU.min))
                done(V_.tensor_tensor(der(D_SP, RC), der(D_SP, RC), Tf[:, 0, 0:RC], ALU.subtract))
                done(V_.tensor_scalar(der(D_SP, RC), der(D_SP, RC), LRU_HALF_C, None, ALU.mult))
                V_.tensor_scalar(der(D_NSP, RC), der(D_SP, RC), -1.0, None, ALU.mult)
                dve.wait_ge(s.lam, 16)
                lam = Fv[:, NB * D:NB * D + 512].rearrange("p (g two d) -> p g two d", two=2, d=64)
                done(V_.tensor_tensor(Tf[:, 1, 0:256].rearrange("p (g d) -> p g d", d=64), lam[:, :, 0, :],
                                      lam[:, :, 1, :], ALU.mult))
                V_.reduce_sum(der(D_RED, 4), Tf[:, 1, 0:256].rearrange("p (g d) -> p g d", d=64), AX).then_inc(s.dve, 1)
                dve.wait_ge(s.dve, c.next("dve"))
                from_act()
                for l in range(2):
                    done(V_.tensor_tensor(der(D_NLAM + l), der(D_RED + 2 * l + 1), der(D_RED + 2 * l), ALU.subtract))
                    done(V_.tensor_scalar(der(D_NLAM + l), der(D_NLAM + l), -LAM_INIT[l], None, ALU.add))

            def post(name):
                return {
                    "attn": post_attn,
                    "gate_a0": lambda g_, i, j: post_gate_a(g_, i, j, 0),
                    "gate_a1": lambda g_, i, j: post_gate_a(g_, i, j, 4),
                    "attn_out": post_attn_out, "x_r": post_x_r,
                    "x_r_last": lambda g_, i, j: post_x_r(g_, i, j, 20),
                    "gate_r": post_gate_r, "g_r": post_g_r,
                    "g_r_last": lambda g_, i, j: post_g_r(g_, i, j, 10),
                    "rnn_out": post_rnn_out, "w_o": lambda g_, i, j: post_fold(g_, 2 * i + j, 0.5, "g_ffn"),
                    "gu0": lambda g_, i, j: post_gu(g_, i, j, 0), "gu1": lambda g_, i, j: post_gu(g_, i, j, 1),
                    "gu2": lambda g_, i, j: post_gu(g_, i, j, 2),
                    "down0": residual, "down1": residual,
                    "down2": lambda g_, i, j: post_fold(g_, 4 * i + j, 1.0, "g_ple"),
                    "proj": post_proj, "ple": post_ple,
                    "conf0": lambda g_, i, j: post_conf(g_, i, j, 0), "conf1": lambda g_, i, j: post_conf(g_, i, j, 1),
                    "dil0": lambda g_, i, j: post_dil(g_, i, j, 0), "dil1": lambda g_, i, j: post_dil(g_, i, j, 1),
                    "diffa0": lambda g_, i, j: post_diffa(g_, i, j, 0),
                    "diffa1": lambda g_, i, j: post_diffa(g_, i, j, 1),
                    "diffb0": lambda g_, i, j: post_diffb(g_, i, j, 0),
                    "diffb1": lambda g_, i, j: post_diffb(g_, i, j, 1),
                    "outa0": lambda g_, i, j: post_outa(g_, j, 0), "outa1": lambda g_, i, j: post_outa(g_, j, 1),
                    "outb0": lambda g_, i, j: post_out(g_, 2 * i + (j + 2)),
                    "outb1": lambda g_, i, j: post_out(g_, 2 * i + (j + 2)),
                }[name]

            between = {"tables": lambda: None, "ln0": lambda: ln(0), "ln1": lambda: ln(1)}
            pending, later = [], [derive]
            for ph in phases:
                if ph.name in between:
                    pending.append(between[ph.name])
                    continue
                fn, J, B = post(ph.name), len(ph.body), ph.body
                for j, grp in enumerate(B):
                    if later:
                        for h in range(DC // UK):
                            norm(h)
                        c.add("unit", SLOTS)
                        dve.wait_ge(s.lo, SLOTS)
                    elif ph.name == "conf1" and j == 0:
                        split(grp, slice(0, UK - 1))
                    else:
                        split(grp)
                    for job in pending:
                        job()
                    if ph.name == "conf1" and j == 0:
                        split(grp, slice(UK - 1, UK))
                    pending = [lambda fn=fn, grp=grp, j=j: fn(grp, 0, j)] + later
                    later = []

                def turn(i):
                    for j, grp in enumerate(B):
                        split(grp)
                        fn(B[J - 1], i - 1, J - 1) if j == 0 else fn(B[j - 1], i, j - 1)
                c.loop(1, ph.n, turn)
                pending = [lambda fn=fn, B=B, n=ph.n, J=J: fn(B[J - 1], n - 1, J - 1)]
            for job in pending:
                job()
            for q in range(DC // 2):
                dve.wait_ge(s.tp, TP_OUT + q + 1)
                V_.tensor_copy(OUTV[:, :, COLS * q:COLS * q + COLS], PG[:, q % 4, :].rearrange(
                    "p (b n) -> p b n", b=NB)).then_inc(s.tpd, 1)
                dve.wait_ge(s.tpd, c.next("tpd"))

        @block.tensor
        def _(pe):
            c = Counts(pe, "pe", turns, real)
            mm = nc.tensor.matmul

            def group(grp, fresh=(), mid=None):
                par = (c.n.get("group", 0) + grp.ahead) % 2
                if grp.opens and c.n.get("group", 0) >= 2:
                    pe.wait_ge(s.evac, c.value("group", grp.ahead - 1))
                units = grp.units()
                for n, (k0, nk) in enumerate(units):
                    slot = c.n.get("unit", 0) % SLOTS
                    pe.wait_ge(s.lo, c.value("unit", 1))
                    if n < len(fresh) and fresh[n]:
                        pe.wait_ge(s.op, c.next("op", fresh[n]))
                    for kk in range(nk):
                        x = grp.X[:, grp.base + k0 + kk, :]
                        for j in range(2):
                            b = 2 * par + j
                            cs = slice(P * j, P * j + P)
                            mm(PG[:, b, :], WH[:, slot, kk, cs], x, start=grp.opens and n == 0 and kk == 0,
                               stop=False)
                            last = mm(PG[:, b, T:2 * T], WL[:, slot, kk, cs], x[:, 0:T], start=False,
                                      stop=grp.closes and n == len(units) - 1 and kk == nk - 1)
                    last.then_inc(s.unit, 1)
                    c.add("unit")
                    if mid and n in mid:
                        mid[n]()
                if grp.closes:
                    c.add("group")

            def ready():
                pe.wait_ge(s.ready, c.next("ready"))

            def squares_in(m=1):
                pe.wait_ge(s.sq, c.next("sq", m))

            def sum_features(bank, src, first, last):
                return mm(PX[:, bank, 0:src.shape[-1]], ONES, src, start=first, stop=last)

            def v_transposes(par):
                for h in range(2):
                    for b in range(NB):
                        at = P * (2 * h + b)
                        last = nc.tensor.transpose(PX[:, 2, at:at + P], G[:, par, h, P * b:P * b + P], IDENT)
                return last

            def z_attn():
                ready()
                for h in range(2):
                    o = T * h
                    mm(PX[:, h, 0:T], QR[:, 1, o:o + P], QR[:, 0, o:o + T], start=True, stop=True)
                    mm(PX[:, h, T:T + P], QR[:, 1, o + P:o + T], QR[:, 0, o + P:o + T], start=True, stop=True)
                v_transposes(c.n["group"] % 2).then_inc(s.scores, 1)

            def e_attn():
                ready()
                for h in range(2):
                    mm(PX[:, 2 + h, T:T + P], AFTER, SP[:, h, T:T + P], start=True, stop=True)
                    mm(PX[:, 2 + h, 0:T], AFTER, SP[:, h, 0:T], start=True, stop=False)
                    last = mm(PX[:, 2 + h, P:T], ONES, SP[:, h, T:T + P], start=False, stop=True)
                last.then_inc(s.later, 1)

            def heads_out(tell):
                ready()
                for h in range(2):
                    o = T * h
                    mm(PX[:, 3, o:o + T], V[:, 2 * h, :], W[:, h, 0:T], start=True, stop=False)
                    last = mm(PX[:, 3, o + P:o + T], V[:, 2 * h + 1, :], W[:, h, T:T + P], start=False, stop=True)
                last.then_inc(tell, 1)

            def vectors():
                pe.wait_ge(s.vecs, 16 * VEC_DMAS)
                for t in range(VEC_TILES):
                    m = min(P, VEC_N - P * t)
                    last = nc.tensor.transpose(PX[:, 2 + t // 4, P * (t % 4):P * (t % 4) + m],
                                               RT[0:m, P * t:P * t + P], IDENT[0:m, 0:m])
                last.then_inc(s.tp, 1)

            def after_attn(i, j):
                if isinstance(i, int) and i == 0 and j == 0:
                    vectors()
                m, what = divmod(j, 3)
                before = not (isinstance(i, int) and i == 0 and m == 0)
                if what == 0:
                    if before:
                        z_attn()
                else:
                    if before:
                        e_attn() if what == 1 else heads_out(s.heads)
                    squares_in()
                    sum_features(what - 1, SQ2[:, what - 1, :], True, True).then_inc(s.rms, 1)

            def after_gate_a0(i, j):
                if j == 0:
                    z_attn()
                elif j == 1:
                    e_attn()
                elif j == 2:
                    heads_out(s.heads)

            def after_gate_r(i, g):
                for j in range(3 * g, min(3 * g + 3, RC)):
                    if j >= 4:
                        pe.wait_ge(s.bdd, j - 3)
                    for m in range(2):
                        for i in users[j]:
                            if m == 0:
                                pe.wait_ge(s.xc, i // 2 + 1)
                                pe.wait_ge(strip_sems[i % 8], strip_due[i])
                            at = P * (j - strips[i][0])
                            last = mm(PX[:, j % 4, T * m:T * m + T], BDS[:, i % 8, m, at:at + P], XC[:, i, :],
                                      start=i == users[j][0], stop=i == users[j][-1])
                    last.then_inc(s.bd, 1)

            def sum_acc(tell):
                ready()
                for e in range(2):
                    last = mm(PX[:, 0, 0:T], ONES, ACC[:, T * e:T * e + T], start=e == 0, stop=e == 1)
                last.then_inc(tell, 1)

            def after_gu0(i, j):
                if not (isinstance(i, int) and i == 0):
                    return
                if j == 0:
                    sum_acc(s.ss)
                    pe.wait_ge(s.p_in, 16)
                    for k in range(2):
                        for b in range(NB):
                            at = T * k + P * b
                            last = nc.tensor.transpose(PX[:, 1, at:at + P],
                                                       RT[:, 3072 + T * b + P * k:3072 + T * b + P * k + P], IDENT)
                    last.then_inc(s.tp, 1)
                    c.add("op")
                elif j == 1:
                    pe.wait_ge(s.tab, 48)
                    mm(PX[0:HEADS2, 2, 0:384], MIXf[0:NBUCK, 3072:3072 + HEADS2], MIXf[0:NBUCK, 3100:3484],
                       start=True, stop=True).then_inc(s.tp, 1)

            def after_gu1(i, j):
                if isinstance(i, int) and i == 0 and j < 3:
                    pe.wait_ge(s.tb, 16 * HEADS2)
                    if j:
                        pe.wait_ge(s.flipped, 2 * j)
                    for h in (2 * j, 2 * j + 1):
                        mm(PX[:, 2 + h % 2, :], FLIP, MIXf[:, 512 * h:512 * h + 512], start=True, stop=True)\
                            .then_inc(s.flip, 1)

            def after_ple(i, j):
                if isinstance(i, int) and i == 0 and j == 0:
                    sum_acc(s.ss)

            def z_soft(comps):
                for h in range(2):
                    for x in range(comps):
                        r = slice(P // comps * x, P // comps * (x + 1))
                        bank, o = comps * h + x, T * h
                        mm(PX[:, bank, 0:P], QR[r, 0, o:o + P], QR[r, 1, o:o + P], start=True, stop=True)
                        last = mm(PX[:, bank, P:3 * P], QR[r, 0, o + P:o + T], QR[r, 1, o:o + T],
                                  start=True, stop=True)
                last.then_inc(s.scores2, 1)

            def pt_soft(comps):
                ready()
                for h in range(2):
                    x = S4[:, comps * h, :]
                    for to, frm in ((0, 0), (P, P), (2 * P, 2 * P)):
                        nc.tensor.transpose(PX[:, h, to:to + P], x[:, frm:frm + P], IDENT)
                v_transposes(c.n["group"] % 2).then_inc(s.turned, 1)

            def diff_sum():
                squares_in()
                sum_features(3, SQa, True, True).then_inc(s.rms, 1)

            def evac_of_k():
                pe.wait_ge(s.evac, c.value("group", -1))

            def after_dil(i, j):
                if j == 0:
                    if not (isinstance(i, int) and i == 0):
                        heads_out(s.heads2)
                elif j == 2:
                    evac_of_k()
                    z_soft(1)
                elif j == 3:
                    pt_soft(1)

            def after_diffa(i, j):
                if j == 0:
                    heads_out(s.heads2)
                    pe.wait_ge(s.conv, c.next("conv"))
                    for ch in range(CONVC):
                        last = sum_features(0, CA[:, ch, :], ch == 0, ch == CONVC - 1)
                    last.then_inc(s.sum, 1)
                elif j == 1:
                    squares_in()
                    for ch in range(CONVC):
                        last = sum_features(1, SC_SQ[:, ch, :], ch == 0, ch == CONVC - 1)
                    last.then_inc(s.sumsq, 1)
                elif j == 2:
                    evac_of_k()
                    ready()
                    z_soft(2)
                else:
                    pt_soft(2)

            def after_diffb(i, j):
                if j == 0:
                    heads_out(s.heads2)
                elif j == 1:
                    diff_sum()
                elif j == 4:
                    evac_of_k()
                    pe.wait_ge(s.op, c.value("op", 2))
                    z_soft(2)
                elif j == 5:
                    pt_soft(2)

            def after_outa(i, j):
                if j == 0:
                    heads_out(s.heads2)

            def after_outb(i, j):
                if isinstance(i, int) and i == 0 and j == 0:
                    sum_acc(s.sum)

            def ln():
                pe.wait_ge(s.acc, c.next("acc", DC // 2 - 4))
                for o, src in ((0, ACC), (T, ACC2)):
                    for e in range(2):
                        mm(PX[:, o // T, 0:T], ONES, src[:, T * e:T * e + T], start=e == 0, stop=False)
                ready()
                for e in range(2):
                    mm(PX[:, 0, 0:T], ONES, XRES[:, DC - 2 + e, :], start=False, stop=e == 1)
                squares_in()
                for e in range(2):
                    last = mm(PX[:, 1, 0:T], ONES, SQP[:, T * e:T * e + T], start=False, stop=e == 1)
                last.then_inc(s.sum, 1)

            after = {"attn": after_attn, "gate_a0": after_gate_a0, "gate_r": after_gate_r, "gu0": after_gu0,
                     "gu1": after_gu1, "ple": after_ple, "dil0": after_dil, "dil1": after_dil,
                     "diffa0": after_diffa, "diffa1": after_diffa, "diffb0": after_diffb, "diffb1": after_diffb,
                     "outa0": after_outa, "outa1": after_outa, "outb0": after_outb, "outb1": after_outb}
            between = {"tables": lambda: None, "ln0": ln, "ln1": ln}

            pe.wait_ge(s.mats, 16)
            for q in range(DC // 2):
                if q % 4 == 0:
                    pe.wait_ge((s.x_in0, s.x_in1)[q // 4], 16)
                if q == DC // 2 - 1:
                    pe.wait_ge(s.g_in, 16)
                    nc.tensor.transpose(PX[:, 2, 0:DC], RT[0:DC, 0:P], IDENT[0:DC, 0:DC])
                if q >= 4:
                    pe.wait_ge(s.tpd, q - 3)
                for e in range(2):
                    for b in range(NB):
                        at = T * e + P * b
                        src = D * b + P * (2 * q + e)
                        last = nc.tensor.transpose(PG[:, q % 4, at:at + P], Fv[:, src:src + P], IDENT)
                last.then_inc(s.tp, 1)
                if q == 7:
                    ready()
                    for b in range(NB):
                        last = mm(PX[:, 0, P * b:P * b + P], ONES, Gf[:, 1, P * b:P * b + P], start=True, stop=True)
                    last.then_inc(s.ss, 1)
            for ph in phases:
                if ph.name in between:
                    between[ph.name]()
                    continue
                hook = after.get(ph.name)

                def turn(i):
                    for j, grp in enumerate(ph.body):
                        first = isinstance(i, int) and i == 0
                        group(grp, ph.fresh.get(j, ()) if first else (),
                              {0: diff_sum} if j == 1 and ph.name[:4] == "outa" else None)
                        if hook:
                            hook(i, j)
                turn(0)
                c.loop(1, ph.n, turn)
            for q in range(DC // 2):
                if not STOP:
                    pe.wait_ge(s.final, q + 1)
                if q >= 4:
                    pe.wait_ge(s.tpd, TPD_OUT + q - 3)
                for e in range(2):
                    for b in range(NB):
                        at = P * NB * 0 + T * b + P * e
                        last = nc.tensor.transpose(PG[:, q % 4, at:at + P], XRES[:, 2 * q + e, P * b:P * b + P],
                                                   IDENT)
                last.then_inc(s.tp, 1)


_INS = ["x", "p", "g_mix", "w_in", "conv_w", "conv_b", "w_rg_a", "b_rg_a", "w_rg_x", "b_rg_x", "lru_lambda",
        "q_gain", "k_gain", "w_rnn_out", "w_attn_out", "w_o", "g_ffn", "w_ffn_gu", "w_ffn_down", "g_ple",
        "w_ple_gate", "w_ple_proj", "w_in_2", "diff_lambda_2", "diff_head_gain_2", "conv_dw_2", "conv_b_2",
        "conv_ln_g_2", "conv_ln_b_2", "conv_pw_2", "w_out_2", "ln_g_2", "ln_b_2", "rel_bias_2"]


def kernel(**inputs):
    import concourse.bacc as _bacc
    from concourse.bass_utils import run_bass_kernel_spmd as _run

    data = {name: np.ascontiguousarray(inputs[name]) for name in _INS}
    data.update(zip(("c_mats", "c_keep", "c_onehot", "c_add"), shape_constants()))
    turns = {}
    for real in (False, True):
        nc = _bacc.Bacc("TRN2", target_bir_lowering=False, num_devices=1)
        arrays, A = {}, {}
        for name, a in data.items():
            arrays[f"in_{name}_dram"] = a
            A[name] = nc.dram_tensor(f"in_{name}_dram", a.shape, mybir.dt.from_np(a.dtype), kind="ExternalInput").ap()
        A["out"] = nc.dram_tensor("out_0_dram", (1, T, D), mybir.dt.float32, kind="ExternalOutput").ap()
        program(nc, A, turns, real)
    r = _run(nc, [arrays], core_ids=[0])
    return r.results[0]["out_0_dram"]
```
